# Optimizing a Trainium2 kernel written in Bass

```python
import jax, jax.numpy as jnp
from jax import lax
import numpy as np
import math
import jax
import jax.numpy as jnp

D_MODEL = 1024
BATCH = 1
SEQ = 256
DEPTH = 1

CHUNK = 64
LEFT_CHUNKS = 8
BAND = (LEFT_CHUNKS + 1) * CHUNK
N_HEADS = 8
HEAD_DIM = 64
ATTN_W = N_HEADS * HEAD_DIM
CONV_W = D_MODEL // 2
CONV_K = 3
MAX_REL_PAST = 256
NUM_REL = (CHUNK - 1) + MAX_REL_PAST + 1
PLE_DIM = 256
N_GROUPS = 4
EXPERTS_PER_GROUP = 8
N_EXPERTS = N_GROUPS * EXPERTS_PER_GROUP
TOP_K = 2
D_EXPERT = 512
BLK = 128
EPS = 1e-6

IN_WIDTHS = [ATTN_W, ATTN_W, ATTN_W, CONV_W, CONV_W, CONV_W, D_MODEL, D_MODEL]
IN_TOTAL = sum(IN_WIDTHS)
SPLITS = [int(v) for v in np.cumsum(IN_WIDTHS)[:-1]]


def rms_norm(x, g):
    xf = x.astype(jnp.float32)
    y = xf * lax.rsqrt(jnp.mean(xf * xf, axis=-1, keepdims=True) + EPS)
    return (y * g.astype(jnp.float32)).astype(x.dtype)

def chunked_rel_attention(q, k, v, g_q, g_k, rel_bias):
    b, s, h, dh = q.shape
    nc = s // CHUNK
    pad = LEFT_CHUNKS * CHUNK
    q = rms_norm(q, g_q)
    k = rms_norm(k, g_k)
    kp = jnp.pad(k, ((0, 0), (pad, 0), (0, 0), (0, 0)))
    vp = jnp.pad(v, ((0, 0), (pad, 0), (0, 0), (0, 0)))
    dist = jnp.arange(CHUNK)[:, None] - jnp.arange(BAND)[None, :] + pad
    idx = jnp.clip(dist, -(CHUNK - 1), MAX_REL_PAST) + (CHUNK - 1)
    bias = rel_bias[:, idx].astype(jnp.float32)
    qc = q.reshape(b, nc, CHUNK, h, dh).transpose(1, 0, 2, 3, 4)
    scale = dh ** -0.5

    def one_chunk(args):
        q_blk, c = args
        start = c * CHUNK
        kb = lax.dynamic_slice_in_dim(kp, start, BAND, axis=1)
        vb = lax.dynamic_slice_in_dim(vp, start, BAND, axis=1)
        sc = jnp.einsum('bqhd,bkhd->bhqk', q_blk, kb).astype(jnp.float32) * scale + bias
        valid = (start - pad + jnp.arange(BAND)) >= 0
        sc = jnp.where(valid[None, None, None, :], sc, -1e30)
        pr = jax.nn.softmax(sc, axis=-1).astype(vb.dtype)
        return jnp.einsum('bhqk,bkhd->bqhd', pr, vb)

    out = lax.map(one_chunk, (qc, jnp.arange(nc)))
    return out.transpose(1, 0, 2, 3, 4).reshape(b, s, h * dh)

def short_conv(u, bg, cg, w, bias):
    s = u.shape[1]
    zp = jnp.pad(cg * u, ((0, 0), (CONV_K - 1, 0), (0, 0)))
    y = bias
    for j in range(CONV_K):
        y = y + w[j] * zp[:, j:j + s]
    return bg * y

def hier_moe(xn, w_group, b_group, w_router, b_router, w1, w3, w2):
    t, d = xn.shape
    gl = (xn @ w_group).astype(jnp.float32) + b_group
    grp = jnp.argmax(gl, axis=-1)
    p_grp = jnp.take_along_axis(jax.nn.softmax(gl, axis=-1), grp[:, None], axis=1)
    el = ((xn @ w_router).astype(jnp.float32) + b_router).reshape(t, N_GROUPS, EXPERTS_PER_GROUP)
    el = jnp.take_along_axis(el, grp[:, None, None], axis=1)[:, 0]
    top_l, top_i = lax.top_k(el, TOP_K)
    wgt = (p_grp * jax.nn.softmax(top_l, axis=-1)).reshape(-1)
    eid = (grp[:, None] * EXPERTS_PER_GROUP + top_i).reshape(-1).astype(jnp.int32)
    tok = jnp.repeat(jnp.arange(t, dtype=jnp.int32), TOP_K)
    a = t * TOP_K
    order = jnp.argsort(eid)
    se = eid[order]
    counts = jnp.bincount(eid, length=N_EXPERTS)
    pcounts = (counts + BLK - 1) // BLK * BLK
    pends = jnp.cumsum(pcounts)
    pstarts = pends - pcounts
    starts = jnp.cumsum(counts) - counts
    dest = pstarts[se] + jnp.arange(a) - starts[se]
    n_rows = (a + BLK - 1) // BLK * BLK + N_EXPERTS * BLK
    n_blk = n_rows // BLK
    row_tok = jnp.zeros((n_rows,), jnp.int32).at[dest].set(tok[order])
    row_w = jnp.zeros((n_rows,), wgt.dtype).at[dest].set(wgt[order])
    blk_e = jnp.minimum(jnp.searchsorted(pends, jnp.arange(n_blk) * BLK, side='right'), N_EXPERTS - 1)
    xs = xn[row_tok].reshape(n_blk, BLK, d)

    def expert_block(args):
        xb, e = args
        hdn = jax.nn.silu(xb @ w1[e]) * (xb @ w3[e])
        return hdn @ w2[e]

    ys = lax.map(expert_block, (xs, blk_e)).reshape(n_rows, d)
    return jnp.zeros((t, d), xn.dtype).at[row_tok].add(ys * row_w[:, None].astype(ys.dtype))

def first_inputs(seed: int = 0) -> dict:
    key = jax.random.key(seed)
    ks = jax.random.split(key, 32)
    nrm = lambda k, shape, sc: jax.random.normal(k, shape, jnp.float32) * sc
    L = DEPTH
    return {
        "x": nrm(ks[0], (BATCH, SEQ, D_MODEL), 1.0),
        "p": nrm(ks[1], (DEPTH, BATCH, SEQ, PLE_DIM), 1.0),
        "g_mix": 1.0 + nrm(ks[2], (L, D_MODEL), 0.02),
        "w_in": nrm(ks[3], (L, D_MODEL, IN_TOTAL), D_MODEL ** -0.5),
        "b_in": nrm(ks[4], (L, IN_TOTAL), 0.02),
        "g_q": 1.0 + nrm(ks[5], (L, HEAD_DIM), 0.02),
        "g_k": 1.0 + nrm(ks[6], (L, HEAD_DIM), 0.02),
        "rel_bias": nrm(ks[7], (L, N_HEADS, NUM_REL), 0.1),
        "conv_w": nrm(ks[8], (L, CONV_K, CONV_W), CONV_K ** -0.5),
        "conv_b": nrm(ks[9], (L, CONV_W), 0.02),
        "w_pa": nrm(ks[10], (L, ATTN_W, D_MODEL), ATTN_W ** -0.5),
        "w_pc": nrm(ks[11], (L, CONV_W, D_MODEL), CONV_W ** -0.5),
        "w_o": nrm(ks[12], (L, D_MODEL, D_MODEL), D_MODEL ** -0.5),
        "g_ffn": 1.0 + nrm(ks[13], (L, D_MODEL), 0.02),
        "w_group": nrm(ks[14], (L, D_MODEL, N_GROUPS), D_MODEL ** -0.5),
        "b_group": nrm(ks[15], (L, N_GROUPS), 0.01),
        "w_router": nrm(ks[16], (L, D_MODEL, N_EXPERTS), D_MODEL ** -0.5),
        "b_router": nrm(ks[17], (L, N_EXPERTS), 0.01),
        "w1": nrm(ks[18], (L, N_EXPERTS, D_MODEL, D_EXPERT), D_MODEL ** -0.5),
        "w3": nrm(ks[19], (L, N_EXPERTS, D_MODEL, D_EXPERT), D_MODEL ** -0.5),
        "w2": nrm(ks[20], (L, N_EXPERTS, D_EXPERT, D_MODEL), D_EXPERT ** -0.5),
        "g_ple": 1.0 + nrm(ks[21], (L, D_MODEL), 0.02),
        "w_ple_gate": nrm(ks[22], (L, D_MODEL, D_MODEL), D_MODEL ** -0.5),
        "b_ple_gate": nrm(ks[23], (L, D_MODEL), 0.02),
        "w_ple_proj": nrm(ks[24], (L, PLE_DIM, D_MODEL), PLE_DIM ** -0.5),
    }

def first_block(x, p, g_mix, w_in, b_in, g_q, g_k, rel_bias, conv_w, conv_b, w_pa, w_pc, w_o,
              g_ffn, w_group, b_group, w_router, b_router, w1, w3, w2,
              g_ple, w_ple_gate, b_ple_gate, w_ple_proj):
    b, s, d = x.shape
    h = x
    for i in range(DEPTH):
        n = rms_norm(h, g_mix[i])
        z = n @ w_in[i] + b_in[i]
        q, k, v, u, bg, cg, ga, gc = jnp.split(z, SPLITS, axis=-1)
        ya = chunked_rel_attention(q.reshape(b, s, N_HEADS, HEAD_DIM),
                                   k.reshape(b, s, N_HEADS, HEAD_DIM),
                                   v.reshape(b, s, N_HEADS, HEAD_DIM),
                                   g_q[i], g_k[i], rel_bias[i])
        yc = short_conv(u, bg, cg, conv_w[i], conv_b[i])
        m = jax.nn.sigmoid(ga) * (ya @ w_pa[i]) + jax.nn.sigmoid(gc) * (yc @ w_pc[i])
        h = h + m @ w_o[i]
        n2 = rms_norm(h, g_ffn[i]).reshape(b * s, d)
        h = h + hier_moe(n2, w_group[i], b_group[i], w_router[i], b_router[i],
                         w1[i], w3[i], w2[i]).reshape(b, s, d)
        gate = jax.nn.sigmoid(rms_norm(h, g_ple[i]) @ w_ple_gate[i] + b_ple_gate[i])
        h = h + gate * (p[i] @ w_ple_proj[i])
    return h


MEM_LEN = 256
NEG_INF = -1e30
BIG = 1e30

GLA_HEADS = 4
GLA_DK = 64
GLA_DV = 128
GLA_RANK = 16
GLA_TAU = 16.0
GLA_CHUNK = 64

NSA_HEADS = 8
NSA_KV_GROUPS = 2
NSA_HPG = NSA_HEADS // NSA_KV_GROUPS
NSA_DH = 64
CMP_BLOCK = 32
CMP_STRIDE = 16
CMP_HIDDEN = 128
SLC_BLOCK = 64
SLC_TOPK = 16
WINDOW = 512
Q_BLOCK = 128

REL_BUCKETS = 32
REL_MAX_DIST = 2048

XA_HEADS = 4
XA_DH = D_MODEL // XA_HEADS

PEER_HEADS = 8
PEER_NKEYS = 128
PEER_EXPERTS = PEER_NKEYS * PEER_NKEYS
PEER_TOPK = 16
PEER_DKEY = 128
PEER_TOKEN_CHUNK = 128

IN_SIZES = (GLA_HEADS * GLA_DK, GLA_HEADS * GLA_DK, GLA_HEADS * GLA_DV, GLA_HEADS * GLA_DV, GLA_RANK,
            NSA_HEADS * NSA_DH,
            NSA_KV_GROUPS * NSA_DH, NSA_KV_GROUPS * NSA_DH,
            NSA_KV_GROUPS * NSA_DH, NSA_KV_GROUPS * NSA_DH,
            NSA_KV_GROUPS * NSA_DH, NSA_KV_GROUPS * NSA_DH,
            NSA_HEADS * 3)
IN_COLS = sum(IN_SIZES)


def rms_norm_2(x, g):
    xf = x.astype(jnp.float32)
    y = xf * lax.rsqrt(jnp.mean(xf * xf, axis=-1, keepdims=True) + EPS)
    return (y * g.astype(jnp.float32)).astype(x.dtype)

def _masked_softmax(s, mask):
    s = jnp.where(mask, s.astype(jnp.float32), NEG_INF)
    p = jax.nn.softmax(s, axis=-1)
    return p * jnp.any(mask, axis=-1, keepdims=True)

def _t5_bucket(dist):
    n = jnp.maximum(dist, 0)
    max_exact = REL_BUCKETS // 2
    nf = jnp.maximum(n, 1).astype(jnp.float32)
    log_ratio = jnp.log(nf / max_exact) / math.log(REL_MAX_DIST / max_exact)
    large = max_exact + (log_ratio * (REL_BUCKETS - max_exact)).astype(jnp.int32)
    large = jnp.minimum(large, REL_BUCKETS - 1)
    return jnp.where(n < max_exact, n, large)

def _head_bias(dist, rel_bias):
    b = jnp.moveaxis(rel_bias[_t5_bucket(dist)], -1, 0)
    return b.reshape((NSA_KV_GROUPS, NSA_HPG) + dist.shape).astype(jnp.float32)

def _split_cols(z):
    offs = np.cumsum(np.array(IN_SIZES))[:-1].tolist()
    return jnp.split(z, offs, axis=-1)

def _gla_chunked(q, k, v, log_a):
    B, T, H, dk = q.shape
    dv = v.shape[-1]
    C = GLA_CHUNK
    nc = T // C

    def to_chunks(a):
        return a.astype(jnp.float32).reshape(B, nc, C, H, a.shape[-1]).transpose(1, 0, 3, 2, 4)

    qc, kc, vc, ac = to_chunks(q), to_chunks(k), to_chunks(v), to_chunks(log_a)
    causal = jnp.tril(jnp.ones((C, C), dtype=bool))[..., None]

    def step(S, inp):
        qi, ki, vi, ai = inp
        b = jnp.cumsum(ai, axis=-2)
        diff = b[..., :, None, :] - b[..., None, :, :]
        decay = jnp.exp(jnp.where(causal, diff, NEG_INF))
        A = jnp.einsum('bhtd,bhsd,bhtsd->bhts', qi, ki, decay)
        o = jnp.einsum('bhts,bhsv->bhtv', A, vi) + jnp.einsum('bhtd,bhdv->bhtv', qi * jnp.exp(b), S)
        b_last = b[..., -1:, :]
        S_new = jnp.exp(b_last[..., 0, :])[..., None] * S + jnp.einsum(
            'bhsd,bhsv->bhdv', ki * jnp.exp(b_last - b), vi)
        return S_new, o

    S0 = jnp.zeros((B, H, dk, dv), jnp.float32)
    _, o = lax.scan(step, S0, (qc, kc, vc, ac))
    return o.transpose(1, 0, 3, 2, 4).reshape(B, T, H, dv)

def gla_mixer(gq, gk, gv, gr, glr, gate_w2, gate_b, out_norm):
    B, T, _ = gq.shape
    q = gq.reshape(B, T, GLA_HEADS, GLA_DK) * (GLA_DK ** -0.5)
    k = gk.reshape(B, T, GLA_HEADS, GLA_DK)
    v = gv.reshape(B, T, GLA_HEADS, GLA_DV)
    log_a = jax.nn.log_sigmoid((glr @ gate_w2 + gate_b).astype(jnp.float32)) / GLA_TAU
    log_a = log_a.reshape(B, T, GLA_HEADS, GLA_DK)
    o = _gla_chunked(q, k, v, log_a)
    o = rms_norm_2(o, out_norm).reshape(B, T, GLA_HEADS * GLA_DV)
    return (o * jax.nn.silu(gr.astype(jnp.float32))).astype(gq.dtype)

def _compress(kv, pos, w1, w2):
    B, T, G, dh = kv.shape
    n_cmp = (T - CMP_BLOCK) // CMP_STRIDE + 1
    idx = jnp.arange(n_cmp)[:, None] * CMP_STRIDE + jnp.arange(CMP_BLOCK)[None, :]
    blocks = kv[:, idx] + pos[None, None, :, None, :]
    blocks = blocks.transpose(0, 3, 1, 2, 4).reshape(B, G, n_cmp, CMP_BLOCK * dh)
    return jax.nn.gelu(blocks @ w1) @ w2

def _slc_importance(p_grp, n_slc):
    n_cmp = p_grp.shape[-1]
    ratio = SLC_BLOCK // CMP_STRIDE
    back = CMP_BLOCK // CMP_STRIDE - 1
    pad_end = max(ratio * n_slc - n_cmp, 0)
    pp = jnp.pad(p_grp, [(0, 0)] * (p_grp.ndim - 1) + [(back, pad_end)])
    base = jnp.arange(n_slc) * ratio + back
    imp = 0.0
    for r in range(-back, ratio):
        lo = CMP_STRIDE * r
        overlap = min(lo + CMP_BLOCK, SLC_BLOCK) - max(lo, 0)
        imp = imp + (overlap / CMP_BLOCK) * pp[..., base + r]
    return imp

def nsa_mixer(nq, kc, vc, ks, vs, kw, vw, ng, rel_bias, pos_k, pos_v, ck_w1, ck_w2, cv_w1, cv_w2):
    B, T, _ = nq.shape
    G, HPG, dh = NSA_KV_GROUPS, NSA_HPG, NSA_DH
    n_cmp = (T - CMP_BLOCK) // CMP_STRIDE + 1
    n_slc = T // SLC_BLOCK
    n_sel = min(SLC_TOPK, n_slc)
    n_qblk = T // Q_BLOCK
    kv_shape = (B, T, G, dh)

    q = (nq.reshape(B, T, G, HPG, dh) * (dh ** -0.5)).transpose(0, 2, 3, 1, 4)
    gates = jax.nn.sigmoid(ng.astype(jnp.float32)).reshape(B, T, G, HPG, 3).transpose(0, 2, 3, 1, 4)

    k_cmp = _compress(kc.reshape(kv_shape), pos_k, ck_w1, ck_w2)
    v_cmp = _compress(vc.reshape(kv_shape), pos_v, cv_w1, cv_w2)
    k_slc = ks.reshape(kv_shape).transpose(0, 2, 1, 3).reshape(B, G, n_slc, SLC_BLOCK, dh)
    v_slc = vs.reshape(kv_shape).transpose(0, 2, 1, 3).reshape(B, G, n_slc, SLC_BLOCK, dh)
    pad = ((0, 0), (0, 0), (WINDOW, 0), (0, 0))
    k_win = jnp.pad(kw.reshape(kv_shape).transpose(0, 2, 1, 3), pad)
    v_win = jnp.pad(vw.reshape(kv_shape).transpose(0, 2, 1, 3), pad)

    qi = jnp.arange(Q_BLOCK)
    kj = jnp.arange(WINDOW + Q_BLOCK)
    dist_w = qi[:, None] + WINDOW - kj[None, :]
    band = (dist_w >= 0) & (dist_w < WINDOW)
    bias_w = _head_bias(dist_w, rel_bias)
    cmp_end = jnp.arange(n_cmp) * CMP_STRIDE + (CMP_BLOCK - 1)
    slc_ids = jnp.arange(n_slc)
    bidx = jnp.arange(B)[:, None, None, None]
    gidx = jnp.arange(G)[None, :, None, None]
    table_g = rel_bias.reshape(REL_BUCKETS, G, HPG).transpose(1, 0, 2)

    def block(i):
        s0 = i * Q_BLOCK
        t = s0 + qi
        qb = lax.dynamic_slice_in_dim(q, s0, Q_BLOCK, axis=3)
        gb = lax.dynamic_slice_in_dim(gates, s0, Q_BLOCK, axis=3)

        dist_c = t[:, None] - cmp_end[None, :]
        s_c = jnp.einsum('bghqd,bgnd->bghqn', qb, k_cmp) + _head_bias(dist_c, rel_bias)
        p_c = _masked_softmax(s_c, dist_c >= 0)
        o_c = jnp.einsum('bghqn,bgnd->bghqd', p_c.astype(v_cmp.dtype), v_cmp)

        imp = _slc_importance(p_c.sum(axis=2), n_slc)
        cur = (t // SLC_BLOCK)[:, None]
        forced = (slc_ids == 0) | (slc_ids == cur) | (slc_ids == cur - 1)
        visible = (slc_ids * SLC_BLOCK)[None, :] <= t[:, None]
        imp = jnp.where(forced, BIG, jnp.where(visible, imp, NEG_INF))
        _, sel = lax.top_k(imp, n_sel)
        k_sel = k_slc[bidx, gidx, sel].reshape(B, G, Q_BLOCK, n_sel * SLC_BLOCK, dh)
        v_sel = v_slc[bidx, gidx, sel].reshape(B, G, Q_BLOCK, n_sel * SLC_BLOCK, dh)
        kpos = (sel[..., None] * SLC_BLOCK + jnp.arange(SLC_BLOCK)).reshape(B, G, Q_BLOCK, -1)
        dist_s = t[:, None] - kpos
        bias_s = jnp.moveaxis(table_g[gidx, _t5_bucket(dist_s)], -1, 2).astype(jnp.float32)
        s_s = jnp.einsum('bghqd,bgqkd->bghqk', qb, k_sel) + bias_s
        p_s = _masked_softmax(s_s, (dist_s >= 0)[:, :, None])
        o_s = jnp.einsum('bghqk,bgqkd->bghqd', p_s.astype(v_sel.dtype), v_sel)

        k_w = lax.dynamic_slice_in_dim(k_win, s0, WINDOW + Q_BLOCK, axis=2)
        v_w = lax.dynamic_slice_in_dim(v_win, s0, WINDOW + Q_BLOCK, axis=2)
        valid_w = band & ((s0 - WINDOW + kj) >= 0)[None, :]
        s_w = jnp.einsum('bghqd,bgkd->bghqk', qb, k_w) + bias_w
        p_w = _masked_softmax(s_w, valid_w)
        o_w = jnp.einsum('bghqk,bgkd->bghqd', p_w.astype(v_w.dtype), v_w)

        o = gb[..., 0:1] * o_c + gb[..., 1:2] * o_s + gb[..., 2:3] * o_w
        return o.astype(nq.dtype)

    o = lax.map(block, jnp.arange(n_qblk))
    return o.transpose(1, 0, 4, 2, 3, 5).reshape(B, T, NSA_HEADS * dh)

def cross_attn(hn, memn, wq, wk, wv, wo):
    B, T, _ = hn.shape
    M = memn.shape[1]
    q = (hn @ wq).reshape(B, T, XA_HEADS, XA_DH) * (XA_DH ** -0.5)
    k = (memn @ wk).reshape(B, M, XA_HEADS, XA_DH)
    v = (memn @ wv).reshape(B, M, XA_HEADS, XA_DH)
    s = jnp.einsum('bqhd,bmhd->bhqm', q, k).astype(jnp.float32)
    p = jax.nn.softmax(s, axis=-1).astype(v.dtype)
    o = jnp.einsum('bhqm,bmhd->bqhd', p, v).reshape(B, T, XA_HEADS * XA_DH)
    return o @ wo

def peer_ffn(hn, wq, subkeys, down, up):
    B, T, D = hn.shape
    N = B * T
    H, K = PEER_HEADS, PEER_TOPK
    xt = hn.reshape(N, D)
    q = (xt @ wq).reshape(N, H, 2, PEER_DKEY // 2)
    s = jnp.einsum('nhpd,hpkd->nhpk', q, subkeys).astype(jnp.float32)
    s_half, i_half = lax.top_k(s, K)
    cand_s = (s_half[:, :, 0, :, None] + s_half[:, :, 1, None, :]).reshape(N, H, K * K)
    cand_i = (i_half[:, :, 0, :, None] * PEER_NKEYS + i_half[:, :, 1, None, :]).reshape(N, H, K * K)
    top_s, pos = lax.top_k(cand_s, K)
    eidx = jnp.take_along_axis(cand_i, pos, axis=-1)
    gate = jax.nn.softmax(top_s, axis=-1)
    n_chunks = N // PEER_TOKEN_CHUNK

    def chunk(args):
        xc, ec, gc = args
        u = down[ec]
        act = jax.nn.gelu(jnp.einsum('cd,chkd->chk', xc, u).astype(jnp.float32)) * gc
        return jnp.einsum('chk,chkd->cd', act.astype(up.dtype), up[ec])

    y = lax.map(chunk, (xt.reshape(n_chunks, PEER_TOKEN_CHUNK, D),
                        eidx.reshape(n_chunks, PEER_TOKEN_CHUNK, H, K),
                        gate.reshape(n_chunks, PEER_TOKEN_CHUNK, H, K)))
    return y.reshape(B, T, D).astype(hn.dtype)

def second_inputs(seed: int = 0) -> dict:
    key = jax.random.key(seed)
    ks = jax.random.split(key, 32)
    f32 = jnp.float32
    L, D = DEPTH, D_MODEL

    def nrm(k, shape, scale):
        return jax.random.normal(k, shape, f32) * scale

    def gain(k, shape):
        return 1.0 + 0.02 * jax.random.normal(k, shape, f32)

    return {
        'x': nrm(ks[0], (BATCH, SEQ, D), 1.0),
        'mem': nrm(ks[1], (BATCH, MEM_LEN, D), 1.0),
        'rel_bias': nrm(ks[2], (REL_BUCKETS, NSA_HEADS), 0.5),
        'norm_mix': gain(ks[3], (L, D)),
        'w_in': nrm(ks[4], (L, D, IN_COLS), D ** -0.5),
        'gla_gate_w2': nrm(ks[5], (L, GLA_RANK, GLA_HEADS * GLA_DK), GLA_RANK ** -0.5),
        'gla_gate_b': nrm(ks[6], (L, GLA_HEADS * GLA_DK), 0.1),
        'gla_out_norm': gain(ks[7], (L, GLA_DV)),
        'cmp_pos_k': nrm(ks[8], (L, CMP_BLOCK, NSA_DH), 0.1),
        'cmp_pos_v': nrm(ks[9], (L, CMP_BLOCK, NSA_DH), 0.1),
        'cmp_k_w1': nrm(ks[10], (L, CMP_BLOCK * NSA_DH, CMP_HIDDEN), (CMP_BLOCK * NSA_DH) ** -0.5),
        'cmp_k_w2': nrm(ks[11], (L, CMP_HIDDEN, NSA_DH), CMP_HIDDEN ** -0.5),
        'cmp_v_w1': nrm(ks[12], (L, CMP_BLOCK * NSA_DH, CMP_HIDDEN), (CMP_BLOCK * NSA_DH) ** -0.5),
        'cmp_v_w2': nrm(ks[13], (L, CMP_HIDDEN, NSA_DH), CMP_HIDDEN ** -0.5),
        'w_out': nrm(ks[14], (L, D, D), D ** -0.5),
        'norm_xattn': gain(ks[15], (L, D)),
        'norm_mem': gain(ks[16], (L, D)),
        'xa_wq': nrm(ks[17], (L, D, D), D ** -0.5),
        'xa_wk': nrm(ks[18], (L, D, D), D ** -0.5),
        'xa_wv': nrm(ks[19], (L, D, D), D ** -0.5),
        'xa_wo': nrm(ks[20], (L, D, D), D ** -0.5),
        'norm_ffn': gain(ks[21], (L, D)),
        'peer_wq': nrm(ks[22], (L, D, PEER_HEADS * PEER_DKEY), D ** -0.5),
        'peer_subkeys': nrm(ks[23], (L, PEER_HEADS, 2, PEER_NKEYS, PEER_DKEY // 2), (PEER_DKEY // 2) ** -0.5),
        'peer_down': nrm(ks[24], (L, PEER_EXPERTS, D), D ** -0.5),
        'peer_up': nrm(ks[25], (L, PEER_EXPERTS, D), PEER_HEADS ** -0.5),
        'norm_final': gain(ks[26], (D,)),
    }

def second_block(x, mem, rel_bias, norm_mix, w_in, gla_gate_w2, gla_gate_b, gla_out_norm,
              cmp_pos_k, cmp_pos_v, cmp_k_w1, cmp_k_w2, cmp_v_w1, cmp_v_w2, w_out,
              norm_xattn, norm_mem, xa_wq, xa_wk, xa_wv, xa_wo,
              norm_ffn, peer_wq, peer_subkeys, peer_down, peer_up, norm_final):
    h = x
    for l in range(DEPTH):
        hn = rms_norm_2(h, norm_mix[l])
        (gq, gk, gv, gr, glr, nq, kc, vc, ks_, vs_, kw, vw, ng) = _split_cols(hn @ w_in[l])
        o_gla = gla_mixer(gq, gk, gv, gr, glr, gla_gate_w2[l], gla_gate_b[l], gla_out_norm[l])
        o_nsa = nsa_mixer(nq, kc, vc, ks_, vs_, kw, vw, ng, rel_bias,
                          cmp_pos_k[l], cmp_pos_v[l], cmp_k_w1[l], cmp_k_w2[l], cmp_v_w1[l], cmp_v_w2[l])
        h = h + jnp.concatenate([o_gla, o_nsa], axis=-1) @ w_out[l]
        h = h + cross_attn(rms_norm_2(h, norm_xattn[l]), rms_norm_2(mem, norm_mem[l]),
                           xa_wq[l], xa_wk[l], xa_wv[l], xa_wo[l])
        h = h + peer_ffn(rms_norm_2(h, norm_ffn[l]), peer_wq[l], peer_subkeys[l], peer_down[l], peer_up[l])
    return rms_norm_2(h, norm_final)


def setup_inputs(seed=0):
    out = dict(first_inputs(seed))
    for name, value in second_inputs(seed + 1).items():
        if name != "x":
            out[name + "_2"] = value
    return out


def reference(
    x, p, g_mix, w_in, b_in, g_q, g_k, rel_bias, conv_w, conv_b, w_pa, w_pc, w_o, g_ffn,
    w_group, b_group, w_router, b_router, w1, w3, w2, g_ple, w_ple_gate, b_ple_gate, w_ple_proj,
    mem_2, rel_bias_2, norm_mix_2, w_in_2, gla_gate_w2_2, gla_gate_b_2, gla_out_norm_2,
    cmp_pos_k_2, cmp_pos_v_2, cmp_k_w1_2, cmp_k_w2_2, cmp_v_w1_2, cmp_v_w2_2, w_out_2,
    norm_xattn_2, norm_mem_2, xa_wq_2, xa_wk_2, xa_wv_2, xa_wo_2, norm_ffn_2, peer_wq_2,
    peer_subkeys_2, peer_down_2, peer_up_2, norm_final_2,
):
    x = first_block(
        x, p, g_mix, w_in, b_in, g_q, g_k, rel_bias, conv_w, conv_b, w_pa, w_pc, w_o, g_ffn,
        w_group, b_group, w_router, b_router, w1, w3, w2, g_ple, w_ple_gate, b_ple_gate,
        w_ple_proj,
    )
    return second_block(
        x, mem_2, rel_bias_2, norm_mix_2, w_in_2, gla_gate_w2_2, gla_gate_b_2, gla_out_norm_2,
        cmp_pos_k_2, cmp_pos_v_2, cmp_k_w1_2, cmp_k_w2_2, cmp_v_w1_2, cmp_v_w2_2, w_out_2,
        norm_xattn_2, norm_mem_2, xa_wq_2, xa_wk_2, xa_wv_2, xa_wo_2, norm_ffn_2, peer_wq_2,
        peer_subkeys_2, peer_down_2, peer_up_2, norm_final_2,
    )


_drawn_inputs = setup_inputs


def setup_inputs(seed=0):
    import zlib

    import numpy as np

    out = dict(_drawn_inputs(seed))
    spreads = {}
    factors = {'g_q': 4.453,
     'g_k': 8.0,
     'b_group': 4.688,
     'b_router': 6.493,
     'g_ple': 6.606,
     'b_ple_gate': 5.897,
     'norm_mix_2': 2.733,
     'gla_gate_b_2': 2.753,
     'gla_out_norm_2': 4.922,
     'cmp_pos_k_2': 8.0,
     'norm_xattn_2': 8.0,
     'norm_mem_2': 8.0,
     'norm_ffn_2': 23.2,
     'norm_final_2': 7.609,
     'cmp_pos_v_2': 2.942}
    for name, (base, spread) in spreads.items():
        noise = np.random.default_rng([zlib.crc32(name.encode()), seed]).standard_normal(out[name].shape)
        drawn = base * np.exp(spread * noise) if base else spread * noise
        out[name] = jnp.asarray(drawn.astype(out[name].dtype))
    for name, factor in factors.items():
        out[name] = (out[name] * factor).astype(out[name].dtype)
    return out
```

```python
from contextlib import ExitStack

import numpy as np
import concourse.bass as bass
from concourse import mybir

F32 = mybir.dt.float32
U32 = mybir.dt.uint32
ALU = mybir.AluOpType
ACT = mybir.ActivationFunctionType
X = mybir.AxisListType.X

P = 128
T = 256
TT = T // P
D = 1024
KT = D // P
NEG = -1e30
EPS = 1e-6
HEADS = 8
DH = 64
REL = 320
EXPERTS = 32
GROUPS = 4
PER_GROUP = EXPERTS // GROUPS
FF = 512
FT = FF // P
BUCKETS = 32
TAB = 512
N_CMP = 15
CMP_STRIDE = 16
CMP_BLOCK = 32
SUB = 16
NSUB = T // SUB
GLA_HEADS = 4
XHEADS = 4
PH = 8
TOPK = 16
NKEYS = 128

RING = 6
SLOT = KT * 512

ROWS = [("g_mix", 8), ("b_in", 40), ("conv_w", 12), ("conv_b", 4), ("g_ffn", 8), ("g_ple", 8),
        ("norm_mix_2", 8), ("gla_gate_b_2", 2), ("norm_xattn_2", 8), ("norm_mem_2", 8),
        ("norm_ffn_2", 8), ("gla_out_norm_2", 1)]
COL = {}
NVEC = 0
for _name, _rows in ROWS:
    COL[_name] = NVEC
    NVEC += _rows
COL["g_q"], COL["g_k"] = NVEC, NVEC + 1
NVEC += 2
assert NVEC <= P


def distance_buckets():
    n = np.arange(T)
    far = 16 + np.floor(np.log(np.maximum(n, 1) / 16.0) / np.log(128.0) * 16).astype(np.int64)
    bucket = np.where(n < 16, n, np.minimum(far, BUCKETS - 1))
    return (np.arange(BUCKETS)[:, None] == bucket[None, :]).astype(np.float32)


NVROWS = len(ROWS) + 4
NLATE = 6


class Chain:

    def __init__(self, eng, sem):
        self.eng, self.sem, self.n = eng, sem, 0

    def __call__(self, ins):
        ins.then_inc(self.sem, 1)
        self.n += 1
        self.eng.wait_ge(self.sem, self.n)


def weight_slots(w):
    def cols(name, a, b):
        return w[name][0].rearrange("(k p) n -> p k n", p=P)[:, :, a:b]

    def pairs(name):
        return [[(0, cols(name, 512 * j, 512 * j + 512))] for j in range(2)]

    first = [[(0, cols("w_in", 512 * j, 512 * j + 512))] for j in range(10)]
    first += [[(0, cols("w_pa", 512 * j, 512 * j + 512)), (SLOT // 2, cols("w_pc", 512 * j, 512 * j + 512))]
              for j in range(2)]
    first += pairs("w_o")
    later = pairs("w_ple_gate") + [[(0, cols("w_ple_proj", 0, D))]]
    later += [[(0, cols("w_in_2", a, b))] for a, b in
              ((0, 512), (512, 1024), (1024, 1536), (1552, 2064), (2064, 2448), (2448, 2856))]
    for name in ("w_out_2", "xa_wk_2", "xa_wv_2", "xa_wq_2", "xa_wo_2", "peer_wq_2"):
        later += pairs(name)
    return first, later


def build(nc, w, buckets, out):
    with ExitStack() as ctx:
        def sb(name, shape, dt=F32):
            return ctx.enter_context(nc.sbuf_tensor(name, shape, dt))

        sems = {}

        def S(name):
            if name not in sems:
                sems[name] = ctx.enter_context(nc.semaphore(name))
            return sems[name]

        bank = [ctx.enter_context(nc.psum_tensor(f"bank{i}", [P, 512], F32)) for i in range(8)]
        table_dram = nc.dram_tensor("distance_table", [HEADS, TAB], F32, kind="Internal")

        ident = sb("ident", [P, P])
        mirror = sb("mirror", [P, P])
        ones = sb("ones", [P, P])
        iota = sb("iota", [P, P])
        vecs = sb("vecs", [P, P])
        eps = sb("eps", [P, 1])
        late_row = sb("late_row", [P, 1])
        h = sb("h", [P, TT, D])
        nT = sb("nT", [P, KT, T])
        stat = sb("stat", [P, 3, TT])
        unit = sb("unit", [P, 3, 2])
        brow = sb("brow", [1, 3 * 512])
        qk_stat = sb("qk_stat", [P, 3, 2 * TT * HEADS])
        br36 = sb("br36", [1, 36])
        logit = sb("logit", [P, TT, 40])
        route = sb("route", [P, TT, 80])
        top8 = sb("top8", [P, TT, 16])
        idx8 = sb("idx8", [P, TT, 16], U32)
        idx8f = sb("idx8f", [P, TT, 16])
        gatew = sb("gatew", [P, TT, EXPERTS])
        sel_dup = sb("sel_dup", [P, 2, P])
        modmask = sb("modmask", [P, P + SUB])
        mask_prev = sb("mask_prev", [P, P])
        mask_same = sb("mask_same", [P, P])
        w_glr = sb("w_glr", [P, KT, 16])
        glrT = sb("glrT", [16, T])
        gate_w2 = sb("gate_w2", [16, 256])
        cmp_w2 = sb("cmp_w2", [P, 2, DH])
        pos_rows = sb("pos_rows", [SUB, 2, P])
        posT = sb("posT", [P, 2, SUB])
        cmp_h = sb("cmp_h", [P, 2, 2 * N_CMP])
        k_cmpT = sb("k_cmpT", [P, 2 * N_CMP])
        v_cmp = sb("v_cmp", [N_CMP, 2, DH])
        nsa_gate = sb("nsa_gate", [P, TT, 3 * HEADS])
        gla_stat = sb("gla_stat", [P, 3, TT * GLA_HEADS])
        rel2 = sb("rel2", [BUCKETS, HEADS])
        SCR = SLOT * RING
        ARENA = SCR + 19456
        arena = sb("arena", [P, ARENA])
        slot = [arena[:, SLOT * r:SLOT * (r + 1)] for r in range(RING)]

        def piece(at, *shape):
            n = int(np.prod(shape))
            assert at + n <= ARENA, (at, shape)
            v = arena[:, at:at + n]
            if len(shape) == 2:
                v = v.rearrange("p (a b) -> p a b", b=shape[1])
            if len(shape) == 3:
                v = v.rearrange("p (a b c) -> p a b c", b=shape[1], c=shape[2])
            if len(shape) == 4:
                v = v.rearrange("p (a b c d) -> p a b c d", b=shape[1], c=shape[2], d=shape[3])
            return v

        def scratch(at, *shape):
            return piece(SCR + at, *shape)

        xn = scratch(0, TT, D)
        att_p = scratch(2048, 2, T)
        att_pt = scratch(2560, 2, 2, P)
        vrows = scratch(2048, P)
        B0 = 3072
        z_tok = scratch(B0, 3, TT, 512)
        sq_tok = scratch(B0 + 3072, 2, TT, 512)
        qT = scratch(B0 + 5120, 4, T)
        kT = scratch(B0 + 6144, 4, T)
        convT = scratch(B0 + 7168, 12, T)
        sigT = scratch(B0 + 10240, 16, T)
        bias1 = scratch(B0 + 14336, HEADS, T)
        mixT = scratch(B0 + 3072, 8, T)
        cin = scratch(B0, 4, T + 2)
        mT = scratch(B0 + 5120, KT, T)
        wgr = scratch(B0, KT, 36)
        silu_h = scratch(B0 + 512, FT, T)
        hidT = scratch(B0 + 2048, FT, T)
        p_tok = scratch(B0, TT, 256)
        pT = scratch(B0 + 512, 2, T)
        gate_t = scratch(B0 + 1024, TT, D)
        gqkT = scratch(B0, 4, T)
        gv = scratch(B0 + 1024, TT, 512)
        gr = scratch(B0 + 2048, TT, 512)
        loga = scratch(B0 + 3072, 2, T)
        bcum = scratch(B0 + 3584, 2, T)
        nqT = scratch(B0 + 4096, 4, T)
        kvT = scratch(B0 + 5120, 4, T)
        v_sw = scratch(B0 + 6144, 2, TT, P)
        dupT = scratch(B0 + 6656, 4, T)
        catT = scratch(B0 + 7680, KT, T)
        q_dec = scratch(B0 + 9728, 2, T)
        gla_a = scratch(B0 + 10240, GLA_HEADS, 2, T)
        diag = scratch(B0 + 12288, NSUB, SUB, SUB)
        k_dec = scratch(0, 2, 2, T)
        o_gla = scratch(1024, TT, 512)
        cmp_w1 = scratch(B0 + 10240, 2, SUB, P)
        cmp_in = scratch(B0 + 14336, 2, SUB, 2, N_CMP)
        bias_sw = scratch(B0 + 10240, HEADS, T)
        bias_c = scratch(B0 + 12288, HEADS, T)
        dist_oh = scratch(B0 + 9728, T)
        dist_row = scratch(B0 + 10240, TAB)
        mem_tok = scratch(B0, TT, D)
        xkT = scratch(B0 + 2048, KT, T)
        xv = scratch(B0 + 4096, TT, D)
        xqT = scratch(B0 + 6144, KT, T)
        xoT = scratch(B0 + 8192, KT, T)
        TABLE = NKEYS * T
        gtab = piece(0, NKEYS, T)
        PR = 4
        down = [piece(TABLE + D * r, D) for r in range(PR)]
        up = [piece(TABLE + D * (PR + r), D) for r in range(PR)]
        XT = TABLE + 2 * PR * D
        downT = piece(XT, 2, KT, P)
        idxT = piece(XT, 3, T)
        eh = piece(XT + 2048, 2, T)
        ea = piece(XT + 2560, 2, T)
        hot = piece(XT + 2048, 2, 2, 2, P)
        Q0 = SCR + B0
        pqT = piece(Q0, PH, T)
        sk_rows = piece(Q0 + 2048, 16, DH)
        skT = piece(Q0 + 3072, PH, P)
        sc = piece(0, TT, 16, NKEYS)
        sc2 = piece(4096, TT, 16, NKEYS)
        tv = piece(8192, TT, 16, TOPK)
        tif = piece(8704, TT, 16, TOPK)
        ti = piece(9216, TT, 16, TOPK).bitcast(U32)
        cand = piece(9728, TT, PH, TOPK, TOPK)
        cand2 = piece(13824, TT, PH, 256)
        cv = piece(17920, TT, PH, TOPK)
        ci = piece(18176, TT, PH, TOPK).bitcast(U32)
        cab = piece(18432, 2, TT, PH * TOPK).bitcast(U32)
        cabf = piece(18944, 2, TT, PH * TOPK)
        eq = piece(19456, PH * TOPK, TOPK)
        fin3 = piece(21504, 3, TT, PH * TOPK)
        psum16 = piece(22272, 2, TT * PH)
        gfin = scratch(B0, D)
        iota16 = iota[:, 0:TOPK]

        first, later = weight_slots(w)
        NF = len(first)
        MOE_AT, LATE_AT = NF, NF + 3 * EXPERTS
        landed = [S(f"slot_landed_{r}") for r in range(RING)]
        split_slots = [n for n, pieces in enumerate(first) if len(pieces) > 1]

        def slot_ready(eng, n, i=0):
            extra = sum(1 for m in split_slots if m % RING == n % RING and m <= n)
            eng.wait_ge(landed[n % RING], i * 16 + 16 * (n // RING + 1 + extra))

        def slot_view(n, kt, width):
            return slot[n % RING][:, 0:kt * width].rearrange("p (k n) -> p k n", n=width)

        def col(name, k):
            c = COL[name] + k
            return vecs[:, c:c + 1]

        phases = {}

        def phase_end(eng, key):
            phases[key] = phases.get(key, 0) + 1
            eng.drain().then_inc(S("phase"), 1)
            eng.wait_ge(S("phase"), 3 * phases[key])

        def units_block1():
            for qt in range(TT):
                for head in range(HEADS):
                    r, nb = DH * (head % 2), qt + 1
                    q0 = P * qt
                    yield dict(
                        q=[qT[r:r + DH, head // 2, q0:q0 + P]], k=[kT[r:r + DH, head // 2, 0:P * nb]], n=P * nb,
                        bias=[bias1[:, head, q0 - P * b:q0 - P * b + P] for b in range(nb)],
                        v=[[z_tok[:, 2, b, DH * head:DH * head + DH] for b in range(nb)]],
                        gate=None, base=r, start=True, last=True,
                        dest=mixT[:, head // 2, q0:q0 + P] if head % 2 else None)

        def units_nsa():
            for qt in range(TT):
                q0 = P * qt
                for head in range(HEADS):
                    r, g, nb = DH * (head % 2), head // 4, qt + 1
                    q = [nqT[r:r + DH, head // 2, q0:q0 + P]]
                    yield dict(
                        q=q, k=[k_cmpT[r:r + DH, N_CMP * g:N_CMP * g + N_CMP]], n=N_CMP,
                        bias=[bias_c[0:N_CMP, head, q0:q0 + P]], v=[[v_cmp[:, g, :]]],
                        gate=nsa_gate[:, qt, 3 * head:3 * head + 1], base=r, start=True, last=False, dest=None)
                    for b3 in range(2):
                        yield dict(
                            q=q, k=[dupT[r:r + DH, 2 * b3 + g, 0:P * nb]], n=P * nb,
                            bias=[bias_sw[:, head, q0 - P * b:q0 - P * b + P] for b in range(nb)],
                            v=[[v_sw[:, b3, b, DH * g:DH * g + DH] for b in range(nb)]],
                            gate=nsa_gate[:, qt, 3 * head + 1 + b3:3 * head + 2 + b3], base=r,
                            start=False, last=b3 == 1,
                            dest=catT[:, 4 + head // 2, q0:q0 + P] if head % 2 and b3 == 1 else None)

        def units_cross():
            for qt in range(TT):
                q0 = P * qt
                for head in range(XHEADS):
                    yield dict(
                        q=[xqT[:, 2 * head + c, q0:q0 + P] for c in range(2)],
                        k=[xkT[:, 2 * head + c, :] for c in range(2)], n=T, bias=[],
                        v=[[xv[:, b, 256 * head + P * c:256 * head + P * c + P] for b in range(2)] for c in range(2)],
                        gate=None, base=0, start=True, last=True, dest=xoT[:, 2 * head:2 * head + 2, q0:q0 + P])

        n1, n2 = len(list(units_block1())), len(list(units_nsa()))
        ATT1, NSA, CROSS = (0, 0), (n1, HEADS), (n1 + n2, 2 * HEADS)

        def attention_pe(pe, at, units):
            units = list(units)
            u0, g0 = at
            group = 0

            def scores(u):
                a = units[u]
                if u >= 2:
                    pe.wait_ge(S("att_exp"), u0 + u - 1)
                s = bank[u % 2][:, 0:a["n"]]
                last = len(a["bias"]) == 0
                for c, (q, k) in enumerate(zip(a["q"], a["k"])):
                    mm = nc.tensor.matmul(s, lhsT=q, rhs=k, start=c == 0, stop=last and c == len(a["q"]) - 1)
                for b, bias in enumerate(a["bias"]):
                    n = min(P, a["n"])
                    mm = nc.tensor.matmul(bank[u % 2][:, P * b:P * b + n], lhsT=bias, rhs=mirror[0:n, P - n:P],
                                          start=False, stop=b == len(a["bias"]) - 1)
                mm.then_inc(S("att_scores"), 1)

            def turn(u):
                a = units[u]
                pe.wait_ge(S("att_probs"), u0 + u + 1)
                if u >= 2:
                    pe.wait_ge(S("att_turned"), u0 + u - 1)
                nb = (a["n"] + P - 1) // P
                n = min(P, a["n"])
                for b in range(nb):
                    mm = nc.tensor.transpose(bank[2 + u % 2][0:n, P * b:P * b + P],
                                             att_p[:, u % 2, P * b:P * b + n], ident[:, :])
                mm.then_inc(S("att_turns"), 1)

            def values(u):
                nonlocal group
                a = units[u]
                pe.wait_ge(S("att_turned"), u0 + u + 1)
                if group >= 2 and a["start"]:
                    pe.wait_ge(S("att_out"), g0 + group - 1)
                n = min(P, a["n"])
                for c, blocks in enumerate(a["v"]):
                    for b, v in enumerate(blocks):
                        o = bank[4 + group % 2][a["base"]:a["base"] + v.shape[1], P * c:P * c + P]
                        mm = nc.tensor.matmul(o, lhsT=v, rhs=att_pt[0:n, u % 2, b, :],
                                              start=a["start"] and b == 0, stop=a["last"] and b == len(blocks) - 1)
                mm.then_inc(S("att_values"), 1)
                if a["dest"] is not None:
                    group += 1

            for u in range(len(units) + 2):
                if u < len(units):
                    scores(u)
                if 0 <= u - 1 < len(units):
                    turn(u - 1)
                if u >= 2:
                    values(u - 2)

        def attention_dve(dve, at, units):
            units = list(units)
            u0, g0 = at

            def peak(u):
                dve.wait_ge(S("att_scores"), u0 + u + 1)
                if u >= 2:
                    dve.wait_ge(S("att_exp"), u0 + u - 1)
                nc.vector.tensor_reduce(unit[:, 0, u % 2:u % 2 + 1], bank[u % 2][:, 0:units[u]["n"]], X, ALU.max,
                                        negate=True).then_inc(S("att_max"), 1)

            def norm(u):
                a = units[u]
                n = a["n"]
                dve.wait_ge(S("att_exp"), u0 + u + 1)
                nc.vector.reciprocal(unit[:, 2, u % 2:u % 2 + 1], unit[:, 1, u % 2:u % 2 + 1]).then_inc(
                    S("att_inv"), 1)
                dve.wait_ge(S("att_inv"), u0 + u + 1)
                if a["gate"] is None:
                    ins = nc.vector.tensor_scalar(att_p[:, u % 2, 0:n], att_p[:, u % 2, 0:n],
                                                  unit[:, 2, u % 2:u % 2 + 1], None, ALU.mult)
                else:
                    ins = nc.vector.tensor_scalar(att_p[:, u % 2, 0:n], att_p[:, u % 2, 0:n],
                                                  unit[:, 2, u % 2:u % 2 + 1], a["gate"], ALU.mult, ALU.mult)
                ins.then_inc(S("att_probs"), 1)

            for u in range(len(units) + 1):
                if u < len(units):
                    peak(u)
                if u >= 1:
                    norm(u - 1)

        def attention_act(act, at, units):
            units = list(units)
            u0, g0 = at
            group = 0

            def exps(u):
                n = units[u]["n"]
                act.wait_ge(S("att_max"), u0 + u + 1)
                if u >= 2:
                    act.wait_ge(S("att_turns"), u0 + u - 1)
                nc.scalar.activation(att_p[:, u % 2, 0:n], bank[u % 2][:, 0:n], ACT.Exp,
                                     bias=unit[:, 0, u % 2:u % 2 + 1],
                                     accum_out=unit[:, 1, u % 2:u % 2 + 1]).then_inc(S("att_exp"), 1)

            def copy(u):
                nb, n = (units[u]["n"] + P - 1) // P, min(P, units[u]["n"])
                act.wait_ge(S("att_turns"), u0 + u + 1)
                if u >= 2:
                    act.wait_ge(S("att_values"), u0 + u - 1)
                nc.scalar.copy(att_pt[0:n, u % 2, 0:nb, :].rearrange("p b q -> p (b q)"),
                               bank[2 + u % 2][0:n, 0:P * nb]).then_inc(S("att_turned"), 1)

            def outs(u):
                nonlocal group
                dest = units[u]["dest"]
                if dest is None:
                    return
                act.wait_ge(S("att_values"), u0 + u + 1)
                src = bank[4 + group % 2]
                if len(units[u]["v"]) == 2:
                    src = src[:, 0:2 * P].rearrange("p (c q) -> p c q", c=2)
                else:
                    src = src[:, 0:P]
                nc.scalar.copy(dest, src).then_inc(S("att_out"), 1)
                group += 1

            for u in range(len(units) + 2):
                if u < len(units):
                    exps(u)
                if 0 <= u - 1 < len(units):
                    copy(u - 1)
                if u >= 2:
                    outs(u - 2)

        NORMS = ["mix", "ffn", "ple", "mix2", "mem", "xa", "peer", "fin"]

        def wait_nT(eng, tag, k):
            eng.wait_ge(S("norm_nT"), KT * NORMS.index(tag) + k)

        def norm_act(act, chain, tag, src):
            for t in range(TT):
                chain(nc.scalar.activation(xn[:, t, :], src[:, t, :], ACT.Square, accum_out=stat[:, 0, t:t + 1]))
            nc.scalar.activation(stat[:, 1, :], stat[:, 0, :], ACT.Sqrt, bias=eps[:, 0:1],
                                 scale=1.0 / D).then_inc(S("norm_rms"), 1)

        def norm_dve(dve, chain, tag, src, gain):
            dve.wait_ge(S("norm_rms"), NORMS.index(tag) + 1)
            chain(nc.vector.reciprocal(stat[:, 2, :], stat[:, 1, :]))
            for t in range(TT):
                nc.vector.tensor_scalar(xn[:, t, :], src[:, t, :], stat[:, 2, t:t + 1], None,
                                        ALU.mult).then_inc(S("norm_xn"), 1)
            for k in range(KT):
                if k % 2 == 0:
                    dve.wait_ge(S("norm_turned"), 4 * NORMS.index(tag) + k // 2 + 1)
                nc.vector.tensor_scalar(nT[:, k, :], bank[k // 2][:, T * (k % 2):T * (k % 2) + T], col(gain, k),
                                        None, ALU.mult).then_inc(S("norm_nT"), 1)

        def norm_pe(pe, tag):
            pe.wait_ge(S("norm_xn"), TT * (NORMS.index(tag) + 1))
            for k in range(KT):
                for t in range(TT):
                    at = T * (k % 2) + P * t
                    mm = nc.tensor.transpose(bank[k // 2][:, at:at + P], xn[:, t, P * k:P * k + P], ident[:, :])
                if k % 2:
                    mm.then_inc(S("norm_turned"), 1)

        tile_no = {}
        spent_at = {}

        def tile_bank(pe, tag):
            n = tile_no[tag] = len(tile_no)
            if n >= 4:
                pe.wait_ge(S("tile_read"), n - 3)
            return bank[4 + n % 4]

        def project_T(pe, tag, wv, kt, c0, cols, src):
            b = tile_bank(pe, tag)
            for k in range(kt):
                mm = nc.tensor.matmul(b[0:cols, 0:T], lhsT=wv[:, k, c0:c0 + cols], rhs=src[:, k, :],
                                      start=k == 0, stop=k == kt - 1)
            mm.then_inc(S("tile_done"), 1)

        def project_tok(pe, tag, wv, kt, c0, cols, t, src, bias=None):
            b = tile_bank(pe, tag)
            if bias is not None:
                nc.tensor.matmul(b[:, 0:cols], lhsT=ones[0:1, :], rhs=bias, start=True, stop=False)
            for k in range(kt):
                mm = nc.tensor.matmul(b[:, 0:cols], lhsT=src[:, k, P * t:P * t + P], rhs=wv[:, k, c0:c0 + cols],
                                      start=k == 0 and bias is None, stop=k == kt - 1)
            mm.then_inc(S("tile_done"), 1)

        def spent(n):
            spent_at[n] = len(tile_no)

        def tile_in(eng, tag):
            n = tile_no[tag]
            eng.wait_ge(S("tile_done"), n + 1)
            return bank[4 + n % 4]

        def residual_pe(pe, tag, at, src):
            for j in range(2):
                slot_ready(pe, at + j)
                for t in range(TT):
                    project_tok(pe, (tag, j, t), slot_view(at + j, KT, 512), KT, 0, 512, t, src)
                spent(at + j)

        def residual_dve(dve, tag):
            for j in range(2):
                for t in range(TT):
                    b = tile_in(dve, (tag, j, t))
                    hs = h[:, t, 512 * j:512 * j + 512]
                    nc.vector.tensor_tensor(hs, hs, b[:, :], ALU.add).then_inc(S("tile_read"), 1)

        def spread(ap, n):
            return ap.unsqueeze(len(ap.shape)).to_broadcast(list(ap.shape) + [n])

        def toeplitz(tensor, offset, step, rows, heads, pitch, width):
            return bass.AP(tensor=tensor, offset=offset, ap=[[step, rows], [pitch, heads], [1, width]])

        block = ctx.enter_context(nc.Block())

        @block.tensor
        def _(pe):
            pe.wait_ge(S("consts"), 1)
            pe.wait_ge(S("vrows_landed"), 16 * NVROWS)
            nc.tensor.transpose(bank[0][:, 0:NVEC], vrows[0:NVEC, :], ident[0:NVEC, 0:NVEC]).then_inc(S("vecs_turned"), 1)
            pe.wait_ge(S("table_in"), 32)
            nc.tensor.matmul(bank[1][0:HEADS, 0:T], lhsT=rel2[:, :], rhs=dist_oh[0:BUCKETS, :], start=True,
                             stop=True).then_inc(S("table_done"), 1)
            phase_end(pe, "pe")

            norm_pe(pe, "mix")
            wait_nT(pe, "mix", KT)
            pe.wait_ge(S("brow_in"), 16)
            for s in range(3):
                slot_ready(pe, s)
                for t in range(TT):
                    project_tok(pe, ("qkv", s, t), slot_view(s, KT, 512), KT, 0, 512, t, nT,
                                brow[0:1, 512 * s:512 * s + 512])
                spent(s)
            for s in range(3, 10):
                slot_ready(pe, s)
                for m in range(4):
                    project_T(pe, ("in1", 4 * (s - 3) + m), slot_view(s, KT, 512), KT, P * m, P, nT)
                spent(s)
            phase_end(pe, "pe")

            for s in range(2):
                pe.wait_ge(S("qk_normed"), s + 1)
                for m in range(4):
                    for t in range(TT):
                        at = T * (m % 2) + P * t
                        mm = nc.tensor.transpose(bank[2 * s + m // 2][:, at:at + P],
                                                 z_tok[:, s, t, P * m:P * m + P], ident[:, :])
                mm.then_inc(S("qk_turned"), 1)
            phase_end(pe, "pe")
            attention_pe(pe, ATT1, units_block1())
            phase_end(pe, "pe")
            pe.wait_ge(S("conv_done"), 4)
            for s in range(10, 12):
                slot_ready(pe, s)
                wv = slot_view(s, KT, 512)
                for m in range(4):
                    b = tile_bank(pe, ("mix", 4 * (s - 10) + m))
                    for part in range(2):
                        for k in range(4):
                            mm = nc.tensor.matmul(b[:, T * part:T * part + T],
                                                  lhsT=wv[:, 4 * part + k, P * m:P * m + P],
                                                  rhs=mixT[:, 4 * part + k, :], start=k == 0, stop=k == 3)
                    mm.then_inc(S("tile_done"), 1)
                spent(s)
            pe.wait_ge(S("mT_ready"), KT)
            residual_pe(pe, "wo", 12, mT)
            phase_end(pe, "pe")

            norm_pe(pe, "ffn")
            wait_nT(pe, "ffn", KT)
            pe.wait_ge(S("router_in"), 16 * 4)
            for t in range(TT):
                project_tok(pe, ("router", t), wgr, KT, 0, 36, t, nT, br36[0:1, :])
            phase_end(pe, "pe")
            with pe.Fori(0, EXPERTS // 2) as i:
                for j in range(2):
                    n = MOE_AT + 3 * j
                    slot_ready(pe, n, i)
                    slot_ready(pe, n + 1, i)
                    w1v, w3v = slot_view(n, KT, FF), slot_view(n + 1, KT, FF)
                    for f in range(FT):
                        pe.wait_ge(S("moe_hidden"), i * (2 * FT) + (FT * j + f + 1))
                        for part, wv in enumerate((w1v, w3v)):
                            for k in range(KT):
                                mm = nc.tensor.matmul(bank[f][:, T * part:T * part + T],
                                                      lhsT=wv[:, k, P * f:P * f + P], rhs=nT[:, k, :],
                                                      start=k == 0, stop=k == KT - 1)
                        mm.then_inc(S("moe_products"), 1)
                    slot_ready(pe, n + 2, i)
                    w2v = slot_view(n + 2, FT, D)
                    pe.wait_ge(S("moe_hidden"), i * (2 * FT) + FT * (j + 2))
                    for c in range(4):
                        t, half = c // 2, c % 2
                        pe.wait_ge(S("moe_added"), i * 8 + (4 * j + c + 1))
                        for f in range(FT):
                            mm = nc.tensor.matmul(bank[4 + c][:, :], lhsT=hidT[:, f, P * t:P * t + P],
                                                  rhs=w2v[:, f, 512 * half:512 * half + 512],
                                                  start=f == 0, stop=f == FT - 1)
                        mm.then_inc(S("moe_out"), 1)
            phase_end(pe, "pe")

            norm_pe(pe, "ple")
            pe.wait_ge(S("ple_in"), 32)
            for k in range(2):
                for t in range(TT):
                    wait_nT(pe, "ple", 2)
                    mm = nc.tensor.transpose(bank[0][:, T * k + P * t:T * k + P * t + P],
                                             p_tok[:, t, P * k:P * k + P], ident[:, :])
            mm.then_inc(S("p_turned"), 1)
            wait_nT(pe, "ple", KT)
            for j in range(2):
                n = LATE_AT + j
                slot_ready(pe, n)
                for t in range(TT):
                    project_tok(pe, ("gate", j, t), slot_view(n, KT, 512), KT, 0, 512, t, nT,
                                brow[0:1, 512 * j:512 * j + 512])
                spent(n)
            pe.wait_ge(S("pT_ready"), 1)
            n = LATE_AT + 2
            slot_ready(pe, n)
            for j in range(2):
                for t in range(TT):
                    project_tok(pe, ("ple", j, t), slot_view(n, 2, D), 2, 512 * j, 512, t, pT)
            spent(n)
            phase_end(pe, "pe")

            norm_pe(pe, "mix2")
            wait_nT(pe, "mix2", KT)
            n = LATE_AT + 3
            slot_ready(pe, n)
            for m in range(4):
                project_T(pe, ("gqk", m), slot_view(n, KT, 512), KT, P * m, P, nT)
            spent(n)
            for s in range(2):
                slot_ready(pe, n + 1 + s)
                for t in range(TT):
                    project_tok(pe, ("gvr", s, t), slot_view(n + 1 + s, KT, 512), KT, 0, 512, t, nT)
                spent(n + 1 + s)
            slot_ready(pe, n + 3)
            for m in range(4):
                project_T(pe, ("nq", m), slot_view(n + 3, KT, 512), KT, P * m, P, nT)
            spent(n + 3)
            slot_ready(pe, n + 4)
            for m in range(3):
                project_T(pe, ("kv", m), slot_view(n + 4, KT, 384), KT, P * m, P, nT)
            spent(n + 4)
            slot_ready(pe, n + 5)
            wv = slot_view(n + 5, KT, 408)
            project_T(pe, ("kv", 3), wv, KT, P, P, nT)
            for s in range(2):
                for t in range(TT):
                    project_tok(pe, ("vsw", s, t), wv, KT, 256 * s, P, t, nT)
            for t in range(TT):
                project_tok(pe, ("ng", t), wv, KT, 384, 24, t, nT)
            spent(n + 5)
            pe.wait_ge(S("late_in"), 16 * NLATE)
            project_T(pe, ("glr", 0), w_glr, KT, 0, 16, nT)
            pe.wait_ge(S("glr_ready"), 1)
            for c in range(2):
                b = tile_bank(pe, ("loga", c))
                nc.tensor.matmul(b[:, 0:T], lhsT=gate_w2[:, P * c:P * c + P], rhs=glrT[:, :], start=True,
                                 stop=True).then_inc(S("tile_done"), 1)
            phase_end(pe, "pe")

            for b, m in ((0, 0), (1, 1), (4, 2), (5, 3)):
                for g in range(2):
                    mm = nc.tensor.matmul(bank[b][:, T * g:T * g + T], lhsT=sel_dup[:, g, :], rhs=kvT[:, m, :],
                                          start=True, stop=True)
                mm.then_inc(S("dup_done"), 1)
            for s in range(2):
                mm = nc.tensor.transpose(bank[6][:, SUB * s:SUB * s + SUB], pos_rows[:, s, :], ident[0:SUB, 0:SUB])
            mm.then_inc(S("pos_turned"), 1)
            pe.wait_ge(S("cmp_in_ready"), 2)
            for s in range(2):
                for i in range(SUB):
                    mm = nc.tensor.matmul(bank[2][:, 32 * s:32 * s + 2 * N_CMP], lhsT=cmp_w1[:, s, i, :],
                                          rhs=cmp_in[:, s, i, :, :].rearrange("p g n -> p (g n)"),
                                          start=i == 0, stop=i == SUB - 1)
            mm.then_inc(S("cmp_hidden"), 1)
            pe.wait_ge(S("cmp_gelu"), 1)
            for half in range(2):
                nc.tensor.matmul(bank[3][DH * half:DH * half + DH, 0:2 * N_CMP], lhsT=cmp_w2[:, 0, :],
                                 rhs=cmp_h[:, 0, :], start=True, stop=True)
            for g in range(2):
                mm = nc.tensor.matmul(bank[7][0:N_CMP, DH * g:DH * g + DH],
                                      lhsT=cmp_h[:, 1, N_CMP * g:N_CMP * g + N_CMP], rhs=cmp_w2[:, 1, :],
                                      start=True, stop=True)
            mm.then_inc(S("cmp_out"), 1)
            phase_end(pe, "pe")

            pe.wait_ge(S("q_dec_ready"), 2)
            for u in range(NSUB):
                for c in range(2):
                    pe.wait_ge(S("k_dec_ready"), 2 * u + c + 1)
                    for r in range(2):
                        rows = slice(DH * r, DH * r + DH)
                        for st in range(1 if u < NSUB // 2 else 2):
                            mm = nc.tensor.matmul(bank[2 * c + r][:, T * st + SUB * u:T * st + SUB * u + SUB],
                                                  lhsT=k_dec[rows, u % 2, c, P * st:P * st + P],
                                                  rhs=q_dec[rows, c, SUB * u:SUB * u + SUB], start=True, stop=True)
                    mm.then_inc(S("k_dec_used"), 1)
            for c in range(2):
                pe.wait_ge(S("diag_ready"), c + 1)
                for r in range(2):
                    rows = slice(DH * r, DH * r + DH)
                    dv = diag[rows, :, :, :].rearrange("p u t j -> p (u t) j")
                    for j in range(SUB):
                        mm = nc.tensor.matmul(bank[4 + 2 * c + r][:, 0:T], lhsT=modmask[rows, SUB - 1 - j:SUB - 1 - j + P],
                                              rhs=dv[:, :, j], start=j == 0, stop=j == SUB - 1)
                mm.then_inc(S("diag_used"), 1)
            pe.wait_ge(S("gla_a_ready"), 1)
            for t in range(TT):
                for hh in range(GLA_HEADS):
                    for st in range(t + 1):
                        mm = nc.tensor.matmul(bank[t][:, P * hh:P * hh + P], lhsT=gla_a[:, hh, st, P * t:P * t + P],
                                              rhs=gv[:, st, P * hh:P * hh + P], start=st == 0, stop=st == t)
            mm.then_inc(S("gla_out"), 1)
            pe.wait_ge(S("gla_normed"), 1)
            for hh in range(GLA_HEADS):
                for t in range(TT):
                    at = T * (hh % 2) + P * t
                    mm = nc.tensor.transpose(bank[2 + hh // 2][:, at:at + P], o_gla[:, t, P * hh:P * hh + P],
                                             ident[:, :])
            mm.then_inc(S("gla_turned"), 1)
            phase_end(pe, "pe")
            pe.wait_ge(S("bias2_in"), 32)
            attention_pe(pe, NSA, units_nsa())
            phase_end(pe, "pe")
            residual_pe(pe, "wout", LATE_AT + 9, catT)
            phase_end(pe, "pe")

            norm_pe(pe, "mem")
            wait_nT(pe, "mem", KT)
            for s in range(2):
                n = LATE_AT + 11 + s
                slot_ready(pe, n)
                for m in range(4):
                    project_T(pe, ("xk", 4 * s + m), slot_view(n, KT, 512), KT, P * m, P, nT)
                spent(n)
            residual_pe(pe, "xv", LATE_AT + 13, nT)
            phase_end(pe, "pe")
            norm_pe(pe, "xa")
            wait_nT(pe, "xa", KT)
            for s in range(2):
                n = LATE_AT + 15 + s
                slot_ready(pe, n)
                for m in range(4):
                    project_T(pe, ("xq", 4 * s + m), slot_view(n, KT, 512), KT, P * m, P, nT)
                spent(n)
            phase_end(pe, "pe")
            attention_pe(pe, CROSS, units_cross())
            phase_end(pe, "pe")
            residual_pe(pe, "xo", LATE_AT + 17, xoT)
            phase_end(pe, "pe")
            phases["rings free"] = phases["pe"]

            norm_pe(pe, "peer")
            pe.wait_ge(S("sk_in"), 16)
            for hh in range(PH):
                wait_nT(pe, "peer", 4)
                mm = nc.tensor.transpose(bank[hh // 4][:, P * (hh % 4):P * (hh % 4) + P],
                                         sk_rows[:, 2 * hh:2 * hh + 2, :].rearrange("p a d -> p (a d)"), ident[:, :])
            mm.then_inc(S("sk_turned"), 1)
            wait_nT(pe, "peer", KT)
            for s in range(2):
                n = LATE_AT + 19 + s
                slot_ready(pe, n)
                for m in range(4):
                    project_T(pe, ("pq", 4 * s + m), slot_view(n, KT, 512), KT, P * m, P, nT)
                spent(n)
            phase_end(pe, "pe")
            for t in range(TT):
                for q in range(4):
                    for x in range(4):
                        hp = 2 * (4 * (q % 2) + x) + q // 2
                        rows = slice(DH * (hp % 2), DH * (hp % 2) + DH)
                        mm = nc.tensor.matmul(bank[4 * t + q][:, P * x:P * x + P],
                                              lhsT=pqT[rows, hp // 2, P * t:P * t + P], rhs=skT[rows, hp // 2, :],
                                              start=True, stop=True)
                    mm.then_inc(S("peer_scores"), 1)
            phase_end(pe, "pe")
            for a in range(3):
                pe.wait_ge(S("peer_top"), 1)
                for t in range(TT):
                    mm = nc.tensor.transpose(bank[a][:, P * t:P * t + P], fin3[:, a, t, :], ident[:, :])
                mm.then_inc(S("top_turned"), 1)
            phase_end(pe, "pe")

            def gate_group(i, q):
                for pair in range(2):
                    pe.wait_ge(S("hot_ready"), i * 8 + (2 * q + pair + 1))
                    if pair == 0:
                        pe.wait_ge(S("gate_read"), i * 4 + (q + 1))
                    for x in range(2):
                        tok = 2 * pair + x
                        mm = nc.tensor.matmul(bank[4 + q][:, P * tok:P * tok + P], lhsT=hot[:, pair, x, 1, :],
                                              rhs=hot[:, pair, x, 0, :], start=True, stop=True)
                    if pair == 0:
                        mm.then_inc(S("hot_used0"), 1)
                mm.then_inc(S("hot_used1"), 1)

            with pe.Fori(0, T // 16) as i:
                for q in range(4):
                    gate_group(i, q)
            phase_end(pe, "pe")

            def turn(t, r, i, first=False):
                pe.wait_ge(S(f"down_landed_{r}"), i * 16 + 16)
                if not first:
                    pe.wait_ge(S("copied_a"), t)
                    pe.wait_ge(S("copied_b"), t)
                for k in range(KT):
                    mm = nc.tensor.transpose(bank[4 + k // 4][:, P * (k % 4):P * (k % 4) + P],
                                             down[r][:, P * k:P * k + P], ident[:, :])
                mm.then_inc(S("down_turned"), 1)

            def expert_scores(t, r, early):
                pe.wait_ge(S("copied_a"), t + 1)
                pe.wait_ge(S("copied_b"), t + 1)
                if not early:
                    pe.wait_ge(S("expert_gelu"), t - 1)
                for k in range(KT):
                    mm = nc.tensor.matmul(bank[6 + r % 2][:, 0:T], lhsT=downT[:, r % 2, k, :], rhs=nT[:, k, :],
                                          start=k == 0, stop=k == KT - 1)
                mm.then_inc(S("expert_scored"), 1)

            def expert_out(t, r, i, first_tile, last_tile):
                pe.wait_ge(S("expert_gated"), t + 1)
                pe.wait_ge(S(f"up_landed_{r}"), i * 16 + 16)
                for c in range(4):
                    mm = nc.tensor.matmul(bank[c][:, :], lhsT=ea[:, r % 2, P * (c // 2):P * (c // 2) + P],
                                          rhs=up[r][:, 512 * (c % 2):512 * (c % 2) + 512],
                                          start=first_tile, stop=last_tile, skip_group_check=True)
                mm.then_inc(S("up_used"), 1)

            steps = NKEYS // PR
            turn(0, 0, 0, first=True)
            for t in range(PR):
                turn(t + 1, (t + 1) % PR, (t + 1) // PR)
                expert_scores(t, t, t < 2)
                if t:
                    expert_out(t - 1, t - 1, 0, t == 1, False)
            with pe.Fori(1, steps - 1) as i:
                for r in range(PR):
                    turn(i * PR + (r + 1), (r + 1) % PR, i if r + 1 < PR else i + 1)
                    expert_scores(i * PR + r, r, False)
                    expert_out(i * PR + (r - 1), (r - 1) % PR, i if r else i - 1, False, False)
            for t in range(NKEYS - PR, NKEYS):
                if t + 1 < NKEYS:
                    turn(t + 1, (t + 1) % PR, (t + 1) // PR)
                expert_scores(t, t % PR, False)
                expert_out(t - 1, (t - 1) % PR, (t - 1) // PR, False, False)
            expert_out(NKEYS - 1, PR - 1, steps - 1, False, True)
            phase_end(pe, "pe")

        @block.scalar
        def _(act):
            chain = Chain(act, S("act_chain"))
            for name, rows in ROWS:
                src = w[name][0]
                src = src.rearrange("j (k p) -> (j k) p", p=P) if name == "conv_w" else \
                    src.rearrange("(k p) -> k p", p=P)
                act.dma_start(vrows[COL[name]:COL[name] + rows, :], src).then_inc(S("vrows_landed"), 16)
            for name in ("g_q", "g_k"):
                for half in range(2):
                    act.dma_start(vrows[COL[name]:COL[name] + 1, DH * half:DH * half + DH],
                                  w[name][0:1, :]).then_inc(S("vrows_landed"), 16)
            act.dma_start(dist_oh[0:BUCKETS, :], buckets).then_inc(S("table_in"), 16)
            act.dma_start(rel2[:, :], w["rel_bias_2"]).then_inc(S("table_in"), 16)
            act.dma_start(h[:, :, :], w["x"][0].rearrange("(t p) d -> p t d", p=P)).then_inc(S("x_in"), 16)
            act.dma_start(brow[0:1, :], w["b_in"][0:1, 0:1536]).then_inc(S("brow_in"), 16)
            act.wait_ge(S("table_done"), 1)
            nc.scalar.copy(dist_row[0:HEADS, T:TAB], bank[1][0:HEADS, 0:T]).then_inc(S("table_row"), 1)
            act.wait_ge(S("table_row"), 2)
            act.dma_start(table_dram[:, :], dist_row[0:HEADS, :]).then_inc(S("table_out"), 16)
            act.wait_ge(S("table_out"), 16)
            phase_end(act, "act")

            rel1 = w["rel_bias"]
            act.dma_start(bias1[64:P, :, :], toeplitz(rel1.tensor, 0, 1, 64, HEADS, REL, T)).then_inc(S("bias1_in"), 16)
            act.dma_start(bias1[0:64, :, 64:T],
                          toeplitz(rel1.tensor, 0, 1, 64, HEADS, REL, T - 64)).then_inc(S("bias1_in"), 16)
            act.wait_ge(S("x_in"), 16)
            norm_act(act, chain, "mix", h)
            for s in range(3):
                for t in range(TT):
                    b = tile_in(act, ("qkv", s, t))
                    nc.scalar.copy(z_tok[:, s, t, :], b[:, :]).then_inc(S("tile_read"), 1)
            for m in range(28):
                b = tile_in(act, ("in1", m))
                dst = convT[:, m, :] if m < 12 else sigT[:, m - 12, :]
                nc.scalar.activation(dst, b[:, 0:T], ACT.Identity if m < 12 else ACT.Sigmoid,
                                     bias=col("b_in", 12 + m)).then_inc(S("tile_read"), 1)
            phase_end(act, "act")
            act.wait_ge(S("qk_squares"), 2)
            nc.scalar.activation(qk_stat[:, 1, :], qk_stat[:, 0, :], ACT.Sqrt, bias=eps[:, 0:1],
                                 scale=1.0 / DH).then_inc(S("qk_rms"), 1)
            act.wait_ge(S("bias1_in"), 32)
            phase_end(act, "act")
            attention_act(act, ATT1, units_block1())
            phase_end(act, "act")
            act.dma_start(brow[0:1, 0:D], w["b_ple_gate"]).then_inc(S("ple_in"), 16)
            phase_end(act, "act")

            act.dma_start(wgr[:, :, 0:4], w["w_group"][0].rearrange("(k p) n -> p k n", p=P)).then_inc(S("router_in"), 16)
            act.dma_start(wgr[:, :, 4:36], w["w_router"][0].rearrange("(k p) n -> p k n", p=P)).then_inc(S("router_in"), 16)
            act.dma_start(br36[0:1, 0:4], w["b_group"]).then_inc(S("router_in"), 16)
            act.dma_start(br36[0:1, 4:36], w["b_router"]).then_inc(S("router_in"), 16)
            norm_act(act, chain, "ffn", h)
            for t in range(TT):
                b = tile_in(act, ("router", t))
                nc.scalar.copy(logit[:, t, 0:36], b[:, 0:36]).then_inc(S("tile_read"), 1)
            act.wait_ge(S("tile_read"), tile_no[("router", 1)] + 1)
            act.sem_inc(S("logits"), 1)
            act.wait_ge(S("group_shifted"), 1)
            for t in range(TT):
                nc.scalar.activation(route[:, t, 12:16], route[:, t, 12:16], ACT.Exp,
                                     accum_out=route[:, t, 16:17]).then_inc(S("group_exp"), 1)
            act.wait_ge(S("second_gap"), 1)
            nc.scalar.activation(route[:, :, 18:19], route[:, :, 18:19], ACT.Exp).then_inc(S("second_exp"), 1)
            phase_end(act, "act")
            with act.Fori(0, EXPERTS // 2) as i:
                for j in range(2):
                    for f in range(FT):
                        act.wait_ge(S("moe_products"), i * (2 * FT) + (FT * j + f + 1))
                        act.wait_ge(S("moe_hidden"), i * (2 * FT) + (FT * j + f + 1))
                        nc.scalar.activation(silu_h[:, f, :], bank[f][:, 0:T], ACT.Silu).then_inc(S("moe_silu"), 1)
            phase_end(act, "act")

            act.dma_start(p_tok[:, :, :], w["p"][0, 0].rearrange("(t p) d -> p t d", p=P)).then_inc(S("ple_in"), 16)
            norm_act(act, chain, "ple", h)
            act.wait_ge(S("p_turned"), 1)
            nc.scalar.copy(pT[:, :, :].rearrange("p k t -> p (k t)"), bank[0][:, :]).then_inc(S("pT_ready"), 1)
            for j in range(2):
                for t in range(TT):
                    b = tile_in(act, ("gate", j, t))
                    nc.scalar.activation(gate_t[:, t, 512 * j:512 * j + 512], b[:, :], ACT.Sigmoid).then_inc(
                        S("tile_read"), 1)
            act.wait_ge(S("tile_read"), tile_no[("gate", 1, 1)] + 1)
            act.sem_inc(S("gate_ready"), 1)
            act.dma_start(w_glr[:, :, :], w["w_in_2"][0].rearrange("(k p) n -> p k n", p=P)[:, :, 1536:1552]).then_inc(
                S("late_in"), 16)
            act.dma_start(gate_w2[:, :], w["gla_gate_w2_2"][0]).then_inc(S("late_in"), 16)
            for s, name in enumerate(("k", "v")):
                act.dma_start(cmp_w2[:, s, :], w[f"cmp_{name}_w2_2"][0]).then_inc(S("late_in"), 16)
                act.dma_start(pos_rows[:, s, :], w[f"cmp_pos_{name}_2"][0].rearrange("(i a) d -> i (a d)", a=2)).then_inc(
                    S("late_in"), 16)
            phase_end(act, "act")

            for s, name in enumerate(("k", "v")):
                act.dma_start(cmp_w1[:, s, :, :], w[f"cmp_{name}_w1_2"][0].rearrange("(i p) n -> p i n", p=P)).then_inc(
                    S("cmp_w1_in"), 16)
            norm_act(act, chain, "mix2", h)
            for m in range(4):
                b = tile_in(act, ("gqk", m))
                nc.scalar.activation(gqkT[:, m, :], b[:, 0:T], ACT.Copy, scale=0.125 if m < 2 else 1.0).then_inc(
                    S("tile_read"), 1)
            for s in range(2):
                for t in range(TT):
                    b = tile_in(act, ("gvr", s, t))
                    nc.scalar.activation((gv, gr)[s][:, t, :], b[:, :], (ACT.Copy, ACT.Silu)[s]).then_inc(
                        S("tile_read"), 1)
            for m in range(4):
                b = tile_in(act, ("nq", m))
                nc.scalar.activation(nqT[:, m, :], b[:, 0:T], ACT.Copy, scale=0.125).then_inc(S("tile_read"), 1)
            for m in range(4):
                b = tile_in(act, ("kv", m))
                nc.scalar.copy(kvT[:, m, :], b[:, 0:T]).then_inc(S("tile_read"), 1)
            for s in range(2):
                for t in range(TT):
                    b = tile_in(act, ("vsw", s, t))
                    nc.scalar.copy(v_sw[:, s, t, :], b[:, 0:P]).then_inc(S("tile_read"), 1)
            for t in range(TT):
                b = tile_in(act, ("ng", t))
                nc.scalar.activation(nsa_gate[:, t, :], b[:, 0:24], ACT.Sigmoid).then_inc(S("tile_read"), 1)
            b = tile_in(act, ("glr", 0))
            nc.scalar.copy(glrT[:, :], b[0:16, 0:T]).then_inc(S("tile_read"), 1)
            act.wait_ge(S("tile_read"), tile_no[("glr", 0)] + 1)
            act.sem_inc(S("glr_ready"), 1)
            for c in range(2):
                b = tile_in(act, ("loga", c))
                nc.scalar.activation(loga[:, c, :], b[:, 0:T], ACT.Identity, bias=col("gla_gate_b_2", c)).then_inc(
                    S("tile_read"), 1)
            act.wait_ge(S("tile_read"), tile_no[("loga", 1)] + 1)
            tmp = k_dec[:, 0, :, :]
            chain(nc.scalar.activation(tmp, loga[:, :, :], ACT.Abs))
            chain(nc.scalar.activation(tmp, tmp, ACT.Exp, scale=-1.0))
            nc.scalar.activation(tmp, tmp, ACT.Ln, bias=1.0).then_inc(S("log_part"), 1)
            act.wait_ge(S("cmp_w1_in"), 32)
            phase_end(act, "act")

            act.wait_ge(S("pos_turned"), 1)
            nc.scalar.copy(posT[:, :, :].rearrange("p s i -> p (s i)"), bank[6][:, 0:2 * SUB]).then_inc(S("pos_ready"), 1)
            act.wait_ge(S("dup_done"), 4)
            for s in range(2):
                nc.scalar.copy(dupT[:, 2 * s:2 * s + 2, :].rearrange("p g t -> p (g t)"), bank[4 + s][:, :])
            act.wait_ge(S("cmp_hidden"), 1)
            nc.scalar.activation(cmp_h[:, :, :], bank[2][:, 0:64].rearrange("p (s n) -> p s n", s=2)[:, :, 0:2 * N_CMP],
                                 ACT.Gelu_apprx_tanh).then_inc(S("cmp_gelu"), 1)
            act.wait_ge(S("cmp_out"), 1)
            nc.scalar.copy(k_cmpT[:, :], bank[3][:, 0:2 * N_CMP])
            nc.scalar.copy(v_cmp[:, :, :].rearrange("n g d -> n (g d)"), bank[7][0:N_CMP, 0:P])
            phase_end(act, "act")

            for c in range(2):
                act.wait_ge(S("q_diff"), c + 1)
                nc.scalar.activation(q_dec[:, c, :], q_dec[:, c, :], ACT.Exp).then_inc(S("q_exp"), 1)
            for u in range(NSUB):
                for c in range(2):
                    act.wait_ge(S("k_diff"), 2 * u + c + 1)
                    nc.scalar.activation(k_dec[:, u % 2, c, :], k_dec[:, u % 2, c, :], ACT.Exp, scale=-1.0).then_inc(
                        S("k_exp"), 1)
            for c in range(2):
                act.wait_ge(S("diag_diff"), c + 1)
                nc.scalar.activation(diag[:, :, :, :], diag[:, :, :, :], ACT.Exp).then_inc(S("diag_exp"), 1)
            act.wait_ge(S("gla_out"), 1)
            for t in range(TT):
                nc.scalar.copy(o_gla[:, t, :], bank[t][:, :]).then_inc(S("o_gla_ready"), 1)
            act.wait_ge(S("gla_squares"), 1)
            nc.scalar.activation(gla_stat[:, 1, :], gla_stat[:, 0, :], ACT.Sqrt, bias=eps[:, 0:1],
                                 scale=1.0 / P).then_inc(S("gla_rms"), 1)
            phase_end(act, "act")
            act.dma_start(bias_sw[:, :, :], toeplitz(table_dram, T - P + 1, 1, P, HEADS, TAB, T)).then_inc(S("bias2_in"), 16)
            act.dma_start(bias_c[0:N_CMP, :, :], toeplitz(
                table_dram, T - (CMP_BLOCK - 1) - CMP_STRIDE * (N_CMP - 1), CMP_STRIDE, N_CMP, HEADS, TAB, T)).then_inc(S("bias2_in"), 16)
            attention_act(act, NSA, units_nsa())
            phase_end(act, "act")
            act.dma_start(mem_tok[:, :, :], w["mem_2"][0].rearrange("(t p) d -> p t d", p=P)).then_inc(S("mem_in"), 16)
            phase_end(act, "act")

            act.wait_ge(S("mem_in"), 16)
            norm_act(act, chain, "mem", mem_tok)
            for m in range(KT):
                b = tile_in(act, ("xk", m))
                nc.scalar.copy(xkT[:, m, :], b[:, 0:T]).then_inc(S("tile_read"), 1)
            for j in range(2):
                for t in range(TT):
                    b = tile_in(act, ("xv", j, t))
                    nc.scalar.copy(xv[:, t, 512 * j:512 * j + 512], b[:, :]).then_inc(S("tile_read"), 1)
            phase_end(act, "act")
            norm_act(act, chain, "xa", h)
            for m in range(KT):
                b = tile_in(act, ("xq", m))
                nc.scalar.activation(xqT[:, m, :], b[:, 0:T], ACT.Copy, scale=1.0 / 16).then_inc(S("tile_read"), 1)
            phase_end(act, "act")
            attention_act(act, CROSS, units_cross())
            phase_end(act, "act")
            act.dma_start(sk_rows[:, :, :], w["peer_subkeys_2"][0].rearrange("h a k d -> k (h a) d")).then_inc(
                S("sk_in"), 16)
            phase_end(act, "act")

            norm_act(act, chain, "peer", h)
            act.wait_ge(S("sk_turned"), 1)
            for b in range(2):
                nc.scalar.copy(skT[:, 4 * b:4 * b + 4, :].rearrange("p a k -> p (a k)"), bank[b][:, :])
            for m in range(KT):
                b = tile_in(act, ("pq", m))
                nc.scalar.copy(pqT[:, m, :], b[:, 0:T]).then_inc(S("tile_read"), 1)
            phase_end(act, "act")
            for b in range(8):
                act.wait_ge(S("peer_scores"), b + 1)
                t, q = b // 4, b % 4
                nc.scalar.copy(sc[:, t, 8 * (q % 2) + q // 2:8 * (q % 2) + 8:2, :],
                               bank[b][:, :].rearrange("p (a k) -> p a k", k=NKEYS))
            phase_end(act, "act")
            act.wait_ge(S("gate_shifted"), 1)
            nc.scalar.activation(cv[:, :, :, :], cv[:, :, :, :], ACT.Exp).then_inc(S("gate_exp"), 1)
            for a in range(3):
                act.wait_ge(S("top_turned"), a + 1)
                nc.scalar.copy(idxT[:, a, :], bank[a][:, 0:T])
            phase_end(act, "act")
            with act.Fori(0, T // 16) as i:
                for q in range(4):
                    act.wait_ge(S("hot_used1"), i * 4 + (q + 2))
                    nc.scalar.copy(gtab[:, :, bass.ds(i * 16 + 4 * q, 4)].rearrange("p i t -> p t i"),
                                   bank[4 + q][:, :].rearrange("p (t i) -> p t i", t=4)).then_inc(S("gate_read"), 1)
            phase_end(act, "act")

            def copy_a(t, r, early):
                act.wait_ge(S("down_turned"), t + 1)
                if not early:
                    act.wait_ge(S("expert_scored"), t - 1)
                nc.scalar.copy(downT[:, r % 2, 0:4, :].rearrange("p k e -> p (k e)"), bank[4][:, :]).then_inc(
                    S("copied_a"), 1)

            def gelu(t, r, early):
                act.wait_ge(S("expert_scored"), t + 1)
                if not early:
                    act.wait_ge(S("expert_gated"), t - 1)
                nc.scalar.activation(eh[:, r % 2, :], bank[6 + r % 2][:, 0:T], ACT.Gelu_apprx_tanh).then_inc(
                    S("expert_gelu"), 1)

            copy_a(0, 0, True)
            for t in range(PR):
                copy_a(t + 1, t + 1, t + 1 < 2)
                gelu(t, t, t < 2)
            with act.Fori(1, NKEYS // PR - 1) as i:
                for r in range(PR):
                    copy_a(i * PR + (r + 1), r + 1, False)
                    gelu(i * PR + r, r, False)
            for t in range(NKEYS - PR, NKEYS):
                if t + 1 < NKEYS:
                    copy_a(t + 1, t + 1, False)
                gelu(t, t, False)
            phase_end(act, "act")
            act.dma_start(gfin[:, :], w["norm_final_2"].partition_broadcast(P)).then_inc(S("gfin_in"), 16)
            act.wait_ge(S("h_final"), 4)
            norm_act(act, chain, "fin", h)
            for t in range(TT):
                act.wait_ge(S("fin_out"), t + 1)
                act.dma_start(out[0].rearrange("(t p) d -> p t d", p=P)[:, t, :], h[:, t, :]).then_inc(S("stored"), 16)
            act.wait_ge(S("stored"), 16 * TT)

        @block.vector
        def _(dve):
            chain = Chain(dve, S("dve_chain"))
            dve.wait_ge(S("vecs_turned"), 1)
            nc.vector.tensor_copy(vecs[:, 0:NVEC], bank[0][:, 0:NVEC])
            nc.vector.memset(dist_row[0:HEADS, 0:T], NEG).then_inc(S("table_row"), 1)
            phase_end(dve, "dve")
            dve.wait_ge(S("x_in"), 16)
            norm_dve(dve, chain, "mix", h, "g_mix")
            phase_end(dve, "dve")

            for s in range(2):
                chain(nc.vector.tensor_tensor(sq_tok[:, s, :, :], z_tok[:, s, :, :], z_tok[:, s, :, :], ALU.mult))
                nc.vector.tensor_reduce(qk_stat[:, 0, 16 * s:16 * s + 16],
                                        sq_tok[:, s, :, :].rearrange("p t (a d) -> p (t a) d", d=DH), X,
                                        ALU.add).then_inc(S("qk_squares"), 1)
            dve.wait_ge(S("qk_rms"), 1)
            chain(nc.vector.reciprocal(qk_stat[:, 2, :], qk_stat[:, 1, :]))
            for s in range(2):
                zv = z_tok[:, s, :, :].rearrange("p t (a d) -> p (t a) d", d=DH)
                nc.vector.tensor_tensor(zv, zv, spread(qk_stat[:, 2, 16 * s:16 * s + 16], DH),
                                        ALU.mult).then_inc(S("qk_normed"), 1)
            for s in range(2):
                dve.wait_ge(S("qk_turned"), s + 1)
                for m in range(4):
                    src = bank[2 * s + m // 2][:, T * (m % 2):T * (m % 2) + T]
                    nc.vector.tensor_scalar((qT, kT)[s][:, m, :], src, col(("g_q", "g_k")[s], 0),
                                            (0.125, 1.0)[s], ALU.mult, ALU.mult)
            phase_end(dve, "dve")
            attention_dve(dve, ATT1, units_block1())
            phase_end(dve, "dve")
            chain(nc.vector.memset(cin[:, :, 0:2], 0.0))
            chain(nc.vector.tensor_tensor(cin[:, :, 2:T + 2], convT[:, 8:12, :], convT[:, 0:4, :], ALU.mult))
            for m in range(4):
                y = mixT[:, 4 + m, :]
                chain(nc.vector.tensor_scalar(y, cin[:, m, 0:T], col("conv_w", m), col("conv_b", m), ALU.mult, ALU.add))
                for j in (1, 2):
                    chain(nc.vector.scalar_tensor_tensor(out=y, in0=cin[:, m, j:j + T], scalar=col("conv_w", 4 * j + m),
                                                         in1=y, op0=ALU.mult, op1=ALU.add))
                nc.vector.tensor_tensor(y, y, convT[:, 4 + m, :], ALU.mult).then_inc(S("conv_done"), 1)
            for m in range(KT):
                b = tile_in(dve, ("mix", m))
                chain(nc.vector.tensor_tensor(mT[:, m, :], sigT[:, m, :], b[:, 0:T], ALU.mult))
                chain(nc.vector.tensor_tensor(sigT[:, 8 + m, :], sigT[:, 8 + m, :], b[:, T:2 * T], ALU.mult))
                nc.vector.tensor_tensor(mT[:, m, :], mT[:, m, :], sigT[:, 8 + m, :], ALU.add).then_inc(S("mT_ready"), 1)
                dve.wait_ge(S("mT_ready"), m + 1)
                dve.sem_inc(S("tile_read"), 1)
            residual_dve(dve, "wo")
            phase_end(dve, "dve")

            norm_dve(dve, chain, "ffn", h, "g_ffn")
            dve.wait_ge(S("logits"), 1)
            chain(nc.vector.memset(route[:, :, 4:8], NEG))
            chain(nc.vector.tensor_copy(route[:, :, 0:4], logit[:, :, 0:4]))
            for t in range(TT):
                chain(nc.vector.max(top8[:, t, 0:8], route[:, t, 0:8]))
                chain(nc.vector.max_index(idx8[:, t, 0:8], top8[:, t, 0:8], route[:, t, 0:8]))
            chain(nc.vector.tensor_copy(idx8f[:, :, 0:8], idx8[:, :, 0:8]))
            for t in range(TT):
                r = route[:, t, :]
                chain(nc.vector.tensor_scalar(r[:, 12:16], r[:, 0:4], top8[:, t, 0:1], None, ALU.subtract))
                chain(nc.vector.tensor_scalar(r[:, 8:12], iota[:, 0:4], idx8f[:, t, 0:1], None, ALU.is_equal))
                chain(nc.vector.tensor_scalar(r[:, 20:24], r[:, 8:12], -1.0, -NEG, ALU.add, ALU.mult))
                chain(nc.vector.tensor_tensor(r[:, 24:56].rearrange("p (g e) -> p g e", g=GROUPS),
                                              logit[:, t, 4:36].rearrange("p (g e) -> p g e", g=GROUPS),
                                              spread(r[:, 20:24], PER_GROUP), ALU.add))
                chain(nc.vector.max(top8[:, t, 8:16], r[:, 24:56]))
                chain(nc.vector.max_index(idx8[:, t, 8:16], top8[:, t, 8:16], r[:, 24:56]))
                chain(nc.vector.tensor_tensor(r[:, 18:19], top8[:, t, 9:10], top8[:, t, 8:9], ALU.subtract))
            chain(nc.vector.tensor_copy(idx8f[:, :, 8:16], idx8[:, :, 8:16]))
            dve.sem_inc(S("group_shifted"), 1)
            dve.sem_inc(S("second_gap"), 1)
            dve.wait_ge(S("group_exp"), TT)
            dve.wait_ge(S("second_exp"), 1)
            for t in range(TT):
                r = route[:, t, :]
                chain(nc.vector.reciprocal(r[:, 17:18], r[:, 16:17]))
                chain(nc.vector.tensor_scalar(r[:, 19:20], r[:, 18:19], 1.0, None, ALU.add))
                chain(nc.vector.reciprocal(r[:, 19:20], r[:, 19:20]))
                chain(nc.vector.tensor_tensor(r[:, 56:57], r[:, 19:20], r[:, 17:18], ALU.mult))
                chain(nc.vector.tensor_tensor(r[:, 57:58], r[:, 56:57], r[:, 18:19], ALU.mult))
                chain(nc.vector.tensor_scalar(gatew[:, t, :], iota[:, 0:EXPERTS], idx8f[:, t, 8:9], r[:, 56:57],
                                              ALU.is_equal, ALU.mult))
                chain(nc.vector.tensor_scalar(r[:, 24:56], iota[:, 0:EXPERTS], idx8f[:, t, 9:10], r[:, 57:58],
                                              ALU.is_equal, ALU.mult))
                chain(nc.vector.tensor_tensor(gatew[:, t, :], gatew[:, t, :], r[:, 24:56], ALU.add))
            dve.sem_inc(S("moe_hidden"), FT)
            dve.sem_inc(S("moe_added"), 4)
            phase_end(dve, "dve")
            with dve.Fori(0, EXPERTS // 2) as i:
                for j in range(2):
                    for f in range(FT):
                        dve.wait_ge(S("moe_silu"), i * (2 * FT) + (FT * j + f + 1))
                        dve.wait_ge(S("moe_added"), i * 8 + (4 * j + 4))
                        nc.vector.tensor_tensor(hidT[:, f, :], silu_h[:, f, :], bank[f][:, T:2 * T],
                                                ALU.mult).then_inc(S("moe_hidden"), 1)
                    for c in range(4):
                        t, half = c // 2, c % 2
                        dve.wait_ge(S("moe_out"), i * 8 + (4 * j + c + 1))
                        hs = h[:, t, 512 * half:512 * half + 512]
                        nc.vector.scalar_tensor_tensor(out=hs, in0=bank[4 + c][:, :],
                                                       scalar=gatew[:, t, bass.ds(i * 2 + j, 1)], in1=hs,
                                                       op0=ALU.mult, op1=ALU.add).then_inc(S("moe_added"), 1)
            phase_end(dve, "dve")

            norm_dve(dve, chain, "ple", h, "g_ple")
            dve.wait_ge(S("gate_ready"), 1)
            for j in range(2):
                for t in range(TT):
                    b = tile_in(dve, ("ple", j, t))
                    g = gate_t[:, t, 512 * j:512 * j + 512]
                    hs = h[:, t, 512 * j:512 * j + 512]
                    nc.vector.tensor_tensor(g, g, b[:, :], ALU.mult).then_inc(S("tile_read"), 1)
                    dve.wait_ge(S("tile_read"), tile_no[("ple", j, t)] + 1)
                    nc.vector.tensor_tensor(hs, hs, g, ALU.add)
            phase_end(dve, "dve")

            norm_dve(dve, chain, "mix2", h, "norm_mix_2")
            dve.wait_ge(S("log_part"), 1)
            chain(nc.vector.tensor_scalar(loga[:, :, :], loga[:, :, :], 0.0, None, ALU.min))
            chain(nc.vector.tensor_tensor(loga[:, :, :], loga[:, :, :], k_dec[:, 0, :, :], ALU.subtract))
            chain(nc.vector.tensor_scalar(loga[:, :, :], loga[:, :, :], 0.5 / 16.0, None, ALU.mult))
            for c in range(2):
                nc.vector.tensor_tensor_scan(bcum[:, c, :], loga[:, c, :], loga[:, c, :], 0.0, ALU.add, ALU.add)
            cg = nsa_gate[:, 0, :].rearrange("p (a b) -> p a b", b=3)[:, :, 0]
            nc.vector.tensor_scalar(cg, cg, late_row[:, 0:1], None, ALU.mult)
            phase_end(dve, "dve")

            dve.wait_ge(S("dup_done"), 2)
            dve.wait_ge(S("pos_ready"), 1)
            for s in range(2):
                for g in range(2):
                    for half in range(2):
                        rows = slice(DH * half, DH * half + DH)
                        kv = bank[s][rows, T * g:T * g + T].rearrange("p (n a) -> p a n", a=CMP_STRIDE)
                        for far in range(2):
                            ins = nc.vector.tensor_tensor(
                                cmp_in[rows, s, 8 * far:8 * far + 8, g, :], kv[:, half::2, far:far + N_CMP],
                                spread(posT[rows, s, 8 * far:8 * far + 8], N_CMP), ALU.add)
                ins.then_inc(S("cmp_in_ready"), 1)
            phase_end(dve, "dve")

            for c in range(2):
                chain(nc.vector.tensor_copy(q_dec[:, c, 0:SUB], bcum[:, c, 0:SUB]))
                nc.vector.tensor_tensor(q_dec[:, c, SUB:T].rearrange("p (u t) -> p u t", t=SUB),
                                        bcum[:, c, SUB:T].rearrange("p (u t) -> p u t", t=SUB),
                                        spread(bcum[:, c, SUB - 1:T - SUB:SUB], SUB), ALU.subtract).then_inc(
                    S("q_diff"), 1)
            for c in range(2):
                dve.wait_ge(S("q_exp"), c + 1)
                nc.vector.tensor_tensor(q_dec[:, c, :], q_dec[:, c, :], gqkT[:, c, :], ALU.mult).then_inc(
                    S("q_dec_ready"), 1)

            def k_diff(u):
                for c in range(2):
                    if u >= 2:
                        dve.wait_ge(S("k_dec_used"), 2 * (u - 2) + c + 1)
                    before = bcum[:, c, SUB * u - 1:SUB * u] if u else 0.0
                    nc.vector.tensor_scalar(k_dec[:, u % 2, c, :], bcum[:, c, :], before, 0.0, ALU.subtract,
                                            ALU.max).then_inc(S("k_diff"), 1)

            k_diff(0)
            for u in range(NSUB):
                if u + 1 < NSUB:
                    k_diff(u + 1)
                for c in range(2):
                    dve.wait_ge(S("k_exp"), 2 * u + c + 1)
                    nc.vector.tensor_tensor(k_dec[:, u % 2, c, :], k_dec[:, u % 2, c, :], gqkT[:, 2 + c, :],
                                            ALU.mult).then_inc(S("k_dec_ready"), 1)
            for c in range(2):
                if c:
                    dve.wait_ge(S("diag_used"), c)
                bt = bcum[:, c, :].rearrange("p (u t) -> p u t", t=SUB)
                kt_ = gqkT[:, 2 + c, :].rearrange("p (u t) -> p u t", t=SUB)
                flat = diag[:, :, :, :].rearrange("p u t j -> p (u t) j")

                def by_key(v):
                    return v.unsqueeze(2).to_broadcast([P, NSUB, SUB, SUB])

                chain(nc.vector.tensor_copy(diag[:, :, :, :], by_key(bt)))
                chain(nc.vector.tensor_tensor(flat, spread(bcum[:, c, :], SUB), flat, ALU.subtract))
                nc.vector.tensor_scalar(flat, flat, 0.0, None, ALU.min).then_inc(S("diag_diff"), 1)
                dve.wait_ge(S("diag_exp"), c + 1)
                chain(nc.vector.tensor_tensor(flat, flat, spread(gqkT[:, c, :], SUB), ALU.mult))
                nc.vector.tensor_tensor(diag[:, :, :, :], diag[:, :, :, :], by_key(kt_), ALU.mult).then_inc(
                    S("diag_ready"), 1)
            dve.wait_ge(S("diag_used"), 2)
            dve.wait_ge(S("k_dec_used"), 2 * NSUB)
            for hh in range(GLA_HEADS):
                far, near = bank[hh], bank[4 + hh]
                tmp = k_dec[:, 0, 0, 0:P]
                nc.vector.tensor_copy(gla_a[:, hh, 0, P:T], far[:, P:T])
                for t in range(TT):
                    a = gla_a[:, hh, t, P * t:P * t + P]
                    chain(nc.vector.tensor_tensor(a, far[:, T * t + P * t:T * t + P * t + P], mask_prev[:, :], ALU.mult))
                    chain(nc.vector.tensor_tensor(tmp, near[:, P * t:P * t + P], mask_same[:, :], ALU.mult))
                    chain(nc.vector.tensor_tensor(a, a, tmp, ALU.add))
            dve.sem_inc(S("gla_a_ready"), 1)
            dve.wait_ge(S("o_gla_ready"), TT)
            og = o_gla[:, :, :].rearrange("p t (a d) -> p (t a) d", d=P)
            sq = scratch(0, TT * GLA_HEADS, P)
            chain(nc.vector.tensor_tensor(sq, og, og, ALU.mult))
            nc.vector.tensor_reduce(gla_stat[:, 0, :], sq, X, ALU.add).then_inc(S("gla_squares"), 1)
            dve.wait_ge(S("gla_rms"), 1)
            chain(nc.vector.reciprocal(gla_stat[:, 2, :], gla_stat[:, 1, :]))
            chain(nc.vector.tensor_tensor(og, og, spread(gla_stat[:, 2, :], P), ALU.mult))
            nc.vector.tensor_tensor(o_gla[:, :, :], o_gla[:, :, :], gr[:, :, :], ALU.mult).then_inc(S("gla_normed"), 1)
            dve.wait_ge(S("gla_turned"), 1)
            for hh in range(GLA_HEADS):
                nc.vector.tensor_scalar(catT[:, hh, :], bank[2 + hh // 2][:, T * (hh % 2):T * (hh % 2) + T],
                                        col("gla_out_norm_2", 0), None, ALU.mult)
            phase_end(dve, "dve")
            attention_dve(dve, NSA, units_nsa())
            phase_end(dve, "dve")
            residual_dve(dve, "wout")
            phase_end(dve, "dve")
            dve.wait_ge(S("mem_in"), 16)
            norm_dve(dve, chain, "mem", mem_tok, "norm_mem_2")
            phase_end(dve, "dve")
            norm_dve(dve, chain, "xa", h, "norm_xattn_2")
            phase_end(dve, "dve")
            attention_dve(dve, CROSS, units_cross())
            phase_end(dve, "dve")
            residual_dve(dve, "xo")
            phase_end(dve, "dve")
            norm_dve(dve, chain, "peer", h, "norm_ffn_2")
            phase_end(dve, "dve")
            phase_end(dve, "dve")

            for t in range(TT):
                for hp in range(16):
                    s1, s2 = sc[:, t, hp, :], sc2[:, t, hp, :]
                    v1, v2 = tv[:, t, hp, 0:8], tv[:, t, hp, 8:16]
                    chain(nc.vector.max(v1, s1))
                    nc.vector.max_index(ti[:, t, hp, 0:8], v1, s1)
                    chain(nc.vector.match_replace(s2, v1, s1, -3.0e38))
                    chain(nc.vector.max(v2, s2))
                    chain(nc.vector.max_index(ti[:, t, hp, 8:16], v2, s2))
            chain(nc.vector.tensor_copy(tif[:, :, :, :], ti))
            for t in range(TT):
                for hh in range(PH):
                    chain(nc.vector.tensor_tensor(
                        cand[:, t, hh, :, :], spread(tv[:, t, 2 * hh, :], TOPK),
                        tv[:, t, 2 * hh + 1, :].unsqueeze(1).to_broadcast([P, TOPK, TOPK]), ALU.add))
                    c1, c2 = cand[:, t, hh, :, :].rearrange("p a b -> p (a b)"), cand2[:, t, hh, :]
                    v1, v2 = cv[:, t, hh, 0:8], cv[:, t, hh, 8:16]
                    chain(nc.vector.max(v1, c1))
                    nc.vector.max_index(ci[:, t, hh, 0:8], v1, c1)
                    chain(nc.vector.match_replace(c2, v1, c1, -3.0e38))
                    chain(nc.vector.max(v2, c2))
                    chain(nc.vector.max_index(ci[:, t, hh, 8:16], v2, c2))
            chain(nc.vector.tensor_copy(psum16[:, 1, :], cv[:, :, :, 0].rearrange("p t a -> p (t a)")))
            cvf = cv[:, :, :, :].rearrange("p t a k -> p (t a) k")
            nc.vector.tensor_tensor(cvf, cvf, spread(psum16[:, 1, :], TOPK), ALU.subtract).then_inc(S("gate_shifted"), 1)
            cif = ci.rearrange("p t a k -> p t (a k)")
            chain(nc.vector.tensor_scalar(cab[:, 0, :, :], cif, 4, None, ALU.logical_shift_right))
            chain(nc.vector.tensor_scalar(cab[:, 1, :, :], cif, TOPK - 1, None, ALU.bitwise_and))
            chain(nc.vector.tensor_copy(cabf[:, :, :, :], cab))
            for t in range(TT):
                for a in range(2):
                    chain(nc.vector.tensor_tensor(eq, spread(cabf[:, a, t, :], TOPK),
                                                  iota16.unsqueeze(1).to_broadcast([P, PH * TOPK, TOPK]), ALU.is_equal))
                    for hh in range(PH):
                        e = eq[:, TOPK * hh:TOPK * hh + TOPK, :]
                        ins = nc.vector.tensor_tensor(
                            e, e, tif[:, t, 2 * hh + a, :].unsqueeze(1).to_broadcast([P, TOPK, TOPK]), ALU.mult)
                    chain(ins)
                    chain(nc.vector.tensor_reduce(fin3[:, a, t, :], eq, X, ALU.add))
            dve.wait_ge(S("gate_exp"), 1)
            chain(nc.vector.tensor_reduce(psum16[:, 0, :], cvf, X, ALU.add))
            chain(nc.vector.reciprocal(psum16[:, 1, :], psum16[:, 0, :]))
            nc.vector.tensor_tensor(fin3[:, 2, :, :].rearrange("p t (a k) -> p (t a) k", k=TOPK), cvf,
                                    spread(psum16[:, 1, :], TOPK), ALU.mult).then_inc(S("peer_top"), 1)
            dve.sem_inc(S("gate_read"), 4)
            dve.sem_inc(S("hot_used0"), 1)
            dve.sem_inc(S("hot_used1"), 1)
            phase_end(dve, "dve")
            with dve.Fori(0, T // 16) as i:
                for q in range(4):
                    for pair in range(2):
                        dve.wait_ge(S(f"hot_used{pair}"), i * 4 + (q + 1))
                        for x in range(2):
                            tok = bass.ds(i * 16 + (4 * q + 2 * pair + x), 1)
                            nc.vector.tensor_scalar(hot[:, pair, x, 0, :], iota[:, :], idxT[:, 0, tok], None, ALU.is_equal)
                            ins = nc.vector.tensor_scalar(hot[:, pair, x, 1, :], iota[:, :], idxT[:, 1, tok],
                                                          idxT[:, 2, tok], ALU.is_equal, ALU.mult)
                        ins.then_inc(S("hot_ready"), 1)
            phase_end(dve, "dve")

            def copy_b(t, r, early):
                dve.wait_ge(S("down_turned"), t + 1)
                if not early:
                    dve.wait_ge(S("expert_scored"), t - 1)
                nc.vector.tensor_copy(downT[:, r % 2, 4:8, :].rearrange("p k e -> p (k e)"), bank[5][:, :]).then_inc(
                    S("copied_b"), 1)

            def gated(t, r, column, early):
                dve.wait_ge(S("expert_gelu"), t + 1)
                if not early:
                    dve.wait_ge(S("up_used"), t - 1)
                nc.vector.tensor_tensor(ea[:, r % 2, :], eh[:, r % 2, :], column, ALU.mult).then_inc(
                    S("expert_gated"), 1)

            copy_b(0, 0, True)
            for t in range(PR):
                copy_b(t + 1, t + 1, t + 1 < 2)
                gated(t, t, gtab[:, t, :], t < 2)
            with dve.Fori(1, NKEYS // PR - 1) as i:
                for r in range(PR):
                    copy_b(i * PR + (r + 1), r + 1, False)
                    gated(i * PR + r, r, gtab[:, bass.ds(i * PR + r, 1), :].rearrange("p a t -> p (a t)"), False)
            for t in range(NKEYS - PR, NKEYS):
                if t + 1 < NKEYS:
                    copy_b(t + 1, t + 1, False)
                gated(t, t, gtab[:, t, :], False)
            phase_end(dve, "dve")
            for c in range(4):
                hs = h[:, c // 2, 512 * (c % 2):512 * (c % 2) + 512]
                nc.vector.tensor_tensor(hs, hs, bank[c][:, :], ALU.add).then_inc(S("h_final"), 1)
            dve.wait_ge(S("norm_rms"), len(NORMS))
            dve.wait_ge(S("h_final"), 4)
            dve.wait_ge(S("gfin_in"), 16)
            chain(nc.vector.reciprocal(stat[:, 2, :], stat[:, 1, :]))
            for t in range(TT):
                nc.vector.scalar_tensor_tensor(out=h[:, t, :], in0=h[:, t, :], scalar=stat[:, 2, t:t + 1],
                                               in1=gfin, op0=ALU.mult, op1=ALU.mult).then_inc(S("fin_out"), 1)

        @block.gpsimd
        def _(pool):
            chain = Chain(pool, S("pool_chain"))
            nc.gpsimd.memset(eps[:, :], EPS)
            nc.gpsimd.memset(sel_dup[:, :, :], 0.0)
            nc.gpsimd.memset(modmask[:, :], 0.0)
            nc.gpsimd.memset(ident[:, :], 0.0)
            nc.gpsimd.memset(mirror[:, :], 0.0)
            chain(nc.gpsimd.memset(ones[:, :], 1.0))
            nc.gpsimd.iota(iota[:, :], pattern=[[1, P]], base=0, channel_multiplier=0,
                           allow_small_or_imprecise_dtypes=True)
            nc.gpsimd.affine_select(out=ident[:, :], in_=ident[:, :], compare_op=ALU.not_equal, fill=1.0, base=0,
                                    pattern=[[-1, P]], channel_multiplier=1)
            nc.gpsimd.affine_select(out=mirror[:, :], in_=mirror[:, :], compare_op=ALU.not_equal, fill=1.0, base=1 - P,
                                    pattern=[[1, P]], channel_multiplier=1)
            nc.gpsimd.memset(modmask[:, SUB - 1::SUB], 1.0)
            for g in range(2):
                d = sel_dup[:, g, :].rearrange("p (a b) -> p a b", a=2)
                nc.gpsimd.affine_select(out=d, in_=d, compare_op=ALU.not_equal, fill=1.0, base=-DH * g,
                                        pattern=[[0, 2], [-1, DH]], channel_multiplier=1)
            nc.gpsimd.affine_select(out=mask_prev[:, :].rearrange("p (u t) -> p u t", t=SUB),
                                    in_=ones[:, :].rearrange("p (u t) -> p u t", t=SUB), compare_op=ALU.is_gt, fill=0.0,
                                    base=0, pattern=[[SUB, P // SUB], [0, SUB]], channel_multiplier=-1)
            chain(nc.gpsimd.affine_select(out=mask_same[:, :], in_=ones[:, :], compare_op=ALU.is_ge, fill=0.0, base=0,
                                          pattern=[[1, P]], channel_multiplier=-1))
            nc.gpsimd.tensor_tensor(mask_same[:, :], mask_same[:, :], mask_prev[:, :], ALU.subtract)
            chain(nc.gpsimd.affine_select(out=late_row[:, :], in_=ones[:, 0:1], compare_op=ALU.is_ge, fill=0.0,
                                          base=-(CMP_BLOCK - 1), pattern=[[0, 1]], channel_multiplier=1))
            nc.gpsimd.memset(bias1[0:64, :, 0:64], NEG)
            pool.drain().then_inc(S("consts"), 1)

        @block.sync
        def _(sp):
            def load(n, pieces):
                if n >= RING:
                    m = n - RING
                    if m in spent_at:
                        sp.wait_ge(S("tile_done"), spent_at[m])
                    else:
                        e, kind = (m - MOE_AT) // 3, (m - MOE_AT) % 3
                        sp.wait_ge(S("moe_out" if kind == 2 else "moe_products"), 4 * (e + 1))
                for at, src in pieces:
                    kt, width = src.shape[1], src.shape[2]
                    dst = slot[n % RING][:, at:at + kt * width].rearrange("p (k n) -> p k n", n=width)
                    sp.dma_start(dst, src).then_inc(landed[n % RING], 16)

            for n, pieces in enumerate(first):
                load(n, pieces)
            tabs = [w["w1"][0].rearrange("e (k p) n -> e p k n", p=P), w["w3"][0].rearrange("e (k p) n -> e p k n", p=P),
                    w["w2"][0].rearrange("e (k p) n -> e p k n", p=P)]
            for j in range(6):
                load(MOE_AT + j, [(0, tabs[j % 3][j // 3])])
            with sp.Fori(1, EXPERTS // 2) as i:
                for j in range(6):
                    sp.wait_ge(S("moe_out" if j % 3 == 2 else "moe_products"), i * 8 + (4 * (j // 3) - 4))
                    src = tabs[j % 3][bass.ds(i * 2 + j // 3, 1)].rearrange("e p k n -> p (e k) n")
                    dst = slot[(MOE_AT + j) % RING].rearrange("p (k n) -> p k n", n=src.shape[2])
                    sp.dma_start(dst, src).then_inc(landed[(MOE_AT + j) % RING], 16)
            for m, pieces in enumerate(later):
                load(LATE_AT + m, pieces)
            sp.wait_ge(S("phase"), 3 * phases["rings free"])
            dn = w["peer_down_2"][0].rearrange("(i p) d -> i p d", p=P)
            upt = w["peer_up_2"][0].rearrange("(i p) d -> i p d", p=P)
            for r in range(PR):
                sp.dma_start(down[r], dn[r]).then_inc(S(f"down_landed_{r}"), 16)
                sp.dma_start(up[r], upt[r]).then_inc(S(f"up_landed_{r}"), 16)
            with sp.Fori(1, NKEYS // PR) as i:
                for r in range(PR):
                    e = bass.ds(i * PR + r, 1)
                    sp.wait_ge(S("down_turned"), i * PR + (r - PR + 1))
                    sp.dma_start(down[r], dn[e].rearrange("a p d -> p (a d)")).then_inc(S(f"down_landed_{r}"), 16)
                    sp.wait_ge(S("up_used"), i * PR + (r - PR + 1))
                    sp.dma_start(up[r], upt[e].rearrange("a p d -> p (a d)")).then_inc(S(f"up_landed_{r}"), 16)

        assert phases["pe"] == phases["act"] == phases["dve"], phases


_INS = ['x', 'p', 'g_mix', 'w_in', 'b_in', 'g_q', 'g_k', 'rel_bias', 'conv_w', 'conv_b', 'w_pa', 'w_pc', 'w_o',
        'g_ffn', 'w_group', 'b_group', 'w_router', 'b_router', 'w1', 'w3', 'w2', 'g_ple', 'w_ple_gate',
        'b_ple_gate', 'w_ple_proj', 'mem_2', 'rel_bias_2', 'norm_mix_2', 'w_in_2', 'gla_gate_w2_2',
        'gla_gate_b_2', 'gla_out_norm_2', 'cmp_pos_k_2', 'cmp_pos_v_2', 'cmp_k_w1_2', 'cmp_k_w2_2',
        'cmp_v_w1_2', 'cmp_v_w2_2', 'w_out_2', 'norm_xattn_2', 'norm_mem_2', 'xa_wq_2', 'xa_wk_2',
        'xa_wv_2', 'xa_wo_2', 'norm_ffn_2', 'peer_wq_2', 'peer_subkeys_2', 'peer_down_2', 'peer_up_2',
        'norm_final_2']


def kernel(**inputs):
    import concourse.bacc as _bacc
    from concourse.bass_utils import run_bass_kernel_spmd as _run

    nc = _bacc.Bacc("TRN2", target_bir_lowering=False, num_devices=1)
    arrays, args = {}, {}
    for name in _INS:
        a = np.ascontiguousarray(inputs[name])
        arrays[f"in_{name}_dram"] = a
        args[name] = nc.dram_tensor(f"in_{name}_dram", a.shape, mybir.dt.from_np(a.dtype), kind="ExternalInput").ap()
    buckets = nc.inline_tensor(distance_buckets(), "distance_buckets").ap()
    out = nc.dram_tensor("out_0_dram", (1, T, D), F32, kind="ExternalOutput").ap()
    build(nc, args, buckets, out)
    r = _run(nc, [arrays], core_ids=[0])
    return r.results[0]["out_0_dram"]
```

```python
from contextlib import ExitStack

import numpy as np
import concourse.bass as bass
from concourse import mybir

F32 = mybir.dt.float32
F32R = mybir.dt.float32r
U32 = mybir.dt.uint32
ALU = mybir.AluOpType
ACT = mybir.ActivationFunctionType
X = mybir.AxisListType.X

P = 128
T = 256
TT = T // P
D = 1024
KT = D // P
NEG = -1e30
EPS = 1e-6
HEADS = 8
DH = 64
REL = 320
EXPERTS = 32
GROUPS = 4
PER_GROUP = EXPERTS // GROUPS
FF = 512
FT = FF // P
BUCKETS = 32
TAB = 512
N_CMP = 15
CMP_STRIDE = 16
CMP_BLOCK = 32
SUB = 16
NSUB = T // SUB
GLA_HEADS = 4
XHEADS = 4
PH = 8
GROUPS = 8
TOPK = 16
NKEYS = 128

RING = 6
SLOT = KT * 512

ROWS = [("g_mix", 8), ("b_in", 40), ("conv_w", 12), ("conv_b", 4), ("g_ffn", 8), ("g_ple", 8),
        ("norm_mix_2", 8), ("gla_gate_b_2", 2), ("norm_xattn_2", 8), ("norm_mem_2", 8),
        ("norm_ffn_2", 8), ("gla_out_norm_2", 1)]
COL = {}
NVEC = 0
for _name, _rows in ROWS:
    COL[_name] = NVEC
    NVEC += _rows
COL["g_q"], COL["g_k"] = NVEC, NVEC + 1
NVEC += 2
assert NVEC <= P


def distance_buckets():
    n = np.arange(T)
    far = 16 + np.floor(np.log(np.maximum(n, 1) / 16.0) / np.log(128.0) * 16).astype(np.int64)
    bucket = np.where(n < 16, n, np.minimum(far, BUCKETS - 1))
    return (np.arange(BUCKETS)[:, None] == bucket[None, :]).astype(np.float32)


NVROWS = len(ROWS) + 4
NLATE = 6


class Chain:

    def __init__(self, eng, sem):
        self.eng, self.sem, self.n = eng, sem, 0

    def __call__(self, ins):
        ins.then_inc(self.sem, 1)
        self.n += 1
        self.eng.wait_ge(self.sem, self.n)


def weight_slots(w):
    def cols(name, a, b):
        return w[name][0].rearrange("(k p) n -> p k n", p=P)[:, :, a:b]

    def pairs(name):
        return [[(0, cols(name, 512 * j, 512 * j + 512))] for j in range(2)]

    first = [[(0, cols("w_in", 512 * j, 512 * j + 512))] for j in range(10)]
    first += [[(0, cols("w_pa", 512 * j, 512 * j + 512)), (SLOT // 2, cols("w_pc", 512 * j, 512 * j + 512))]
              for j in range(2)]
    first += pairs("w_o")
    later = pairs("w_ple_gate") + [[(0, cols("w_ple_proj", 0, D))]]
    later += [[(0, cols("w_in_2", a, b))] for a, b in
              ((0, 512), (512, 1024), (1024, 1536), (1552, 2064), (2064, 2448), (2448, 2856))]
    for name in ("w_out_2", "xa_wk_2", "xa_wv_2", "xa_wq_2", "xa_wo_2", "peer_wq_2"):
        later += pairs(name)
    return first, later


def build(nc, w, buckets, out):
    with ExitStack() as ctx:
        def sb(name, shape, dt=F32):
            return ctx.enter_context(nc.sbuf_tensor(name, shape, dt))

        sems = {}

        def S(name):
            if name not in sems:
                sems[name] = ctx.enter_context(nc.semaphore(name))
            return sems[name]

        bank = [ctx.enter_context(nc.psum_tensor(f"bank{i}", [P, 512], F32)) for i in range(8)]
        table_dram = nc.dram_tensor("distance_table", [HEADS, TAB], F32, kind="Internal")

        ident = sb("ident", [P, P])
        mirror = sb("mirror", [P, P])
        ones = sb("ones", [P, P])
        iota = sb("iota", [P, P])
        vecs = sb("vecs", [P, P])
        eps = sb("eps", [P, 1])
        late_row = sb("late_row", [P, 1])
        h = sb("h", [P, TT, D])
        nT = sb("nT", [P, KT, T])
        nT_at = nc.sbuf_base - 4 * KT * T
        stat = sb("stat", [P, 3, TT])
        unit = sb("unit", [P, 3, 2])
        small = sb("small", [P, 3 * 512])
        brow = small[0:1, :]
        qk_stat = sb("qk_stat", [P, 3, 2 * TT * HEADS])
        br36 = sb("br36", [1, 36])
        logit = sb("logit", [P, TT, 40])
        route = sb("route", [P, TT, 80])
        top8 = sb("top8", [P, TT, 16])
        idx8 = sb("idx8", [P, TT, 16], U32)
        idx8f = sb("idx8f", [P, TT, 16])
        earlier = sb("earlier", [P, P])
        fullest = sb("fullest", [P, 1])
        overfull = sb("overfull", [P, 1], mybir.dt.int32)
        gatew = sb("gatew", [P, TT, EXPERTS])
        sel_dup = sb("sel_dup", [P, 2, P])
        modmask = sb("modmask", [P, P + SUB])
        mask_prev = sb("mask_prev", [P, P])
        mask_same = sb("mask_same", [P, P])
        w_glr = sb("w_glr", [P, KT, 16])
        glrT = sb("glrT", [16, T])
        gate_w2 = sb("gate_w2", [16, 256])
        cmp_w2 = sb("cmp_w2", [P, 2, DH])
        pos_rows = sb("pos_rows", [SUB, 2, P])
        posT = sb("posT", [P, 2, SUB])
        cmp_h = sb("cmp_h", [P, 2, 2 * N_CMP])
        k_cmpT = sb("k_cmpT", [P, 2 * N_CMP])
        v_cmp = sb("v_cmp", [N_CMP, 2, DH])
        nsa_gate = sb("nsa_gate", [P, TT, 3 * HEADS])
        gla_stat = sb("gla_stat", [P, 3, TT * GLA_HEADS])
        rel2 = sb("rel2", [BUCKETS, HEADS])
        SCR = SLOT * RING
        ARENA = SCR + 19456
        arena = sb("arena", [P, ARENA])
        arena_at = nc.sbuf_base - 4 * ARENA
        slot = [arena[:, SLOT * r:SLOT * (r + 1)] for r in range(RING)]

        def piece(at, *shape):
            n = int(np.prod(shape))
            assert at + n <= ARENA, (at, shape)
            v = arena[:, at:at + n]
            if len(shape) == 2:
                v = v.rearrange("p (a b) -> p a b", b=shape[1])
            if len(shape) == 3:
                v = v.rearrange("p (a b c) -> p a b c", b=shape[1], c=shape[2])
            if len(shape) == 4:
                v = v.rearrange("p (a b c d) -> p a b c d", b=shape[1], c=shape[2], d=shape[3])
            return v

        def scratch(at, *shape):
            return piece(SCR + at, *shape)

        xn = scratch(0, TT, D)
        att_p = scratch(2048, 2, T)
        att_pt = scratch(2560, 2, 2, P)
        vrows = scratch(2048, P)
        B0 = 3072
        z_tok = scratch(B0, 3, TT, 512)
        sq_tok = scratch(B0 + 3072, 2, TT, 512)
        qT = scratch(B0 + 5120, 4, T)
        kT = scratch(B0 + 6144, 4, T)
        convT = scratch(B0 + 7168, 12, T)
        sigT = scratch(B0 + 10240, 16, T)
        bias1 = scratch(B0 + 14336, HEADS, T)
        mixT = scratch(B0 + 3072, 8, T)
        cin = scratch(B0, 4, T + 2)
        mT = scratch(B0 + 5120, KT, T)
        wgr = scratch(B0, KT, 36)
        silu_h = scratch(B0 + 512, FT, T)
        hidT = scratch(B0 + 2048, FT, T)
        M0 = B0 + 4096
        gain_row = scratch(M0, D)
        picked = scratch(M0 + 1024, TT, EXPERTS)
        place = scratch(M0 + 1088, TT, EXPERTS + 2)
        pick = scratch(M0 + 1160, 2, TT, P)
        pickT = scratch(M0 + 1672, TT, P)
        gathT = scratch(M0 + 1928, KT, P)
        silu_r = scratch(M0 + 2952, FF)
        hid_r = scratch(M0 + 3464, FF)
        hid_rT = scratch(M0 + 3976, FT, P)
        row_w = scratch(M0 + 4488, 1)
        out_r = scratch(M0 + 4496, D)
        p_tok = scratch(B0, TT, 256)
        pT = scratch(B0 + 512, 2, T)
        gate_t = scratch(B0 + 1024, TT, D)
        gqkT = scratch(B0, 4, T)
        gv = scratch(B0 + 1024, TT, 512)
        gr = scratch(B0 + 2048, TT, 512)
        loga = scratch(B0 + 3072, 2, T)
        bcum = scratch(B0 + 3584, 2, T)
        nqT = scratch(B0 + 4096, 4, T)
        kvT = scratch(B0 + 5120, 4, T)
        v_sw = scratch(B0 + 6144, 2, TT, P)
        dupT = scratch(B0 + 6656, 4, T)
        catT = scratch(B0 + 7680, KT, T)
        q_dec = scratch(B0 + 9728, 2, T)
        gla_a = scratch(B0 + 10240, GLA_HEADS, 2, T)
        diag = scratch(B0 + 12288, NSUB, SUB, SUB)
        k_dec = scratch(0, 2, 2, T)
        o_gla = scratch(1024, TT, 512)
        cmp_w1 = scratch(B0 + 10240, 2, SUB, P)
        cmp_in = scratch(B0 + 14336, 2, SUB, 2, N_CMP)
        bias_sw = scratch(B0 + 10240, HEADS, T)
        bias_c = scratch(B0 + 12288, HEADS, T)
        dist_oh = scratch(B0 + 9728, T)
        dist_row = scratch(B0 + 10240, TAB)
        mem_tok = scratch(B0, TT, D)
        xkT = scratch(B0 + 2048, KT, T)
        xv = scratch(B0 + 4096, TT, D)
        xqT = scratch(B0 + 6144, KT, T)
        xoT = scratch(B0 + 8192, KT, T)
        TABLE = NKEYS * T
        gtab = piece(0, NKEYS, T)
        PR = 4
        def part(name, at, *shape):
            return nc.alloc_sbuf_tensor_at(name, [P, *shape], F32R, offset=at)

        down = [piece(TABLE + D * r, D) for r in range(PR)]
        DT = TABLE + PR * D
        downT_hi = part("downT_hi", arena_at + 4 * DT, 2, KT, P)
        downT_lo = part("downT_lo", arena_at + 4 * (DT + 2048), 2, KT, P)
        x_hi = part("x_hi", arena_at + 4 * (DT + 4096), KT, T)
        x_lo = part("x_lo", nT_at, KT, T)
        idxT = piece(DT + 6144, 3, T)
        hot = piece(TABLE, 2, 2, 2, P)
        gates = piece(TABLE + 1024, 4, 4 * P)
        e_hi = part("e_hi", arena_at + 4 * (TABLE + 1024), 2, T)
        e_lo = part("e_lo", arena_at + 4 * (TABLE + 1536), 2, T)
        u_hi = part("u_hi", arena_at + 4 * (TABLE + 2048), 2, D)
        u_lo = part("u_lo", arena_at + 4 * (TABLE + 4096), 2, D)
        up = [piece(TABLE + 6144 + D * r, D) for r in range(PR)]
        Q0 = SCR + B0
        pqT = piece(Q0, PH, T)
        sk_rows = piece(Q0 + 2048, 16, DH)
        skT = piece(Q0 + 3072, PH, P)
        TOP = TABLE // 2
        sc = piece(TOP, 16, NKEYS)
        tv = piece(TOP + 2048, TT, 16, TOPK)
        tif = piece(TOP + 2560, TT, 16, TOPK)
        ti = piece(TOP + 3072, TT, 16, TOPK).bitcast(U32)
        cand = piece(TOP + 3584, TT, PH, TOPK, TOPK)
        ci = piece(TOP + 7680, TT, PH, TOPK).bitcast(U32)
        cab = piece(TOP + 7936, 2, TT, PH * TOPK).bitcast(U32)
        cabf = piece(TOP + 8448, 2, TT, PH * TOPK)
        eq = piece(TOP + 8960, 2, 2, TOPK, TOPK)
        fin3 = small[:, 0:768].rearrange("p (c t a) -> p c t a", c=3, t=TT)
        cv = small[:, 768:1024].rearrange("p (t a k) -> p t a k", t=TT, a=PH)
        psum16 = small[:, 1024:1056].rearrange("p (c a) -> p c a", c=2)
        gfin = scratch(B0, D)
        iota16 = iota[:, 0:TOPK]

        first, later = weight_slots(w)
        NF = len(first)
        MOE_AT, LATE_AT = NF, NF + 3 * EXPERTS
        landed = [S(f"slot_landed_{r}") for r in range(RING)]
        split_slots = [n for n, pieces in enumerate(first) if len(pieces) > 1]

        def slot_ready(eng, n, i=0):
            extra = sum(1 for m in split_slots if m % RING == n % RING and m <= n)
            eng.wait_ge(landed[n % RING], i * 16 + 16 * (n // RING + 1 + extra))

        def slot_view(n, kt, width):
            return slot[n % RING][:, 0:kt * width].rearrange("p (k n) -> p k n", n=width)

        def col(name, k):
            c = COL[name] + k
            return vecs[:, c:c + 1]

        phases = {}

        def phase_end(eng, key):
            phases[key] = phases.get(key, 0) + 1
            eng.drain().then_inc(S("phase"), 1)
            eng.wait_ge(S("phase"), 3 * phases[key])

        def units_block1():
            for qt in range(TT):
                for head in range(HEADS):
                    r, nb = DH * (head % 2), qt + 1
                    q0 = P * qt
                    yield dict(
                        q=[qT[r:r + DH, head // 2, q0:q0 + P]], k=[kT[r:r + DH, head // 2, 0:P * nb]], n=P * nb,
                        bias=[bias1[:, head, q0 - P * b:q0 - P * b + P] for b in range(nb)],
                        v=[[z_tok[:, 2, b, DH * head:DH * head + DH] for b in range(nb)]],
                        gate=None, base=r, start=True, last=True,
                        dest=mixT[:, head // 2, q0:q0 + P] if head % 2 else None)

        def units_nsa():
            for qt in range(TT):
                q0 = P * qt
                for head in range(HEADS):
                    r, g, nb = DH * (head % 2), head // 4, qt + 1
                    q = [nqT[r:r + DH, head // 2, q0:q0 + P]]
                    yield dict(
                        q=q, k=[k_cmpT[r:r + DH, N_CMP * g:N_CMP * g + N_CMP]], n=N_CMP,
                        bias=[bias_c[0:N_CMP, head, q0:q0 + P]], v=[[v_cmp[:, g, :]]],
                        gate=nsa_gate[:, qt, 3 * head:3 * head + 1], base=r, start=True, last=False, dest=None)
                    for b3 in range(2):
                        yield dict(
                            q=q, k=[dupT[r:r + DH, 2 * b3 + g, 0:P * nb]], n=P * nb,
                            bias=[bias_sw[:, head, q0 - P * b:q0 - P * b + P] for b in range(nb)],
                            v=[[v_sw[:, b3, b, DH * g:DH * g + DH] for b in range(nb)]],
                            gate=nsa_gate[:, qt, 3 * head + 1 + b3:3 * head + 2 + b3], base=r,
                            start=False, last=b3 == 1,
                            dest=catT[:, 4 + head // 2, q0:q0 + P] if head % 2 and b3 == 1 else None)

        def units_cross():
            for qt in range(TT):
                q0 = P * qt
                for head in range(XHEADS):
                    yield dict(
                        q=[xqT[:, 2 * head + c, q0:q0 + P] for c in range(2)],
                        k=[xkT[:, 2 * head + c, :] for c in range(2)], n=T, bias=[],
                        v=[[xv[:, b, 256 * head + P * c:256 * head + P * c + P] for b in range(2)] for c in range(2)],
                        gate=None, base=0, start=True, last=True, dest=xoT[:, 2 * head:2 * head + 2, q0:q0 + P])

        n1, n2 = len(list(units_block1())), len(list(units_nsa()))
        ATT1, NSA, CROSS = (0, 0), (n1, HEADS), (n1 + n2, 2 * HEADS)

        def attention_pe(pe, at, units):
            units = list(units)
            u0, g0 = at
            group = 0

            def scores(u):
                a = units[u]
                if u >= 2:
                    pe.wait_ge(S("att_exp"), u0 + u - 1)
                s = bank[u % 2][:, 0:a["n"]]
                last = len(a["bias"]) == 0
                for c, (q, k) in enumerate(zip(a["q"], a["k"])):
                    mm = nc.tensor.matmul(s, lhsT=q, rhs=k, start=c == 0, stop=last and c == len(a["q"]) - 1)
                for b, bias in enumerate(a["bias"]):
                    n = min(P, a["n"])
                    mm = nc.tensor.matmul(bank[u % 2][:, P * b:P * b + n], lhsT=bias, rhs=mirror[0:n, P - n:P],
                                          start=False, stop=b == len(a["bias"]) - 1)
                mm.then_inc(S("att_scores"), 1)

            def turn(u):
                a = units[u]
                pe.wait_ge(S("att_probs"), u0 + u + 1)
                if u >= 2:
                    pe.wait_ge(S("att_turned"), u0 + u - 1)
                nb = (a["n"] + P - 1) // P
                n = min(P, a["n"])
                for b in range(nb):
                    mm = nc.tensor.transpose(bank[2 + u % 2][0:n, P * b:P * b + P],
                                             att_p[:, u % 2, P * b:P * b + n], ident[:, :])
                mm.then_inc(S("att_turns"), 1)

            def values(u):
                nonlocal group
                a = units[u]
                pe.wait_ge(S("att_turned"), u0 + u + 1)
                if group >= 2 and a["start"]:
                    pe.wait_ge(S("att_out"), g0 + group - 1)
                n = min(P, a["n"])
                for c, blocks in enumerate(a["v"]):
                    for b, v in enumerate(blocks):
                        o = bank[4 + group % 2][a["base"]:a["base"] + v.shape[1], P * c:P * c + P]
                        mm = nc.tensor.matmul(o, lhsT=v, rhs=att_pt[0:n, u % 2, b, :],
                                              start=a["start"] and b == 0, stop=a["last"] and b == len(blocks) - 1)
                mm.then_inc(S("att_values"), 1)
                if a["dest"] is not None:
                    group += 1

            for u in range(len(units) + 2):
                if u < len(units):
                    scores(u)
                if 0 <= u - 1 < len(units):
                    turn(u - 1)
                if u >= 2:
                    values(u - 2)

        def attention_dve(dve, at, units):
            units = list(units)
            u0, g0 = at

            def peak(u):
                dve.wait_ge(S("att_scores"), u0 + u + 1)
                if u >= 2:
                    dve.wait_ge(S("att_exp"), u0 + u - 1)
                nc.vector.tensor_reduce(unit[:, 0, u % 2:u % 2 + 1], bank[u % 2][:, 0:units[u]["n"]], X, ALU.max,
                                        negate=True).then_inc(S("att_max"), 1)

            def norm(u):
                a = units[u]
                n = a["n"]
                dve.wait_ge(S("att_exp"), u0 + u + 1)
                nc.vector.reciprocal(unit[:, 2, u % 2:u % 2 + 1], unit[:, 1, u % 2:u % 2 + 1]).then_inc(
                    S("att_inv"), 1)
                dve.wait_ge(S("att_inv"), u0 + u + 1)
                if a["gate"] is None:
                    ins = nc.vector.tensor_scalar(att_p[:, u % 2, 0:n], att_p[:, u % 2, 0:n],
                                                  unit[:, 2, u % 2:u % 2 + 1], None, ALU.mult)
                else:
                    ins = nc.vector.tensor_scalar(att_p[:, u % 2, 0:n], att_p[:, u % 2, 0:n],
                                                  unit[:, 2, u % 2:u % 2 + 1], a["gate"], ALU.mult, ALU.mult)
                ins.then_inc(S("att_probs"), 1)

            for u in range(len(units) + 1):
                if u < len(units):
                    peak(u)
                if u >= 1:
                    norm(u - 1)

        def attention_act(act, at, units):
            units = list(units)
            u0, g0 = at
            group = 0

            def exps(u):
                n = units[u]["n"]
                act.wait_ge(S("att_max"), u0 + u + 1)
                if u >= 2:
                    act.wait_ge(S("att_turns"), u0 + u - 1)
                nc.scalar.activation(att_p[:, u % 2, 0:n], bank[u % 2][:, 0:n], ACT.Exp,
                                     bias=unit[:, 0, u % 2:u % 2 + 1],
                                     accum_out=unit[:, 1, u % 2:u % 2 + 1]).then_inc(S("att_exp"), 1)

            def copy(u):
                nb, n = (units[u]["n"] + P - 1) // P, min(P, units[u]["n"])
                act.wait_ge(S("att_turns"), u0 + u + 1)
                if u >= 2:
                    act.wait_ge(S("att_values"), u0 + u - 1)
                nc.scalar.copy(att_pt[0:n, u % 2, 0:nb, :].rearrange("p b q -> p (b q)"),
                               bank[2 + u % 2][0:n, 0:P * nb]).then_inc(S("att_turned"), 1)

            def outs(u):
                nonlocal group
                dest = units[u]["dest"]
                if dest is None:
                    return
                act.wait_ge(S("att_values"), u0 + u + 1)
                src = bank[4 + group % 2]
                if len(units[u]["v"]) == 2:
                    src = src[:, 0:2 * P].rearrange("p (c q) -> p c q", c=2)
                else:
                    src = src[:, 0:P]
                nc.scalar.copy(dest, src).then_inc(S("att_out"), 1)
                group += 1

            for u in range(len(units) + 2):
                if u < len(units):
                    exps(u)
                if 0 <= u - 1 < len(units):
                    copy(u - 1)
                if u >= 2:
                    outs(u - 2)

        NORMS = ["mix", "ffn", "ple", "mix2", "mem", "xa", "peer", "fin"]

        def wait_nT(eng, tag, k):
            eng.wait_ge(S("norm_nT"), KT * NORMS.index(tag) + k)

        def norm_act(act, chain, tag, src):
            for t in range(TT):
                chain(nc.scalar.activation(xn[:, t, :], src[:, t, :], ACT.Square, accum_out=stat[:, 0, t:t + 1]))
            nc.scalar.activation(stat[:, 1, :], stat[:, 0, :], ACT.Sqrt, bias=eps[:, 0:1],
                                 scale=1.0 / D).then_inc(S("norm_rms"), 1)

        def norm_dve(dve, chain, tag, src, gain):
            dve.wait_ge(S("norm_rms"), NORMS.index(tag) + 1)
            chain(nc.vector.reciprocal(stat[:, 2, :], stat[:, 1, :]))
            for t in range(TT):
                nc.vector.tensor_scalar(xn[:, t, :], src[:, t, :], stat[:, 2, t:t + 1], None,
                                        ALU.mult).then_inc(S("norm_xn"), 1)
            for k in range(KT):
                if k % 2 == 0:
                    dve.wait_ge(S("norm_turned"), 4 * NORMS.index(tag) + k // 2 + 1)
                nc.vector.tensor_scalar(nT[:, k, :], bank[k // 2][:, T * (k % 2):T * (k % 2) + T], col(gain, k),
                                        None, ALU.mult).then_inc(S("norm_nT"), 1)

        def norm_pe(pe, tag):
            pe.wait_ge(S("norm_xn"), TT * (NORMS.index(tag) + 1))
            for k in range(KT):
                for t in range(TT):
                    at = T * (k % 2) + P * t
                    mm = nc.tensor.transpose(bank[k // 2][:, at:at + P], xn[:, t, P * k:P * k + P], ident[:, :])
                if k % 2:
                    mm.then_inc(S("norm_turned"), 1)

        tile_no = {}
        spent_at = {}

        def tile_bank(pe, tag):
            n = tile_no[tag] = len(tile_no)
            if n >= 4:
                pe.wait_ge(S("tile_read"), n - 3)
            return bank[4 + n % 4]

        def project_T(pe, tag, wv, kt, c0, cols, src):
            b = tile_bank(pe, tag)
            for k in range(kt):
                mm = nc.tensor.matmul(b[0:cols, 0:T], lhsT=wv[:, k, c0:c0 + cols], rhs=src[:, k, :],
                                      start=k == 0, stop=k == kt - 1)
            mm.then_inc(S("tile_done"), 1)

        def project_tok(pe, tag, wv, kt, c0, cols, t, src, bias=None):
            b = tile_bank(pe, tag)
            if bias is not None:
                nc.tensor.matmul(b[:, 0:cols], lhsT=ones[0:1, :], rhs=bias, start=True, stop=False)
            for k in range(kt):
                mm = nc.tensor.matmul(b[:, 0:cols], lhsT=src[:, k, P * t:P * t + P], rhs=wv[:, k, c0:c0 + cols],
                                      start=k == 0 and bias is None, stop=k == kt - 1)
            mm.then_inc(S("tile_done"), 1)

        def spent(n):
            spent_at[n] = len(tile_no)

        def tile_in(eng, tag):
            n = tile_no[tag]
            eng.wait_ge(S("tile_done"), n + 1)
            return bank[4 + n % 4]

        def residual_pe(pe, tag, at, src):
            for j in range(2):
                slot_ready(pe, at + j)
                for t in range(TT):
                    project_tok(pe, (tag, j, t), slot_view(at + j, KT, 512), KT, 0, 512, t, src)
                spent(at + j)

        def residual_dve(dve, tag):
            for j in range(2):
                for t in range(TT):
                    b = tile_in(dve, (tag, j, t))
                    hs = h[:, t, 512 * j:512 * j + 512]
                    nc.vector.tensor_tensor(hs, hs, b[:, :], ALU.add).then_inc(S("tile_read"), 1)

        def spread(ap, n):
            return ap.unsqueeze(len(ap.shape)).to_broadcast(list(ap.shape) + [n])

        def toeplitz(tensor, offset, step, rows, heads, pitch, width):
            return bass.AP(tensor=tensor, offset=offset, ap=[[step, rows], [pitch, heads], [1, width]])

        block = ctx.enter_context(nc.Block())

        @block.tensor
        def _(pe):
            pe.wait_ge(S("consts"), 1)
            pe.wait_ge(S("vrows_landed"), 16 * NVROWS)
            nc.tensor.transpose(bank[0][:, 0:NVEC], vrows[0:NVEC, :], ident[0:NVEC, 0:NVEC]).then_inc(S("vecs_turned"), 1)
            pe.wait_ge(S("table_in"), 32)
            nc.tensor.matmul(bank[1][0:HEADS, 0:T], lhsT=rel2[:, :], rhs=dist_oh[0:BUCKETS, :], start=True,
                             stop=True).then_inc(S("table_done"), 1)
            phase_end(pe, "pe")

            norm_pe(pe, "mix")
            wait_nT(pe, "mix", KT)
            pe.wait_ge(S("brow_in"), 16)
            for s in range(3):
                slot_ready(pe, s)
                for t in range(TT):
                    project_tok(pe, ("qkv", s, t), slot_view(s, KT, 512), KT, 0, 512, t, nT,
                                brow[0:1, 512 * s:512 * s + 512])
                spent(s)
            for s in range(3, 10):
                slot_ready(pe, s)
                for m in range(4):
                    project_T(pe, ("in1", 4 * (s - 3) + m), slot_view(s, KT, 512), KT, P * m, P, nT)
                spent(s)
            phase_end(pe, "pe")

            for s in range(2):
                pe.wait_ge(S("qk_normed"), s + 1)
                for m in range(4):
                    for t in range(TT):
                        at = T * (m % 2) + P * t
                        mm = nc.tensor.transpose(bank[2 * s + m // 2][:, at:at + P],
                                                 z_tok[:, s, t, P * m:P * m + P], ident[:, :])
                mm.then_inc(S("qk_turned"), 1)
            phase_end(pe, "pe")
            attention_pe(pe, ATT1, units_block1())
            phase_end(pe, "pe")
            pe.wait_ge(S("conv_done"), 4)
            for s in range(10, 12):
                slot_ready(pe, s)
                wv = slot_view(s, KT, 512)
                for m in range(4):
                    b = tile_bank(pe, ("mix", 4 * (s - 10) + m))
                    for part in range(2):
                        for k in range(4):
                            mm = nc.tensor.matmul(b[:, T * part:T * part + T],
                                                  lhsT=wv[:, 4 * part + k, P * m:P * m + P],
                                                  rhs=mixT[:, 4 * part + k, :], start=k == 0, stop=k == 3)
                    mm.then_inc(S("tile_done"), 1)
                spent(s)
            pe.wait_ge(S("mT_ready"), KT)
            residual_pe(pe, "wo", 12, mT)
            phase_end(pe, "pe")

            norm_pe(pe, "ffn")
            wait_nT(pe, "ffn", KT)
            pe.wait_ge(S("router_in"), 16 * 4)
            for t in range(TT):
                project_tok(pe, ("router", t), wgr, KT, 0, 36, t, nT, br36[0:1, :])
            pe.wait_ge(S("picked_ready"), 1)
            b = bank[0]
            nc.tensor.matmul(b[:, 0:EXPERTS], lhsT=earlier[:, :], rhs=picked[:, 0, :], start=True, stop=True)
            nc.tensor.matmul(b[:, 64:64 + EXPERTS], lhsT=earlier[:, :], rhs=picked[:, 1, :], start=True, stop=False)
            nc.tensor.matmul(b[:, 64:64 + EXPERTS], lhsT=ones[:, :], rhs=picked[:, 0, :], start=False, stop=True)
            nc.tensor.matmul(b[:, 128:128 + EXPERTS], lhsT=ones[:, :], rhs=picked[:, 0, :], start=True, stop=False)
            nc.tensor.matmul(b[:, 128:128 + EXPERTS], lhsT=ones[:, :], rhs=picked[:, 1, :], start=False,
                             stop=True).then_inc(S("rows_counted"), 1)
            phase_end(pe, "pe")
            def gather(buf):
                for k in range(KT):
                    for t in range(TT):
                        mm = nc.tensor.matmul(bank[k // 4][:, P * (k % 4):P * (k % 4) + P],
                                              lhsT=xn[:, t, P * k:P * k + P], rhs=pick[:, buf, t, :],
                                              start=t == 0, stop=t == TT - 1)
                mm.then_inc(S("gathered"), 1)

            def scatter(i, j):
                pe.wait_ge(S("out_a"), i * 2 + (j + 1))
                pe.wait_ge(S("out_b"), i * 2 + (j + 1))
                pe.wait_ge(S("turned_pick"), i * 2 + (j + 1))
                for c in range(4):
                    if c >= 2:
                        pe.wait_ge(S("row_added"), i * 8 + (4 * j + c - 1))
                    nc.tensor.matmul(bank[6 + c % 2][:, :], lhsT=pickT[:, c // 2, :],
                                     rhs=out_r[:, 512 * (c % 2):512 * (c % 2) + 512], start=True,
                                     stop=True).then_inc(S("scattered"), 1)

            over = pe.value_load(overfull[0:1, 0:1], min_val=0, max_val=1)
            with pe.If(over < 1):
                gather(0)
                with pe.Fori(0, EXPERTS // 2) as i:
                    for j in range(2):
                        n = MOE_AT + 3 * j
                        pe.wait_ge(S("gathT_a"), i * 2 + (j + 1))
                        pe.wait_ge(S("gathT_b"), i * 2 + (j + 1))
                        pe.wait_ge(S("hid_ready"), i * 2 + (j + 1))
                        for part in range(2):
                            slot_ready(pe, n + part, i)
                            wv = slot_view(n + part, KT, FF)
                            for k in range(KT):
                                mm = nc.tensor.matmul(bank[2 + part][:, :], lhsT=gathT[:, k, :], rhs=wv[:, k, :],
                                                      start=k == 0, stop=k == KT - 1)
                        mm.then_inc(S("w13_used"), 1)
                        pe.wait_ge(S("pick_ready"), i * 2 + (j + 2))
                        gather((j + 1) % 2)
                        pe.wait_ge(S("hid_ready"), i * 2 + (j + 2))
                        pe.wait_ge(S("hid_rT_ready"), i * 2 + (j + 1))
                        for f in range(FT):
                            mm = nc.tensor.transpose(bank[4][:, P * f:P * f + P], hid_r[:, P * f:P * f + P],
                                                     ident[:, :])
                        mm.then_inc(S("hid_turned"), 1)
                        scatter(i, j)
                        for t in range(TT):
                            nc.tensor.transpose(bank[5][:, P * (t + 1):P * (t + 2)], pick[:, j, t, :], ident[:, :])
                        for t in range(TT):
                            mm = nc.tensor.matmul(bank[5][:, 0:1], lhsT=pick[:, j, t, :],
                                                  rhs=gatew[:, t, bass.ds(i * 2 + j, 1)], start=t == 0,
                                                  stop=t == TT - 1)
                        mm.then_inc(S("pick_turned"), 1)
                        pe.wait_ge(S("hid_rT_ready"), i * 2 + (j + 2))
                        slot_ready(pe, n + 2, i)
                        w2v = slot_view(n + 2, FT, D)
                        for half in range(2):
                            pe.wait_ge(S("row_added"), i * 8 + (4 * j + 3 + half))
                            for f in range(FT):
                                mm = nc.tensor.matmul(bank[6 + half][:, :], lhsT=hid_rT[:, f, :],
                                                      rhs=w2v[:, f, 512 * half:512 * half + 512],
                                                      start=f == 0, stop=f == FT - 1)
                        mm.then_inc(S("w2_used"), 1)
                scatter(EXPERTS // 2, 0)
            with pe.Else():
                with pe.Fori(0, EXPERTS // 2) as i:
                    for j in range(2):
                        n = MOE_AT + 3 * j
                        slot_ready(pe, n, i)
                        slot_ready(pe, n + 1, i)
                        w1v, w3v = slot_view(n, KT, FF), slot_view(n + 1, KT, FF)
                        for f in range(FT):
                            pe.wait_ge(S("moe_hidden"), i * (2 * FT) + (FT * j + f + 1))
                            for part, wv in enumerate((w1v, w3v)):
                                for k in range(KT):
                                    mm = nc.tensor.matmul(bank[f][:, T * part:T * part + T],
                                                          lhsT=wv[:, k, P * f:P * f + P], rhs=nT[:, k, :],
                                                          start=k == 0, stop=k == KT - 1)
                            mm.then_inc(S("moe_products"), 1)
                        pe.drain().then_inc(S("w13_used"), 1)
                        slot_ready(pe, n + 2, i)
                        w2v = slot_view(n + 2, FT, D)
                        pe.wait_ge(S("moe_hidden"), i * (2 * FT) + FT * (j + 2))
                        for c in range(4):
                            t, half = c // 2, c % 2
                            pe.wait_ge(S("moe_added"), i * 8 + (4 * j + c + 1))
                            for f in range(FT):
                                mm = nc.tensor.matmul(bank[4 + c][:, :], lhsT=hidT[:, f, P * t:P * t + P],
                                                      rhs=w2v[:, f, 512 * half:512 * half + 512],
                                                      start=f == 0, stop=f == FT - 1)
                            mm.then_inc(S("moe_out"), 1)
                        pe.drain().then_inc(S("w2_used"), 1)
            phase_end(pe, "pe")

            norm_pe(pe, "ple")
            pe.wait_ge(S("ple_in"), 32)
            for k in range(2):
                for t in range(TT):
                    wait_nT(pe, "ple", 2)
                    mm = nc.tensor.transpose(bank[0][:, T * k + P * t:T * k + P * t + P],
                                             p_tok[:, t, P * k:P * k + P], ident[:, :])
            mm.then_inc(S("p_turned"), 1)
            wait_nT(pe, "ple", KT)
            for j in range(2):
                n = LATE_AT + j
                slot_ready(pe, n)
                for t in range(TT):
                    project_tok(pe, ("gate", j, t), slot_view(n, KT, 512), KT, 0, 512, t, nT,
                                brow[0:1, 512 * j:512 * j + 512])
                spent(n)
            pe.wait_ge(S("pT_ready"), 1)
            n = LATE_AT + 2
            slot_ready(pe, n)
            for j in range(2):
                for t in range(TT):
                    project_tok(pe, ("ple", j, t), slot_view(n, 2, D), 2, 512 * j, 512, t, pT)
            spent(n)
            phase_end(pe, "pe")

            norm_pe(pe, "mix2")
            wait_nT(pe, "mix2", KT)
            n = LATE_AT + 3
            slot_ready(pe, n)
            for m in range(4):
                project_T(pe, ("gqk", m), slot_view(n, KT, 512), KT, P * m, P, nT)
            spent(n)
            for s in range(2):
                slot_ready(pe, n + 1 + s)
                for t in range(TT):
                    project_tok(pe, ("gvr", s, t), slot_view(n + 1 + s, KT, 512), KT, 0, 512, t, nT)
                spent(n + 1 + s)
            slot_ready(pe, n + 3)
            for m in range(4):
                project_T(pe, ("nq", m), slot_view(n + 3, KT, 512), KT, P * m, P, nT)
            spent(n + 3)
            slot_ready(pe, n + 4)
            for m in range(3):
                project_T(pe, ("kv", m), slot_view(n + 4, KT, 384), KT, P * m, P, nT)
            spent(n + 4)
            slot_ready(pe, n + 5)
            wv = slot_view(n + 5, KT, 408)
            project_T(pe, ("kv", 3), wv, KT, P, P, nT)
            for s in range(2):
                for t in range(TT):
                    project_tok(pe, ("vsw", s, t), wv, KT, 256 * s, P, t, nT)
            for t in range(TT):
                project_tok(pe, ("ng", t), wv, KT, 384, 24, t, nT)
            spent(n + 5)
            pe.wait_ge(S("late_in"), 16 * NLATE)
            project_T(pe, ("glr", 0), w_glr, KT, 0, 16, nT)
            pe.wait_ge(S("glr_ready"), 1)
            for c in range(2):
                b = tile_bank(pe, ("loga", c))
                nc.tensor.matmul(b[:, 0:T], lhsT=gate_w2[:, P * c:P * c + P], rhs=glrT[:, :], start=True,
                                 stop=True).then_inc(S("tile_done"), 1)
            phase_end(pe, "pe")

            for b, m in ((0, 0), (1, 1), (4, 2), (5, 3)):
                for g in range(2):
                    mm = nc.tensor.matmul(bank[b][:, T * g:T * g + T], lhsT=sel_dup[:, g, :], rhs=kvT[:, m, :],
                                          start=True, stop=True)
                mm.then_inc(S("dup_done"), 1)
            for s in range(2):
                mm = nc.tensor.transpose(bank[6][:, SUB * s:SUB * s + SUB], pos_rows[:, s, :], ident[0:SUB, 0:SUB])
            mm.then_inc(S("pos_turned"), 1)
            pe.wait_ge(S("cmp_in_ready"), 2)
            for s in range(2):
                for i in range(SUB):
                    mm = nc.tensor.matmul(bank[2][:, 32 * s:32 * s + 2 * N_CMP], lhsT=cmp_w1[:, s, i, :],
                                          rhs=cmp_in[:, s, i, :, :].rearrange("p g n -> p (g n)"),
                                          start=i == 0, stop=i == SUB - 1)
            mm.then_inc(S("cmp_hidden"), 1)
            pe.wait_ge(S("cmp_gelu"), 1)
            for half in range(2):
                nc.tensor.matmul(bank[3][DH * half:DH * half + DH, 0:2 * N_CMP], lhsT=cmp_w2[:, 0, :],
                                 rhs=cmp_h[:, 0, :], start=True, stop=True)
            for g in range(2):
                mm = nc.tensor.matmul(bank[7][0:N_CMP, DH * g:DH * g + DH],
                                      lhsT=cmp_h[:, 1, N_CMP * g:N_CMP * g + N_CMP], rhs=cmp_w2[:, 1, :],
                                      start=True, stop=True)
            mm.then_inc(S("cmp_out"), 1)
            phase_end(pe, "pe")

            pe.wait_ge(S("q_dec_ready"), 2)
            for u in range(NSUB):
                for c in range(2):
                    pe.wait_ge(S("k_dec_ready"), 2 * u + c + 1)
                    for r in range(2):
                        rows = slice(DH * r, DH * r + DH)
                        for st in range(1 if u < NSUB // 2 else 2):
                            mm = nc.tensor.matmul(bank[2 * c + r][:, T * st + SUB * u:T * st + SUB * u + SUB],
                                                  lhsT=k_dec[rows, u % 2, c, P * st:P * st + P],
                                                  rhs=q_dec[rows, c, SUB * u:SUB * u + SUB], start=True, stop=True)
                    mm.then_inc(S("k_dec_used"), 1)
            for c in range(2):
                pe.wait_ge(S("diag_ready"), c + 1)
                for r in range(2):
                    rows = slice(DH * r, DH * r + DH)
                    dv = diag[rows, :, :, :].rearrange("p u t j -> p (u t) j")
                    for j in range(SUB):
                        mm = nc.tensor.matmul(bank[4 + 2 * c + r][:, 0:T], lhsT=modmask[rows, SUB - 1 - j:SUB - 1 - j + P],
                                              rhs=dv[:, :, j], start=j == 0, stop=j == SUB - 1)
                mm.then_inc(S("diag_used"), 1)
            pe.wait_ge(S("gla_a_ready"), 1)
            for t in range(TT):
                for hh in range(GLA_HEADS):
                    for st in range(t + 1):
                        mm = nc.tensor.matmul(bank[t][:, P * hh:P * hh + P], lhsT=gla_a[:, hh, st, P * t:P * t + P],
                                              rhs=gv[:, st, P * hh:P * hh + P], start=st == 0, stop=st == t)
            mm.then_inc(S("gla_out"), 1)
            pe.wait_ge(S("gla_normed"), 1)
            for hh in range(GLA_HEADS):
                for t in range(TT):
                    at = T * (hh % 2) + P * t
                    mm = nc.tensor.transpose(bank[2 + hh // 2][:, at:at + P], o_gla[:, t, P * hh:P * hh + P],
                                             ident[:, :])
            mm.then_inc(S("gla_turned"), 1)
            phase_end(pe, "pe")
            pe.wait_ge(S("bias2_in"), 32)
            attention_pe(pe, NSA, units_nsa())
            phase_end(pe, "pe")
            residual_pe(pe, "wout", LATE_AT + 9, catT)
            phase_end(pe, "pe")

            norm_pe(pe, "mem")
            wait_nT(pe, "mem", KT)
            for s in range(2):
                n = LATE_AT + 11 + s
                slot_ready(pe, n)
                for m in range(4):
                    project_T(pe, ("xk", 4 * s + m), slot_view(n, KT, 512), KT, P * m, P, nT)
                spent(n)
            residual_pe(pe, "xv", LATE_AT + 13, nT)
            phase_end(pe, "pe")
            norm_pe(pe, "xa")
            wait_nT(pe, "xa", KT)
            for s in range(2):
                n = LATE_AT + 15 + s
                slot_ready(pe, n)
                for m in range(4):
                    project_T(pe, ("xq", 4 * s + m), slot_view(n, KT, 512), KT, P * m, P, nT)
                spent(n)
            phase_end(pe, "pe")
            attention_pe(pe, CROSS, units_cross())
            phase_end(pe, "pe")
            residual_pe(pe, "xo", LATE_AT + 17, xoT)
            phase_end(pe, "pe")
            phases["rings free"] = phases["pe"]

            norm_pe(pe, "peer")
            pe.wait_ge(S("sk_in"), 16)
            for hh in range(PH):
                wait_nT(pe, "peer", 4)
                mm = nc.tensor.transpose(bank[hh // 4][:, P * (hh % 4):P * (hh % 4) + P],
                                         sk_rows[:, 2 * hh:2 * hh + 2, :].rearrange("p a d -> p (a d)"), ident[:, :])
            mm.then_inc(S("sk_turned"), 1)
            wait_nT(pe, "peer", KT)
            for s in range(2):
                n = LATE_AT + 19 + s
                slot_ready(pe, n)
                for m in range(4):
                    project_T(pe, ("pq", 4 * s + m), slot_view(n, KT, 512), KT, P * m, P, nT)
                spent(n)
            phase_end(pe, "pe")
            for t in range(TT):
                for q in range(4):
                    for x in range(4):
                        hp = 2 * (4 * (q % 2) + x) + q // 2
                        rows = slice(DH * (hp % 2), DH * (hp % 2) + DH)
                        mm = nc.tensor.matmul(bank[4 * t + q][:, P * x:P * x + P],
                                              lhsT=pqT[rows, hp // 2, P * t:P * t + P], rhs=skT[rows, hp // 2, :],
                                              start=True, stop=True)
                    mm.then_inc(S("peer_scores"), 1)
            phase_end(pe, "pe")
            def turn(t, r, i, first=False):
                pe.wait_ge(S(f"down_landed_{r}"), i * 16 + 16)
                for b in range(2):
                    if not first:
                        pe.wait_ge(S(f"down_lo_{b}"), t)
                    for k in range(4 * b, 4 * b + 4):
                        mm = nc.tensor.transpose(bank[4 + b][:, P * (k % 4):P * (k % 4) + P],
                                                 down[r][:, P * k:P * k + P], ident[:, :])
                    mm.then_inc(S(f"down_turned_{b}"), 1)

            def expert_scores(t, r, early):
                if not early:
                    pe.wait_ge(S("expert_gelu"), t - 1)
                out_bank = bank[6 + r % 2][:, 0:T]
                terms = [(downT_hi, x_hi, "down_hi"), (downT_hi, x_lo, None), (downT_lo, x_hi, "down_lo")]
                for a, b, sem in terms:
                    for k in range(KT):
                        if sem and k % 4 == 0:
                            pe.wait_ge(S(f"{sem}_{k // 4}"), t + 1)
                        mm = nc.tensor.matmul(out_bank, lhsT=a[:, r % 2, k, :], rhs=b[:, k, :],
                                              start=a is downT_hi and b is x_hi and k == 0,
                                              stop=a is downT_lo and k == KT - 1)
                mm.then_inc(S("expert_scored"), 1)

            steps = NKEYS // PR
            pe.wait_ge(S("x_lo"), 1)
            turn(0, 0, 0, first=True)
            for t in range(PR):
                turn(t + 1, (t + 1) % PR, (t + 1) // PR)
                expert_scores(t, t, t < 2)
            with pe.Fori(1, steps - 1) as i:
                for r in range(PR):
                    turn(i * PR + (r + 1), (r + 1) % PR, i if r + 1 < PR else i + 1)
                    expert_scores(i * PR + r, r, False)
            for t in range(NKEYS - PR, NKEYS):
                if t + 1 < NKEYS:
                    turn(t + 1, (t + 1) % PR, (t + 1) // PR)
                expert_scores(t, t % PR, False)
            phase_end(pe, "pe")
            phases["scores done"] = phases["pe"]

            pe.wait_ge(S("peer_top"), 1)
            for a in range(3):
                for t in range(TT):
                    mm = nc.tensor.transpose(bank[a][:, P * t:P * t + P], fin3[:, a, t, :], ident[:, :])
                mm.then_inc(S("top_turned"), 1)
            phase_end(pe, "pe")
            phases["indices turned"] = phases["pe"]

            def gate_group(i, q):
                for pair in range(2):
                    pe.wait_ge(S("hot_ready"), i * (2 * GROUPS) + (2 * q + pair + 1))
                    if pair == 0:
                        pe.wait_ge(S("gate_read"), i * GROUPS + (q + 1))
                    for x in range(2):
                        tok = 2 * pair + x
                        mm = nc.tensor.matmul(bank[4 + q % 4][:, P * tok:P * tok + P], lhsT=hot[:, pair, x, 1, :],
                                              rhs=hot[:, pair, x, 0, :], start=True, stop=True)
                    if pair == 0:
                        mm.then_inc(S("hot_used0"), 1)
                mm.then_inc(S("hot_used1"), 1)

            with pe.Fori(0, T // (4 * GROUPS)) as i:
                for q in range(GROUPS):
                    gate_group(i, q)
            phase_end(pe, "pe")

            def expert_out(t, r, first_tile, last_tile):
                terms = [(e_hi, u_hi, ("expert_hi", "up_hi")), (e_lo, u_hi, ("expert_lo",)), (e_hi, u_lo, ("up_lo",))]
                for n, (a, b, needed) in enumerate(terms):
                    for sem in needed:
                        pe.wait_ge(S(sem), t + 1)
                    for c in range(4):
                        mm = nc.tensor.matmul(bank[c][:, :], lhsT=a[:, r % 2, P * (c // 2):P * (c // 2) + P],
                                              rhs=b[:, r % 2, 512 * (c % 2):512 * (c % 2) + 512],
                                              start=first_tile and n == 0, stop=last_tile and n == 2,
                                              skip_group_check=True)
                mm.then_inc(S("up_used"), 1)

            for t in range(PR):
                expert_out(t, t, t == 0, False)
            with pe.Fori(1, steps - 1) as i:
                for r in range(PR):
                    expert_out(i * PR + r, r, False, False)
            for t in range(NKEYS - PR, NKEYS):
                expert_out(t, t % PR, False, t == NKEYS - 1)
            phase_end(pe, "pe")

        @block.scalar
        def _(act):
            chain = Chain(act, S("act_chain"))
            for name, rows in ROWS:
                src = w[name][0]
                src = src.rearrange("j (k p) -> (j k) p", p=P) if name == "conv_w" else \
                    src.rearrange("(k p) -> k p", p=P)
                act.dma_start(vrows[COL[name]:COL[name] + rows, :], src).then_inc(S("vrows_landed"), 16)
            for name in ("g_q", "g_k"):
                for half in range(2):
                    act.dma_start(vrows[COL[name]:COL[name] + 1, DH * half:DH * half + DH],
                                  w[name][0:1, :]).then_inc(S("vrows_landed"), 16)
            act.dma_start(dist_oh[0:BUCKETS, :], buckets).then_inc(S("table_in"), 16)
            act.dma_start(rel2[:, :], w["rel_bias_2"]).then_inc(S("table_in"), 16)
            act.dma_start(h[:, :, :], w["x"][0].rearrange("(t p) d -> p t d", p=P)).then_inc(S("x_in"), 16)
            act.dma_start(brow[0:1, :], w["b_in"][0:1, 0:1536]).then_inc(S("brow_in"), 16)
            act.wait_ge(S("table_done"), 1)
            nc.scalar.copy(dist_row[0:HEADS, T:TAB], bank[1][0:HEADS, 0:T]).then_inc(S("table_row"), 1)
            act.wait_ge(S("table_row"), 2)
            act.dma_start(table_dram[:, :], dist_row[0:HEADS, :]).then_inc(S("table_out"), 16)
            act.wait_ge(S("table_out"), 16)
            phase_end(act, "act")

            rel1 = w["rel_bias"]
            act.dma_start(bias1[64:P, :, :], toeplitz(rel1.tensor, 0, 1, 64, HEADS, REL, T)).then_inc(S("bias1_in"), 16)
            act.dma_start(bias1[0:64, :, 64:T],
                          toeplitz(rel1.tensor, 0, 1, 64, HEADS, REL, T - 64)).then_inc(S("bias1_in"), 16)
            act.wait_ge(S("x_in"), 16)
            norm_act(act, chain, "mix", h)
            for s in range(3):
                for t in range(TT):
                    b = tile_in(act, ("qkv", s, t))
                    nc.scalar.copy(z_tok[:, s, t, :], b[:, :]).then_inc(S("tile_read"), 1)
            for m in range(28):
                b = tile_in(act, ("in1", m))
                dst = convT[:, m, :] if m < 12 else sigT[:, m - 12, :]
                nc.scalar.activation(dst, b[:, 0:T], ACT.Identity if m < 12 else ACT.Sigmoid,
                                     bias=col("b_in", 12 + m)).then_inc(S("tile_read"), 1)
            phase_end(act, "act")
            act.wait_ge(S("qk_squares"), 2)
            nc.scalar.activation(qk_stat[:, 1, :], qk_stat[:, 0, :], ACT.Sqrt, bias=eps[:, 0:1],
                                 scale=1.0 / DH).then_inc(S("qk_rms"), 1)
            act.wait_ge(S("bias1_in"), 32)
            phase_end(act, "act")
            attention_act(act, ATT1, units_block1())
            phase_end(act, "act")
            act.dma_start(brow[0:1, 0:D], w["b_ple_gate"]).then_inc(S("ple_in"), 16)
            phase_end(act, "act")

            act.dma_start(wgr[:, :, 0:4], w["w_group"][0].rearrange("(k p) n -> p k n", p=P)).then_inc(S("router_in"), 16)
            act.dma_start(wgr[:, :, 4:36], w["w_router"][0].rearrange("(k p) n -> p k n", p=P)).then_inc(S("router_in"), 16)
            act.dma_start(br36[0:1, 0:4], w["b_group"]).then_inc(S("router_in"), 16)
            act.dma_start(br36[0:1, 4:36], w["b_router"]).then_inc(S("router_in"), 16)
            act.dma_start(gain_row[:, :], w["g_ffn"][0].partition_broadcast(P)).then_inc(S("gain_in"), 16)
            norm_act(act, chain, "ffn", h)
            for t in range(TT):
                b = tile_in(act, ("router", t))
                nc.scalar.copy(logit[:, t, 0:36], b[:, 0:36]).then_inc(S("tile_read"), 1)
            act.wait_ge(S("tile_read"), tile_no[("router", 1)] + 1)
            act.sem_inc(S("logits"), 1)
            act.wait_ge(S("group_shifted"), 1)
            for t in range(TT):
                nc.scalar.activation(route[:, t, 12:16], route[:, t, 12:16], ACT.Exp,
                                     accum_out=route[:, t, 16:17]).then_inc(S("group_exp"), 1)
            act.wait_ge(S("second_gap"), 1)
            nc.scalar.activation(route[:, :, 18:19], route[:, :, 18:19], ACT.Exp).then_inc(S("second_exp"), 1)
            phase_end(act, "act")
            over = act.value_load(overfull[0:1, 0:1], min_val=0, max_val=1)

            def gathered_a(i, j):
                act.wait_ge(S("gathered"), i * 2 + (j + 1))
                nc.scalar.copy(gathT[:, 0:4, :].rearrange("p k s -> p (k s)"), bank[0][:, :]).then_inc(S("gathT_a"), 1)

            with act.If(over < 1):
                act.wait_ge(S("gathered"), 1)
                nc.scalar.copy(gathT[:, 0:4, :].rearrange("p k s -> p (k s)"), bank[0][:, :]).then_inc(S("gathT_a"), 1)
                with act.Fori(0, EXPERTS // 2) as i:
                    for j in range(2):
                        act.wait_ge(S("w13_used"), i * 2 + (j + 1))
                        act.wait_ge(S("hid_ready"), i * 2 + (j + 1))
                        nc.scalar.activation(silu_r[:, :], bank[2][:, :], ACT.Silu).then_inc(S("silu_ready"), 1)
                        gathered_a(i, j + 1)
                        act.wait_ge(S("hid_turned"), i * 2 + (j + 2))
                        nc.scalar.copy(hid_rT[:, :, :].rearrange("p f s -> p (f s)"), bank[4][:, :]).then_inc(
                            S("hid_rT_ready"), 1)
                        act.wait_ge(S("pick_turned"), i * 2 + (j + 1))
                        act.wait_ge(S("scattered"), i * 8 + (4 * j + 4))
                        act.wait_ge(S("out_b"), i * 2 + (j + 1))
                        nc.scalar.copy(row_w[:, :], bank[5][:, 0:1])
                        nc.scalar.copy(pickT[:, :, :].rearrange("p t s -> p (t s)"), bank[5][:, P:3 * P]).then_inc(
                            S("turned_pick"), 1)
                        act.wait_ge(S("w2_used"), i * 2 + (j + 1))
                        act.wait_ge(S("turned_pick"), i * 2 + (j + 2))
                        nc.scalar.activation(out_r[:, 0:512], bank[6][:, :], ACT.Copy, scale=row_w[:, 0:1]).then_inc(
                            S("out_a"), 1)
            with act.Else():
                with act.Fori(0, EXPERTS // 2) as i:
                    for j in range(2):
                        for f in range(FT):
                            act.wait_ge(S("moe_products"), i * (2 * FT) + (FT * j + f + 1))
                            act.wait_ge(S("moe_hidden"), i * (2 * FT) + (FT * j + f + 1))
                            nc.scalar.activation(silu_h[:, f, :], bank[f][:, 0:T], ACT.Silu).then_inc(S("moe_silu"), 1)
            phase_end(act, "act")

            act.dma_start(p_tok[:, :, :], w["p"][0, 0].rearrange("(t p) d -> p t d", p=P)).then_inc(S("ple_in"), 16)
            norm_act(act, chain, "ple", h)
            act.wait_ge(S("p_turned"), 1)
            nc.scalar.copy(pT[:, :, :].rearrange("p k t -> p (k t)"), bank[0][:, :]).then_inc(S("pT_ready"), 1)
            for j in range(2):
                for t in range(TT):
                    b = tile_in(act, ("gate", j, t))
                    nc.scalar.activation(gate_t[:, t, 512 * j:512 * j + 512], b[:, :], ACT.Sigmoid).then_inc(
                        S("tile_read"), 1)
            act.wait_ge(S("tile_read"), tile_no[("gate", 1, 1)] + 1)
            act.sem_inc(S("gate_ready"), 1)
            act.dma_start(w_glr[:, :, :], w["w_in_2"][0].rearrange("(k p) n -> p k n", p=P)[:, :, 1536:1552]).then_inc(
                S("late_in"), 16)
            act.dma_start(gate_w2[:, :], w["gla_gate_w2_2"][0]).then_inc(S("late_in"), 16)
            for s, name in enumerate(("k", "v")):
                act.dma_start(cmp_w2[:, s, :], w[f"cmp_{name}_w2_2"][0]).then_inc(S("late_in"), 16)
                act.dma_start(pos_rows[:, s, :], w[f"cmp_pos_{name}_2"][0].rearrange("(i a) d -> i (a d)", a=2)).then_inc(
                    S("late_in"), 16)
            phase_end(act, "act")

            for s, name in enumerate(("k", "v")):
                act.dma_start(cmp_w1[:, s, :, :], w[f"cmp_{name}_w1_2"][0].rearrange("(i p) n -> p i n", p=P)).then_inc(
                    S("cmp_w1_in"), 16)
            norm_act(act, chain, "mix2", h)
            for m in range(4):
                b = tile_in(act, ("gqk", m))
                nc.scalar.activation(gqkT[:, m, :], b[:, 0:T], ACT.Copy, scale=0.125 if m < 2 else 1.0).then_inc(
                    S("tile_read"), 1)
            for s in range(2):
                for t in range(TT):
                    b = tile_in(act, ("gvr", s, t))
                    nc.scalar.activation((gv, gr)[s][:, t, :], b[:, :], (ACT.Copy, ACT.Silu)[s]).then_inc(
                        S("tile_read"), 1)
            for m in range(4):
                b = tile_in(act, ("nq", m))
                nc.scalar.activation(nqT[:, m, :], b[:, 0:T], ACT.Copy, scale=0.125).then_inc(S("tile_read"), 1)
            for m in range(4):
                b = tile_in(act, ("kv", m))
                nc.scalar.copy(kvT[:, m, :], b[:, 0:T]).then_inc(S("tile_read"), 1)
            for s in range(2):
                for t in range(TT):
                    b = tile_in(act, ("vsw", s, t))
                    nc.scalar.copy(v_sw[:, s, t, :], b[:, 0:P]).then_inc(S("tile_read"), 1)
            for t in range(TT):
                b = tile_in(act, ("ng", t))
                nc.scalar.activation(nsa_gate[:, t, :], b[:, 0:24], ACT.Sigmoid).then_inc(S("tile_read"), 1)
            b = tile_in(act, ("glr", 0))
            nc.scalar.copy(glrT[:, :], b[0:16, 0:T]).then_inc(S("tile_read"), 1)
            act.wait_ge(S("tile_read"), tile_no[("glr", 0)] + 1)
            act.sem_inc(S("glr_ready"), 1)
            for c in range(2):
                b = tile_in(act, ("loga", c))
                nc.scalar.activation(loga[:, c, :], b[:, 0:T], ACT.Identity, bias=col("gla_gate_b_2", c)).then_inc(
                    S("tile_read"), 1)
            act.wait_ge(S("tile_read"), tile_no[("loga", 1)] + 1)
            tmp = k_dec[:, 0, :, :]
            chain(nc.scalar.activation(tmp, loga[:, :, :], ACT.Abs))
            chain(nc.scalar.activation(tmp, tmp, ACT.Exp, scale=-1.0))
            nc.scalar.activation(tmp, tmp, ACT.Ln, bias=1.0).then_inc(S("log_part"), 1)
            act.wait_ge(S("cmp_w1_in"), 32)
            phase_end(act, "act")

            act.wait_ge(S("pos_turned"), 1)
            nc.scalar.copy(posT[:, :, :].rearrange("p s i -> p (s i)"), bank[6][:, 0:2 * SUB]).then_inc(S("pos_ready"), 1)
            act.wait_ge(S("dup_done"), 4)
            for s in range(2):
                nc.scalar.copy(dupT[:, 2 * s:2 * s + 2, :].rearrange("p g t -> p (g t)"), bank[4 + s][:, :])
            act.wait_ge(S("cmp_hidden"), 1)
            nc.scalar.activation(cmp_h[:, :, :], bank[2][:, 0:64].rearrange("p (s n) -> p s n", s=2)[:, :, 0:2 * N_CMP],
                                 ACT.Gelu_apprx_tanh).then_inc(S("cmp_gelu"), 1)
            act.wait_ge(S("cmp_out"), 1)
            nc.scalar.copy(k_cmpT[:, :], bank[3][:, 0:2 * N_CMP])
            nc.scalar.copy(v_cmp[:, :, :].rearrange("n g d -> n (g d)"), bank[7][0:N_CMP, 0:P])
            phase_end(act, "act")

            for c in range(2):
                act.wait_ge(S("q_diff"), c + 1)
                nc.scalar.activation(q_dec[:, c, :], q_dec[:, c, :], ACT.Exp).then_inc(S("q_exp"), 1)
            for u in range(NSUB):
                for c in range(2):
                    act.wait_ge(S("k_diff"), 2 * u + c + 1)
                    nc.scalar.activation(k_dec[:, u % 2, c, :], k_dec[:, u % 2, c, :], ACT.Exp, scale=-1.0).then_inc(
                        S("k_exp"), 1)
            for c in range(2):
                act.wait_ge(S("diag_diff"), c + 1)
                nc.scalar.activation(diag[:, :, :, :], diag[:, :, :, :], ACT.Exp).then_inc(S("diag_exp"), 1)
            act.wait_ge(S("gla_out"), 1)
            for t in range(TT):
                nc.scalar.copy(o_gla[:, t, :], bank[t][:, :]).then_inc(S("o_gla_ready"), 1)
            act.wait_ge(S("gla_squares"), 1)
            nc.scalar.activation(gla_stat[:, 1, :], gla_stat[:, 0, :], ACT.Sqrt, bias=eps[:, 0:1],
                                 scale=1.0 / P).then_inc(S("gla_rms"), 1)
            phase_end(act, "act")
            act.dma_start(bias_sw[:, :, :], toeplitz(table_dram, T - P + 1, 1, P, HEADS, TAB, T)).then_inc(S("bias2_in"), 16)
            act.dma_start(bias_c[0:N_CMP, :, :], toeplitz(
                table_dram, T - (CMP_BLOCK - 1) - CMP_STRIDE * (N_CMP - 1), CMP_STRIDE, N_CMP, HEADS, TAB, T)).then_inc(S("bias2_in"), 16)
            attention_act(act, NSA, units_nsa())
            phase_end(act, "act")
            act.dma_start(mem_tok[:, :, :], w["mem_2"][0].rearrange("(t p) d -> p t d", p=P)).then_inc(S("mem_in"), 16)
            phase_end(act, "act")

            act.wait_ge(S("mem_in"), 16)
            norm_act(act, chain, "mem", mem_tok)
            for m in range(KT):
                b = tile_in(act, ("xk", m))
                nc.scalar.copy(xkT[:, m, :], b[:, 0:T]).then_inc(S("tile_read"), 1)
            for j in range(2):
                for t in range(TT):
                    b = tile_in(act, ("xv", j, t))
                    nc.scalar.copy(xv[:, t, 512 * j:512 * j + 512], b[:, :]).then_inc(S("tile_read"), 1)
            phase_end(act, "act")
            norm_act(act, chain, "xa", h)
            for m in range(KT):
                b = tile_in(act, ("xq", m))
                nc.scalar.activation(xqT[:, m, :], b[:, 0:T], ACT.Copy, scale=1.0 / 16).then_inc(S("tile_read"), 1)
            phase_end(act, "act")
            attention_act(act, CROSS, units_cross())
            phase_end(act, "act")
            act.dma_start(sk_rows[:, :, :], w["peer_subkeys_2"][0].rearrange("h a k d -> k (h a) d")).then_inc(
                S("sk_in"), 16)
            phase_end(act, "act")

            norm_act(act, chain, "peer", h)
            act.wait_ge(S("sk_turned"), 1)
            for b in range(2):
                nc.scalar.copy(skT[:, 4 * b:4 * b + 4, :].rearrange("p a k -> p (a k)"), bank[b][:, :])
            for m in range(KT):
                b = tile_in(act, ("pq", m))
                nc.scalar.copy(pqT[:, m, :], b[:, 0:T]).then_inc(S("tile_read"), 1)
            phase_end(act, "act")
            nc.scalar.copy(x_hi[:, :, :], nT[:, :, :]).then_inc(S("x_hi"), 1)
            for q in range(4):
                act.wait_ge(S("peer_scores"), q + 5)
                nc.scalar.copy(sc[:, 8 * (q % 2) + q // 2:8 * (q % 2) + 8:2, :],
                               bank[4 + q][:, :].rearrange("p (a k) -> p a k", k=NKEYS))
            phase_end(act, "act")

            def down_hi(t, r, early):
                for b in range(2):
                    act.wait_ge(S(f"down_turned_{b}"), t + 1)
                    if not early:
                        act.wait_ge(S("expert_scored"), t - 1)
                    nc.scalar.copy(downT_hi[:, r % 2, 4 * b:4 * b + 4, :].rearrange("p k e -> p (k e)"),
                                   bank[4 + b][:, :]).then_inc(S(f"down_hi_{b}"), 1)

            def gelu(t, r, column):
                act.wait_ge(S("expert_scored"), t + 1)
                nc.scalar.activation(column, bank[6 + r % 2][:, 0:T],
                                     ACT.Gelu_apprx_tanh).then_inc(S("expert_gelu"), 1)

            down_hi(0, 0, True)
            for t in range(PR):
                down_hi(t + 1, t + 1, t + 1 < 2)
                gelu(t, t, gtab[:, t, :])
            with act.Fori(1, NKEYS // PR - 1) as i:
                for r in range(PR):
                    down_hi(i * PR + (r + 1), r + 1, False)
                    gelu(i * PR + r, r, gtab[:, bass.ds(i * PR + r, 1), :].rearrange("p a t -> p (a t)"))
            for t in range(NKEYS - PR, NKEYS):
                if t + 1 < NKEYS:
                    down_hi(t + 1, t + 1, False)
                gelu(t, t, gtab[:, t, :])
            phase_end(act, "act")

            act.wait_ge(S("gate_shifted"), 1)
            nc.scalar.activation(cv[:, :, :, :], cv[:, :, :, :], ACT.Exp).then_inc(S("gate_exp"), 1)
            for a in range(3):
                act.wait_ge(S("top_turned"), a + 1)
                nc.scalar.copy(idxT[:, a, :], bank[a][:, 0:T])
            phase_end(act, "act")
            with act.Fori(0, T // (4 * GROUPS)) as i:
                for q in range(GROUPS):
                    act.wait_ge(S("hot_used1"), i * GROUPS + (q + 2))
                    act.wait_ge(S("gate_scores"), i * GROUPS + (q + 1))
                    nc.scalar.copy(gates[:, q % 4, :], bank[4 + q % 4][:, :]).then_inc(S("gate_read"), 1)
            act.wait_ge(S("gate_scores"), T // 4 + 4)
            phase_end(act, "act")

            def up_parts(t, r, i, column, early):
                if not early:
                    act.wait_ge(S("up_used"), t - 1)
                nc.scalar.copy(e_hi[:, r % 2, :], column).then_inc(S("expert_hi"), 1)
                act.wait_ge(S(f"up_landed_{r}"), i * 16 + 16)
                nc.scalar.copy(u_hi[:, r % 2, :], up[r]).then_inc(S("up_hi"), 1)

            for t in range(PR):
                up_parts(t, t, 0, gtab[:, t, :], t < 2)
            with act.Fori(1, NKEYS // PR) as i:
                for r in range(PR):
                    up_parts(i * PR + r, r, i, gtab[:, bass.ds(i * PR + r, 1), :].rearrange("p a t -> p (a t)"), False)
            phase_end(act, "act")
            act.dma_start(gfin[:, :], w["norm_final_2"].partition_broadcast(P)).then_inc(S("gfin_in"), 16)
            act.wait_ge(S("h_final"), 4)
            norm_act(act, chain, "fin", h)
            for t in range(TT):
                act.wait_ge(S("fin_out"), t + 1)
                act.dma_start(out[0].rearrange("(t p) d -> p t d", p=P)[:, t, :], h[:, t, :]).then_inc(S("stored"), 16)
            act.wait_ge(S("stored"), 16 * TT)

        @block.vector
        def _(dve):
            chain = Chain(dve, S("dve_chain"))
            dve.wait_ge(S("vecs_turned"), 1)
            nc.vector.tensor_copy(vecs[:, 0:NVEC], bank[0][:, 0:NVEC])
            nc.vector.memset(dist_row[0:HEADS, 0:T], NEG).then_inc(S("table_row"), 1)
            phase_end(dve, "dve")
            dve.wait_ge(S("x_in"), 16)
            norm_dve(dve, chain, "mix", h, "g_mix")
            phase_end(dve, "dve")

            for s in range(2):
                chain(nc.vector.tensor_tensor(sq_tok[:, s, :, :], z_tok[:, s, :, :], z_tok[:, s, :, :], ALU.mult))
                nc.vector.tensor_reduce(qk_stat[:, 0, 16 * s:16 * s + 16],
                                        sq_tok[:, s, :, :].rearrange("p t (a d) -> p (t a) d", d=DH), X,
                                        ALU.add).then_inc(S("qk_squares"), 1)
            dve.wait_ge(S("qk_rms"), 1)
            chain(nc.vector.reciprocal(qk_stat[:, 2, :], qk_stat[:, 1, :]))
            for s in range(2):
                zv = z_tok[:, s, :, :].rearrange("p t (a d) -> p (t a) d", d=DH)
                nc.vector.tensor_tensor(zv, zv, spread(qk_stat[:, 2, 16 * s:16 * s + 16], DH),
                                        ALU.mult).then_inc(S("qk_normed"), 1)
            for s in range(2):
                dve.wait_ge(S("qk_turned"), s + 1)
                for m in range(4):
                    src = bank[2 * s + m // 2][:, T * (m % 2):T * (m % 2) + T]
                    nc.vector.tensor_scalar((qT, kT)[s][:, m, :], src, col(("g_q", "g_k")[s], 0),
                                            (0.125, 1.0)[s], ALU.mult, ALU.mult)
            phase_end(dve, "dve")
            attention_dve(dve, ATT1, units_block1())
            phase_end(dve, "dve")
            chain(nc.vector.memset(cin[:, :, 0:2], 0.0))
            chain(nc.vector.tensor_tensor(cin[:, :, 2:T + 2], convT[:, 8:12, :], convT[:, 0:4, :], ALU.mult))
            for m in range(4):
                y = mixT[:, 4 + m, :]
                chain(nc.vector.tensor_scalar(y, cin[:, m, 0:T], col("conv_w", m), col("conv_b", m), ALU.mult, ALU.add))
                for j in (1, 2):
                    chain(nc.vector.scalar_tensor_tensor(out=y, in0=cin[:, m, j:j + T], scalar=col("conv_w", 4 * j + m),
                                                         in1=y, op0=ALU.mult, op1=ALU.add))
                nc.vector.tensor_tensor(y, y, convT[:, 4 + m, :], ALU.mult).then_inc(S("conv_done"), 1)
            for m in range(KT):
                b = tile_in(dve, ("mix", m))
                chain(nc.vector.tensor_tensor(mT[:, m, :], sigT[:, m, :], b[:, 0:T], ALU.mult))
                chain(nc.vector.tensor_tensor(sigT[:, 8 + m, :], sigT[:, 8 + m, :], b[:, T:2 * T], ALU.mult))
                nc.vector.tensor_tensor(mT[:, m, :], mT[:, m, :], sigT[:, 8 + m, :], ALU.add).then_inc(S("mT_ready"), 1)
                dve.wait_ge(S("mT_ready"), m + 1)
                dve.sem_inc(S("tile_read"), 1)
            residual_dve(dve, "wo")
            phase_end(dve, "dve")

            norm_dve(dve, chain, "ffn", h, "g_ffn")
            dve.wait_ge(S("logits"), 1)
            chain(nc.vector.memset(route[:, :, 4:8], NEG))
            chain(nc.vector.tensor_copy(route[:, :, 0:4], logit[:, :, 0:4]))
            for t in range(TT):
                chain(nc.vector.max(top8[:, t, 0:8], route[:, t, 0:8]))
                chain(nc.vector.max_index(idx8[:, t, 0:8], top8[:, t, 0:8], route[:, t, 0:8]))
            chain(nc.vector.tensor_copy(idx8f[:, :, 0:8], idx8[:, :, 0:8]))
            for t in range(TT):
                r = route[:, t, :]
                chain(nc.vector.tensor_scalar(r[:, 12:16], r[:, 0:4], top8[:, t, 0:1], None, ALU.subtract))
                chain(nc.vector.tensor_scalar(r[:, 8:12], iota[:, 0:4], idx8f[:, t, 0:1], None, ALU.is_equal))
                chain(nc.vector.tensor_scalar(r[:, 20:24], r[:, 8:12], -1.0, -NEG, ALU.add, ALU.mult))
                chain(nc.vector.tensor_tensor(r[:, 24:56].rearrange("p (g e) -> p g e", g=GROUPS),
                                              logit[:, t, 4:36].rearrange("p (g e) -> p g e", g=GROUPS),
                                              spread(r[:, 20:24], PER_GROUP), ALU.add))
                chain(nc.vector.max(top8[:, t, 8:16], r[:, 24:56]))
                chain(nc.vector.max_index(idx8[:, t, 8:16], top8[:, t, 8:16], r[:, 24:56]))
                chain(nc.vector.tensor_tensor(r[:, 18:19], top8[:, t, 9:10], top8[:, t, 8:9], ALU.subtract))
            chain(nc.vector.tensor_copy(idx8f[:, :, 8:16], idx8[:, :, 8:16]))
            dve.sem_inc(S("group_shifted"), 1)
            dve.sem_inc(S("second_gap"), 1)
            dve.wait_ge(S("group_exp"), TT)
            dve.wait_ge(S("second_exp"), 1)
            for t in range(TT):
                r = route[:, t, :]
                chain(nc.vector.reciprocal(r[:, 17:18], r[:, 16:17]))
                chain(nc.vector.tensor_scalar(r[:, 19:20], r[:, 18:19], 1.0, None, ALU.add))
                chain(nc.vector.reciprocal(r[:, 19:20], r[:, 19:20]))
                chain(nc.vector.tensor_tensor(r[:, 56:57], r[:, 19:20], r[:, 17:18], ALU.mult))
                chain(nc.vector.tensor_tensor(r[:, 57:58], r[:, 56:57], r[:, 18:19], ALU.mult))
                chain(nc.vector.tensor_scalar(gatew[:, t, :], iota[:, 0:EXPERTS], idx8f[:, t, 8:9], r[:, 56:57],
                                              ALU.is_equal, ALU.mult))
                chain(nc.vector.tensor_scalar(r[:, 24:56], iota[:, 0:EXPERTS], idx8f[:, t, 9:10], r[:, 57:58],
                                              ALU.is_equal, ALU.mult))
                chain(nc.vector.tensor_tensor(gatew[:, t, :], gatew[:, t, :], r[:, 24:56], ALU.add))
                chain(nc.vector.tensor_scalar(picked[:, t, :], iota[:, 0:EXPERTS], idx8f[:, t, 8:9], None, ALU.is_equal))
                chain(nc.vector.scalar_tensor_tensor(out=picked[:, t, :], in0=iota[:, 0:EXPERTS],
                                                     scalar=idx8f[:, t, 9:10], in1=picked[:, t, :],
                                                     op0=ALU.is_equal, op1=ALU.add))
            dve.sem_inc(S("picked_ready"), 1)
            dve.wait_ge(S("gain_in"), 16)
            for t in range(TT):
                nc.vector.tensor_tensor(xn[:, t, :], xn[:, t, :], gain_row[:, :], ALU.mult)
            nc.vector.memset(out_r[:, :], 0.0)
            nc.vector.memset(pickT[:, :, :], 0.0)
            nc.vector.memset(place[:, :, EXPERTS:EXPERTS + 2], -1.0)
            dve.wait_ge(S("rows_counted"), 1)
            for t in range(TT):
                pl = place[:, t, 0:EXPERTS]
                chain(nc.vector.scalar_tensor_tensor(out=pl, in0=bank[0][:, 64 * t:64 * t + EXPERTS], scalar=1.0,
                                                     in1=picked[:, t, :], op0=ALU.add, op1=ALU.mult))
                chain(nc.vector.tensor_scalar(pl, pl, -1.0, None, ALU.add))
            chain(nc.vector.tensor_reduce(fullest[:, :], bank[0][:, 128:128 + EXPERTS], X, ALU.max))
            chain(nc.vector.tensor_scalar(overfull[:, :], fullest[:, :], float(P), None, ALU.is_gt))

            def one_hot(buf, column):
                for t in range(TT):
                    ins = nc.vector.tensor_scalar(pick[:, buf, t, :], iota[:, :], place[:, t, column], None,
                                                  ALU.is_equal)
                ins.then_inc(S("pick_ready"), 1)

            for name in ("hid_ready", "hid_rT_ready", "hid_turned", "out_a", "out_b", "turned_pick"):
                dve.sem_inc(S(name), 1)
            one_hot(0, slice(0, 1))
            one_hot(1, slice(1, 2))
            dve.sem_inc(S("moe_hidden"), FT)
            dve.sem_inc(S("moe_added"), 4)
            phase_end(dve, "dve")
            over = dve.value_load(overfull[0:1, 0:1], min_val=0, max_val=1)

            def add_rows(i, j):
                for c in range(4):
                    dve.wait_ge(S("scattered"), i * 8 + (4 * j + c + 1))
                    hs = h[:, c // 2, 512 * (c % 2):512 * (c % 2) + 512]
                    nc.vector.tensor_tensor(hs, hs, bank[6 + c % 2][:, :], ALU.add).then_inc(S("row_added"), 1)

            with dve.If(over < 1):
                dve.wait_ge(S("gathered"), 1)
                nc.vector.tensor_copy(gathT[:, 4:8, :].rearrange("p k s -> p (k s)"), bank[1][:, :]).then_inc(
                    S("gathT_b"), 1)
                with dve.Fori(0, EXPERTS // 2) as i:
                    for j in range(2):
                        dve.wait_ge(S("silu_ready"), i * 2 + (j + 1))
                        dve.wait_ge(S("hid_turned"), i * 2 + (j + 1))
                        nc.vector.tensor_tensor(hid_r[:, :], silu_r[:, :], bank[3][:, :], ALU.mult).then_inc(
                            S("hid_ready"), 1)
                        dve.wait_ge(S("gathered"), i * 2 + (j + 2))
                        nc.vector.tensor_copy(gathT[:, 4:8, :].rearrange("p k s -> p (k s)"), bank[1][:, :]).then_inc(
                            S("gathT_b"), 1)
                        add_rows(i, j)
                        dve.wait_ge(S("pick_turned"), i * 2 + (j + 1))
                        one_hot(j, bass.ds(i * 2 + (j + 2), 1))
                        dve.wait_ge(S("w2_used"), i * 2 + (j + 1))
                        dve.wait_ge(S("turned_pick"), i * 2 + (j + 2))
                        nc.vector.tensor_scalar(out_r[:, 512:D], bank[7][:, :], row_w[:, 0:1], None,
                                                ALU.mult).then_inc(S("out_b"), 1)
                add_rows(EXPERTS // 2, 0)
            with dve.Else():
                with dve.Fori(0, EXPERTS // 2) as i:
                    for j in range(2):
                        for f in range(FT):
                            dve.wait_ge(S("moe_silu"), i * (2 * FT) + (FT * j + f + 1))
                            dve.wait_ge(S("moe_added"), i * 8 + (4 * j + 4))
                            nc.vector.tensor_tensor(hidT[:, f, :], silu_h[:, f, :], bank[f][:, T:2 * T],
                                                    ALU.mult).then_inc(S("moe_hidden"), 1)
                        for c in range(4):
                            t, half = c // 2, c % 2
                            dve.wait_ge(S("moe_out"), i * 8 + (4 * j + c + 1))
                            hs = h[:, t, 512 * half:512 * half + 512]
                            nc.vector.scalar_tensor_tensor(out=hs, in0=bank[4 + c][:, :],
                                                           scalar=gatew[:, t, bass.ds(i * 2 + j, 1)], in1=hs,
                                                           op0=ALU.mult, op1=ALU.add).then_inc(S("moe_added"), 1)
            phase_end(dve, "dve")

            norm_dve(dve, chain, "ple", h, "g_ple")
            dve.wait_ge(S("gate_ready"), 1)
            for j in range(2):
                for t in range(TT):
                    b = tile_in(dve, ("ple", j, t))
                    g = gate_t[:, t, 512 * j:512 * j + 512]
                    hs = h[:, t, 512 * j:512 * j + 512]
                    nc.vector.tensor_tensor(g, g, b[:, :], ALU.mult).then_inc(S("tile_read"), 1)
                    dve.wait_ge(S("tile_read"), tile_no[("ple", j, t)] + 1)
                    nc.vector.tensor_tensor(hs, hs, g, ALU.add)
            phase_end(dve, "dve")

            norm_dve(dve, chain, "mix2", h, "norm_mix_2")
            dve.wait_ge(S("log_part"), 1)
            chain(nc.vector.tensor_scalar(loga[:, :, :], loga[:, :, :], 0.0, None, ALU.min))
            chain(nc.vector.tensor_tensor(loga[:, :, :], loga[:, :, :], k_dec[:, 0, :, :], ALU.subtract))
            chain(nc.vector.tensor_scalar(loga[:, :, :], loga[:, :, :], 0.5 / 16.0, None, ALU.mult))
            for c in range(2):
                nc.vector.tensor_tensor_scan(bcum[:, c, :], loga[:, c, :], loga[:, c, :], 0.0, ALU.add, ALU.add)
            cg = nsa_gate[:, 0, :].rearrange("p (a b) -> p a b", b=3)[:, :, 0]
            nc.vector.tensor_scalar(cg, cg, late_row[:, 0:1], None, ALU.mult)
            phase_end(dve, "dve")

            dve.wait_ge(S("dup_done"), 2)
            dve.wait_ge(S("pos_ready"), 1)
            for s in range(2):
                for g in range(2):
                    for half in range(2):
                        rows = slice(DH * half, DH * half + DH)
                        kv = bank[s][rows, T * g:T * g + T].rearrange("p (n a) -> p a n", a=CMP_STRIDE)
                        for far in range(2):
                            ins = nc.vector.tensor_tensor(
                                cmp_in[rows, s, 8 * far:8 * far + 8, g, :], kv[:, half::2, far:far + N_CMP],
                                spread(posT[rows, s, 8 * far:8 * far + 8], N_CMP), ALU.add)
                ins.then_inc(S("cmp_in_ready"), 1)
            phase_end(dve, "dve")

            for c in range(2):
                chain(nc.vector.tensor_copy(q_dec[:, c, 0:SUB], bcum[:, c, 0:SUB]))
                nc.vector.tensor_tensor(q_dec[:, c, SUB:T].rearrange("p (u t) -> p u t", t=SUB),
                                        bcum[:, c, SUB:T].rearrange("p (u t) -> p u t", t=SUB),
                                        spread(bcum[:, c, SUB - 1:T - SUB:SUB], SUB), ALU.subtract).then_inc(
                    S("q_diff"), 1)
            for c in range(2):
                dve.wait_ge(S("q_exp"), c + 1)
                nc.vector.tensor_tensor(q_dec[:, c, :], q_dec[:, c, :], gqkT[:, c, :], ALU.mult).then_inc(
                    S("q_dec_ready"), 1)

            def k_diff(u):
                for c in range(2):
                    if u >= 2:
                        dve.wait_ge(S("k_dec_used"), 2 * (u - 2) + c + 1)
                    before = bcum[:, c, SUB * u - 1:SUB * u] if u else 0.0
                    nc.vector.tensor_scalar(k_dec[:, u % 2, c, :], bcum[:, c, :], before, 0.0, ALU.subtract,
                                            ALU.max).then_inc(S("k_diff"), 1)

            k_diff(0)
            for u in range(NSUB):
                if u + 1 < NSUB:
                    k_diff(u + 1)
                for c in range(2):
                    dve.wait_ge(S("k_exp"), 2 * u + c + 1)
                    nc.vector.tensor_tensor(k_dec[:, u % 2, c, :], k_dec[:, u % 2, c, :], gqkT[:, 2 + c, :],
                                            ALU.mult).then_inc(S("k_dec_ready"), 1)
            for c in range(2):
                if c:
                    dve.wait_ge(S("diag_used"), c)
                bt = bcum[:, c, :].rearrange("p (u t) -> p u t", t=SUB)
                kt_ = gqkT[:, 2 + c, :].rearrange("p (u t) -> p u t", t=SUB)
                flat = diag[:, :, :, :].rearrange("p u t j -> p (u t) j")

                def by_key(v):
                    return v.unsqueeze(2).to_broadcast([P, NSUB, SUB, SUB])

                chain(nc.vector.tensor_copy(diag[:, :, :, :], by_key(bt)))
                chain(nc.vector.tensor_tensor(flat, spread(bcum[:, c, :], SUB), flat, ALU.subtract))
                nc.vector.tensor_scalar(flat, flat, 0.0, None, ALU.min).then_inc(S("diag_diff"), 1)
                dve.wait_ge(S("diag_exp"), c + 1)
                chain(nc.vector.tensor_tensor(flat, flat, spread(gqkT[:, c, :], SUB), ALU.mult))
                nc.vector.tensor_tensor(diag[:, :, :, :], diag[:, :, :, :], by_key(kt_), ALU.mult).then_inc(
                    S("diag_ready"), 1)
            dve.wait_ge(S("diag_used"), 2)
            dve.wait_ge(S("k_dec_used"), 2 * NSUB)
            for hh in range(GLA_HEADS):
                far, near = bank[hh], bank[4 + hh]
                tmp = k_dec[:, 0, 0, 0:P]
                nc.vector.tensor_copy(gla_a[:, hh, 0, P:T], far[:, P:T])
                for t in range(TT):
                    a = gla_a[:, hh, t, P * t:P * t + P]
                    chain(nc.vector.tensor_tensor(a, far[:, T * t + P * t:T * t + P * t + P], mask_prev[:, :], ALU.mult))
                    chain(nc.vector.tensor_tensor(tmp, near[:, P * t:P * t + P], mask_same[:, :], ALU.mult))
                    chain(nc.vector.tensor_tensor(a, a, tmp, ALU.add))
            dve.sem_inc(S("gla_a_ready"), 1)
            dve.wait_ge(S("o_gla_ready"), TT)
            og = o_gla[:, :, :].rearrange("p t (a d) -> p (t a) d", d=P)
            sq = scratch(0, TT * GLA_HEADS, P)
            chain(nc.vector.tensor_tensor(sq, og, og, ALU.mult))
            nc.vector.tensor_reduce(gla_stat[:, 0, :], sq, X, ALU.add).then_inc(S("gla_squares"), 1)
            dve.wait_ge(S("gla_rms"), 1)
            chain(nc.vector.reciprocal(gla_stat[:, 2, :], gla_stat[:, 1, :]))
            chain(nc.vector.tensor_tensor(og, og, spread(gla_stat[:, 2, :], P), ALU.mult))
            nc.vector.tensor_tensor(o_gla[:, :, :], o_gla[:, :, :], gr[:, :, :], ALU.mult).then_inc(S("gla_normed"), 1)
            dve.wait_ge(S("gla_turned"), 1)
            for hh in range(GLA_HEADS):
                nc.vector.tensor_scalar(catT[:, hh, :], bank[2 + hh // 2][:, T * (hh % 2):T * (hh % 2) + T],
                                        col("gla_out_norm_2", 0), None, ALU.mult)
            phase_end(dve, "dve")
            attention_dve(dve, NSA, units_nsa())
            phase_end(dve, "dve")
            residual_dve(dve, "wout")
            phase_end(dve, "dve")
            dve.wait_ge(S("mem_in"), 16)
            norm_dve(dve, chain, "mem", mem_tok, "norm_mem_2")
            phase_end(dve, "dve")
            norm_dve(dve, chain, "xa", h, "norm_xattn_2")
            phase_end(dve, "dve")
            attention_dve(dve, CROSS, units_cross())
            phase_end(dve, "dve")
            residual_dve(dve, "xo")
            phase_end(dve, "dve")
            norm_dve(dve, chain, "peer", h, "norm_ffn_2")
            phase_end(dve, "dve")
            dve.wait_ge(S("x_hi"), 1)
            nc.vector.tensor_tensor(x_lo[:, :, :], nT[:, :, :], x_hi[:, :, :].bitcast(F32), ALU.subtract).then_inc(
                S("x_lo"), 1)
            phase_end(dve, "dve")

            def best16(scores, values, places):
                chain(nc.vector.max(values[:, 0:8], scores))
                chain(nc.vector.max_index(places[:, 0:8], values[:, 0:8], scores))
                chain(nc.vector.match_replace(scores, values[:, 0:8], scores, -3.0e38))
                chain(nc.vector.max(values[:, 8:16], scores))
                chain(nc.vector.max_index(places[:, 8:16], values[:, 8:16], scores))

            def best_keys(n):
                t, hp = n // 16, n % 16
                q, x = 2 * (hp % 2) + hp // 8, hp // 2 % 4
                scores = sc[:, hp, :] if t else bank[q][:, NKEYS * x:NKEYS * x + NKEYS]
                best16(scores, tv[:, t, hp, :], ti[:, t, hp, :])

            def best_sums(n):
                t, hh = n // PH, n % PH
                if n == 0:
                    chain(nc.vector.tensor_copy(tif[:, :, :, :], ti))
                chain(nc.vector.tensor_tensor(
                    cand[:, t, hh, :, :], spread(tv[:, t, 2 * hh, :], TOPK),
                    tv[:, t, 2 * hh + 1, :].unsqueeze(1).to_broadcast([P, TOPK, TOPK]), ALU.add))
                best16(cand[:, t, hh, :, :].rearrange("p a b -> p (a b)"), cv[:, t, hh, :], ci[:, t, hh, :])

            def key_indices(n):
                t, a, g = n // 8, n // 4 % 2, n % 4
                if n == 0:
                    cif = ci.rearrange("p t a k -> p t (a k)")
                    nc.vector.tensor_scalar(cab[:, 0, :, :], cif, 4, None, ALU.logical_shift_right)
                    chain(nc.vector.tensor_scalar(cab[:, 1, :, :], cif, TOPK - 1, None, ALU.bitwise_and))
                    chain(nc.vector.tensor_copy(cabf[:, :, :, :], cab))
                part_of = slice(2 * TOPK * g, 2 * TOPK * g + 2 * TOPK)
                e = eq[:, n % 2, :, :, :].rearrange("p h k j -> p (h k) j")
                chain(nc.vector.tensor_tensor(e, spread(cabf[:, a, t, part_of], TOPK),
                                              iota16.unsqueeze(1).to_broadcast([P, 2 * TOPK, TOPK]), ALU.is_equal))
                for x in range(2):
                    hh = 2 * g + x
                    ex = e[:, TOPK * x:TOPK * x + TOPK, :]
                    chain(nc.vector.tensor_tensor(
                        ex, ex, tif[:, t, 2 * hh + a, :].unsqueeze(1).to_broadcast([P, TOPK, TOPK]), ALU.mult))
                chain(nc.vector.tensor_reduce(fin3[:, a, t, part_of], e, X, ALU.add))

            pieces = [(best_keys, n) for n in range(TT * 16)] + [(best_sums, n) for n in range(TT * PH)] + \
                [(key_indices, n) for n in range(16)]
            assert len(pieces) == NKEYS // 2

            def down_lo(t, r, early):
                for b in range(2):
                    dve.wait_ge(S(f"down_hi_{b}"), t + 1)
                    if not early:
                        dve.wait_ge(S("expert_scored"), t - 1)
                    part = slice(4 * b, 4 * b + 4)
                    nc.vector.tensor_tensor(downT_lo[:, r % 2, part, :].rearrange("p k e -> p (k e)"), bank[4 + b][:, :],
                                            downT_hi[:, r % 2, part, :].bitcast(F32).rearrange("p k e -> p (k e)"),
                                            ALU.subtract).then_inc(S(f"down_lo_{b}"), 1)

            for t, (work, n) in enumerate(pieces):
                down_lo(t, t % PR, t < 2)
                work(n)
            with dve.Fori(NKEYS // 2 // PR, NKEYS // PR) as i:
                for r in range(PR):
                    down_lo(i * PR + r, r, False)
            chain(nc.vector.tensor_copy(psum16[:, 1, :], cv[:, :, :, 0].rearrange("p t a -> p (t a)")))
            cvf = cv[:, :, :, :].rearrange("p t a k -> p (t a) k")
            nc.vector.tensor_tensor(cvf, cvf, spread(psum16[:, 1, :], TOPK), ALU.subtract).then_inc(S("gate_shifted"), 1)
            phase_end(dve, "dve")
            dve.wait_ge(S("gate_exp"), 1)
            chain(nc.vector.tensor_reduce(psum16[:, 0, :], cvf, X, ALU.add))
            chain(nc.vector.reciprocal(psum16[:, 1, :], psum16[:, 0, :]))
            nc.vector.tensor_tensor(fin3[:, 2, :, :].rearrange("p t (a k) -> p (t a) k", k=TOPK), cvf,
                                    spread(psum16[:, 1, :], TOPK), ALU.mult).then_inc(S("peer_top"), 1)
            dve.sem_inc(S("gate_read"), 4)
            dve.sem_inc(S("gate_scores"), 4)
            dve.sem_inc(S("hot_used0"), 1)
            dve.sem_inc(S("hot_used1"), 1)
            phase_end(dve, "dve")

            with dve.Fori(0, T // (4 * GROUPS)) as i:
                for q in range(GROUPS):
                    for pair in range(2):
                        dve.wait_ge(S(f"hot_used{pair}"), i * GROUPS + (q + 1))
                        toks = bass.ds(i * (4 * GROUPS) + (4 * q + 2 * pair), 2)
                        nc.vector.tensor_tensor(hot[:, pair, :, 0, :], iota[:, :].unsqueeze(1).to_broadcast([P, 2, P]),
                                                spread(idxT[:, 0, toks], P), ALU.is_equal)
                        for x in range(2):
                            tok = bass.ds(i * (4 * GROUPS) + (4 * q + 2 * pair + x), 1)
                            ins = nc.vector.tensor_scalar(hot[:, pair, x, 1, :], iota[:, :], idxT[:, 1, tok],
                                                          idxT[:, 2, tok], ALU.is_equal, ALU.mult)
                        ins.then_inc(S("hot_ready"), 1)
            phase_end(dve, "dve")

            def lower_parts(t, r, column):
                dve.wait_ge(S("expert_hi"), t + 1)
                nc.vector.tensor_tensor(e_lo[:, r % 2, :], column, e_hi[:, r % 2, :].bitcast(F32),
                                        ALU.subtract).then_inc(S("expert_lo"), 1)
                dve.wait_ge(S("up_hi"), t + 1)
                nc.vector.tensor_tensor(u_lo[:, r % 2, :], up[r], u_hi[:, r % 2, :].bitcast(F32),
                                        ALU.subtract).then_inc(S("up_lo"), 1)

            with dve.Fori(0, NKEYS // PR) as i:
                for r in range(PR):
                    lower_parts(i * PR + r, r, gtab[:, bass.ds(i * PR + r, 1), :].rearrange("p a t -> p (a t)"))
            phase_end(dve, "dve")
            for c in range(4):
                hs = h[:, c // 2, 512 * (c % 2):512 * (c % 2) + 512]
                nc.vector.tensor_tensor(hs, hs, bank[c][:, :], ALU.add).then_inc(S("h_final"), 1)
            dve.wait_ge(S("norm_rms"), len(NORMS))
            dve.wait_ge(S("h_final"), 4)
            dve.wait_ge(S("gfin_in"), 16)
            chain(nc.vector.reciprocal(stat[:, 2, :], stat[:, 1, :]))
            for t in range(TT):
                nc.vector.scalar_tensor_tensor(out=h[:, t, :], in0=h[:, t, :], scalar=stat[:, 2, t:t + 1],
                                               in1=gfin, op0=ALU.mult, op1=ALU.mult).then_inc(S("fin_out"), 1)

        @block.gpsimd
        def _(pool):
            chain = Chain(pool, S("pool_chain"))
            nc.gpsimd.memset(eps[:, :], EPS)
            nc.gpsimd.memset(sel_dup[:, :, :], 0.0)
            nc.gpsimd.memset(modmask[:, :], 0.0)
            nc.gpsimd.memset(ident[:, :], 0.0)
            nc.gpsimd.memset(mirror[:, :], 0.0)
            chain(nc.gpsimd.memset(ones[:, :], 1.0))
            nc.gpsimd.iota(iota[:, :], pattern=[[1, P]], base=0, channel_multiplier=0,
                           allow_small_or_imprecise_dtypes=True)
            nc.gpsimd.affine_select(out=ident[:, :], in_=ident[:, :], compare_op=ALU.not_equal, fill=1.0, base=0,
                                    pattern=[[-1, P]], channel_multiplier=1)
            nc.gpsimd.affine_select(out=mirror[:, :], in_=mirror[:, :], compare_op=ALU.not_equal, fill=1.0, base=1 - P,
                                    pattern=[[1, P]], channel_multiplier=1)
            nc.gpsimd.memset(modmask[:, SUB - 1::SUB], 1.0)
            for g in range(2):
                d = sel_dup[:, g, :].rearrange("p (a b) -> p a b", a=2)
                nc.gpsimd.affine_select(out=d, in_=d, compare_op=ALU.not_equal, fill=1.0, base=-DH * g,
                                        pattern=[[0, 2], [-1, DH]], channel_multiplier=1)
            nc.gpsimd.affine_select(out=mask_prev[:, :].rearrange("p (u t) -> p u t", t=SUB),
                                    in_=ones[:, :].rearrange("p (u t) -> p u t", t=SUB), compare_op=ALU.is_gt, fill=0.0,
                                    base=0, pattern=[[SUB, P // SUB], [0, SUB]], channel_multiplier=-1)
            nc.gpsimd.affine_select(out=earlier[:, :], in_=ones[:, :], compare_op=ALU.is_gt, fill=0.0, base=0,
                                    pattern=[[1, P]], channel_multiplier=-1)
            chain(nc.gpsimd.affine_select(out=mask_same[:, :], in_=ones[:, :], compare_op=ALU.is_ge, fill=0.0, base=0,
                                          pattern=[[1, P]], channel_multiplier=-1))
            nc.gpsimd.tensor_tensor(mask_same[:, :], mask_same[:, :], mask_prev[:, :], ALU.subtract)
            chain(nc.gpsimd.affine_select(out=late_row[:, :], in_=ones[:, 0:1], compare_op=ALU.is_ge, fill=0.0,
                                          base=-(CMP_BLOCK - 1), pattern=[[0, 1]], channel_multiplier=1))
            nc.gpsimd.memset(bias1[0:64, :, 0:64], NEG)
            pool.drain().then_inc(S("consts"), 1)
            pool.wait_ge(S("phase"), 3 * phases["indices turned"])
            with pool.Fori(0, T // (4 * GROUPS)) as i:
                for q in range(GROUPS):
                    pool.wait_ge(S("gate_read"), i * GROUPS + (q + 5))
                    view = gtab[:, :, bass.ds(i * (4 * GROUPS) + 4 * q, 4)].rearrange("p i t -> p t i")
                    nc.gpsimd.tensor_tensor(view, view, gates[:, q % 4, :].rearrange("p (t i) -> p t i", t=4),
                                            ALU.mult).then_inc(S("gate_scores"), 1)

        @block.sync
        def _(sp):
            def load(n, pieces):
                if n >= RING:
                    m = n - RING
                    if m in spent_at:
                        sp.wait_ge(S("tile_done"), spent_at[m])
                    else:
                        e, kind = (m - MOE_AT) // 3, (m - MOE_AT) % 3
                        sp.wait_ge(S("w2_used" if kind == 2 else "w13_used"), e + 1)
                for at, src in pieces:
                    kt, width = src.shape[1], src.shape[2]
                    dst = slot[n % RING][:, at:at + kt * width].rearrange("p (k n) -> p k n", n=width)
                    sp.dma_start(dst, src).then_inc(landed[n % RING], 16)

            for n, pieces in enumerate(first):
                load(n, pieces)
            tabs = [w["w1"][0].rearrange("e (k p) n -> e p k n", p=P), w["w3"][0].rearrange("e (k p) n -> e p k n", p=P),
                    w["w2"][0].rearrange("e (k p) n -> e p k n", p=P)]
            for j in range(6):
                load(MOE_AT + j, [(0, tabs[j % 3][j // 3])])
            with sp.Fori(1, EXPERTS // 2) as i:
                for j in range(6):
                    sp.wait_ge(S("w2_used" if j % 3 == 2 else "w13_used"), i * 2 + (j // 3 - 1))
                    src = tabs[j % 3][bass.ds(i * 2 + j // 3, 1)].rearrange("e p k n -> p (e k) n")
                    dst = slot[(MOE_AT + j) % RING].rearrange("p (k n) -> p k n", n=src.shape[2])
                    sp.dma_start(dst, src).then_inc(landed[(MOE_AT + j) % RING], 16)
            for m, pieces in enumerate(later):
                load(LATE_AT + m, pieces)
            dn = w["peer_down_2"][0].rearrange("(i p) d -> i p d", p=P)
            upt = w["peer_up_2"][0].rearrange("(i p) d -> i p d", p=P)
            sp.wait_ge(S("phase"), 3 * phases["rings free"])
            for r in range(PR):
                sp.dma_start(down[r], dn[r]).then_inc(S(f"down_landed_{r}"), 16)
            with sp.Fori(1, NKEYS // PR) as i:
                for r in range(PR):
                    e = bass.ds(i * PR + r, 1)
                    sp.wait_ge(S("down_turned_1"), i * PR + (r - PR + 1))
                    sp.dma_start(down[r], dn[e].rearrange("a p d -> p (a d)")).then_inc(S(f"down_landed_{r}"), 16)
            sp.wait_ge(S("phase"), 3 * phases["scores done"])
            for r in range(PR):
                sp.dma_start(up[r], upt[r]).then_inc(S(f"up_landed_{r}"), 16)
            with sp.Fori(1, NKEYS // PR) as i:
                for r in range(PR):
                    e = bass.ds(i * PR + r, 1)
                    sp.wait_ge(S("up_lo"), i * PR + (r - PR + 1))
                    sp.dma_start(up[r], upt[e].rearrange("a p d -> p (a d)")).then_inc(S(f"up_landed_{r}"), 16)

        assert phases["pe"] == phases["act"] == phases["dve"], phases


_INS = ['x', 'p', 'g_mix', 'w_in', 'b_in', 'g_q', 'g_k', 'rel_bias', 'conv_w', 'conv_b', 'w_pa', 'w_pc', 'w_o',
        'g_ffn', 'w_group', 'b_group', 'w_router', 'b_router', 'w1', 'w3', 'w2', 'g_ple', 'w_ple_gate',
        'b_ple_gate', 'w_ple_proj', 'mem_2', 'rel_bias_2', 'norm_mix_2', 'w_in_2', 'gla_gate_w2_2',
        'gla_gate_b_2', 'gla_out_norm_2', 'cmp_pos_k_2', 'cmp_pos_v_2', 'cmp_k_w1_2', 'cmp_k_w2_2',
        'cmp_v_w1_2', 'cmp_v_w2_2', 'w_out_2', 'norm_xattn_2', 'norm_mem_2', 'xa_wq_2', 'xa_wk_2',
        'xa_wv_2', 'xa_wo_2', 'norm_ffn_2', 'peer_wq_2', 'peer_subkeys_2', 'peer_down_2', 'peer_up_2',
        'norm_final_2']


def kernel(**inputs):
    import concourse.bacc as _bacc
    from concourse.bass_utils import run_bass_kernel_spmd as _run

    nc = _bacc.Bacc("TRN2", target_bir_lowering=False, num_devices=1)
    arrays, args = {}, {}
    for name in _INS:
        a = np.ascontiguousarray(inputs[name])
        arrays[f"in_{name}_dram"] = a
        args[name] = nc.dram_tensor(f"in_{name}_dram", a.shape, mybir.dt.from_np(a.dtype), kind="ExternalInput").ap()
    buckets = nc.inline_tensor(distance_buckets(), "distance_buckets").ap()
    out = nc.dram_tensor("out_0_dram", (1, T, D), F32, kind="ExternalOutput").ap()
    build(nc, args, buckets, out)
    r = _run(nc, [arrays], core_ids=[0])
    return r.results[0]["out_0_dram"]
```

```python
from contextlib import ExitStack

import numpy as np
import concourse.bass as bass
from concourse import mybir

F32 = mybir.dt.float32
F32R = mybir.dt.float32r
U32 = mybir.dt.uint32
ALU = mybir.AluOpType
ACT = mybir.ActivationFunctionType
X = mybir.AxisListType.X

P = 128
T = 256
TT = T // P
D = 1024
KT = D // P
NEG = -1e30
EPS = 1e-6
HEADS = 8
DH = 64
REL = 320
EXPERTS = 32
GROUPS = 4
PER_GROUP = EXPERTS // GROUPS
FF = 512
FT = FF // P
BUCKETS = 32
TAB = 512
N_CMP = 15
CMP_STRIDE = 16
CMP_BLOCK = 32
SUB = 16
NSUB = T // SUB
GLA_HEADS = 4
XHEADS = 4
PH = 8
DEPTH = 3
GROUPS = 8
TOPK = 16
NKEYS = 128

RING = 6
SLOT = KT * 512

ROWS = [("g_mix", 8), ("b_in", 40), ("conv_w", 12), ("conv_b", 4), ("g_ffn", 8), ("g_ple", 8),
        ("norm_mix_2", 8), ("gla_gate_b_2", 2), ("norm_xattn_2", 8), ("norm_mem_2", 8),
        ("norm_ffn_2", 8), ("gla_out_norm_2", 1)]
COL = {}
NVEC = 0
for _name, _rows in ROWS:
    COL[_name] = NVEC
    NVEC += _rows
COL["g_q"], COL["g_k"] = NVEC, NVEC + 1
NVEC += 2
assert NVEC <= P


def distance_buckets():
    n = np.arange(T)
    far = 16 + np.floor(np.log(np.maximum(n, 1) / 16.0) / np.log(128.0) * 16).astype(np.int64)
    bucket = np.where(n < 16, n, np.minimum(far, BUCKETS - 1))
    return (np.arange(BUCKETS)[:, None] == bucket[None, :]).astype(np.float32)


NVROWS = len(ROWS) + 4
NLATE = 6


class Chain:

    def __init__(self, eng, sem):
        self.eng, self.sem, self.n = eng, sem, 0

    def __call__(self, ins):
        ins.then_inc(self.sem, 1)
        self.n += 1
        self.eng.wait_ge(self.sem, self.n)


def weight_slots(w):
    def cols(name, a, b):
        return w[name][0].rearrange("(k p) n -> p k n", p=P)[:, :, a:b]

    def pairs(name):
        return [[(0, cols(name, 512 * j, 512 * j + 512))] for j in range(2)]

    first = [[(0, cols("w_in", 512 * j, 512 * j + 512))] for j in range(10)]
    first += [[(0, cols("w_pa", 512 * j, 512 * j + 512)), (SLOT // 2, cols("w_pc", 512 * j, 512 * j + 512))]
              for j in range(2)]
    first += pairs("w_o")
    later = pairs("w_ple_gate") + [[(0, cols("w_ple_proj", 0, D))]]
    later += [[(0, cols("w_in_2", a, b))] for a, b in
              ((2064, 2448), (2448, 2856), (0, 512), (512, 1024), (1024, 1536), (1552, 2064))]
    for name in ("w_out_2", "xa_wk_2", "xa_wv_2", "xa_wq_2", "xa_wo_2", "peer_wq_2"):
        later += pairs(name)
    return first, later


def build(nc, w, buckets, out):
    with ExitStack() as ctx:
        def sb(name, shape, dt=F32):
            return ctx.enter_context(nc.sbuf_tensor(name, shape, dt))

        sems = {}

        def S(name):
            if name not in sems:
                sems[name] = ctx.enter_context(nc.semaphore(name))
            return sems[name]

        bank = [ctx.enter_context(nc.psum_tensor(f"bank{i}", [P, 512], F32)) for i in range(8)]
        table_dram = nc.dram_tensor("distance_table", [HEADS, TAB], F32, kind="Internal")

        ident = sb("ident", [P, P])
        mirror = sb("mirror", [P, P])
        ones = sb("ones", [P, P])
        iota = sb("iota", [P, P])
        vecs = sb("vecs", [P, P])
        eps = sb("eps", [P, 1])
        late_row = sb("late_row", [P, 1])
        h = sb("h", [P, TT, D])
        nT = sb("nT", [P, KT, T])
        nT_at = nc.sbuf_base - 4 * KT * T
        stat = sb("stat", [P, 3, TT])
        unit = sb("unit", [P, 3, DEPTH])
        small = sb("small", [P, 3 * 512])
        brow = small[0:1, :]
        qk_stat = sb("qk_stat", [P, 3, 2 * TT * HEADS])
        br36 = sb("br36", [1, 36])
        logit = sb("logit", [P, TT, 40])
        route = sb("route", [P, TT, 80])
        top8 = sb("top8", [P, TT, 16])
        idx8 = sb("idx8", [P, TT, 16], U32)
        idx8f = sb("idx8f", [P, TT, 16])
        earlier = sb("earlier", [P, P])
        fullest = sb("fullest", [P, 1])
        overfull = sb("overfull", [P, 1], mybir.dt.int32)
        gatew = sb("gatew", [P, TT, EXPERTS])
        sel_dup = sb("sel_dup", [P, 2, P])
        modmask = sb("modmask", [P, P + SUB])
        mask_prev = sb("mask_prev", [P, P])
        mask_same = sb("mask_same", [P, P])
        w_glr = sb("w_glr", [P, KT, 16])
        glrT = sb("glrT", [16, T])
        gate_w2 = sb("gate_w2", [16, 256])
        cmp_w2 = sb("cmp_w2", [P, 2, DH])
        pos_rows = sb("pos_rows", [SUB, 2, P])
        posT = sb("posT", [P, 2, SUB])
        cmp_h = sb("cmp_h", [P, 2, 2 * N_CMP])
        k_cmpT = sb("k_cmpT", [P, 2 * N_CMP])
        v_cmp = sb("v_cmp", [N_CMP, 2, DH])
        nsa_gate = sb("nsa_gate", [P, TT, 3 * HEADS])
        gla_stat = sb("gla_stat", [P, 3, TT * GLA_HEADS])
        rel2 = sb("rel2", [BUCKETS, HEADS])
        SCR = SLOT * RING
        ARENA = SCR + 19456
        arena = sb("arena", [P, ARENA])
        arena_at = nc.sbuf_base - 4 * ARENA
        slot = [arena[:, SLOT * r:SLOT * (r + 1)] for r in range(RING)]

        def piece(at, *shape):
            n = int(np.prod(shape))
            assert at + n <= ARENA, (at, shape)
            v = arena[:, at:at + n]
            if len(shape) == 2:
                v = v.rearrange("p (a b) -> p a b", b=shape[1])
            if len(shape) == 3:
                v = v.rearrange("p (a b c) -> p a b c", b=shape[1], c=shape[2])
            if len(shape) == 4:
                v = v.rearrange("p (a b c d) -> p a b c d", b=shape[1], c=shape[2], d=shape[3])
            return v

        def scratch(at, *shape):
            return piece(SCR + at, *shape)

        xn = scratch(0, TT, D)
        att_p = scratch(2048, 2, T)
        att_pt = scratch(2560, 2, 2, P)
        vrows = scratch(2048, P)
        B0 = 3072
        z_tok = scratch(B0, 3, TT, 512)
        sq_tok = scratch(B0 + 3072, 2, TT, 512)
        qT = scratch(B0 + 5120, 4, T)
        kT = scratch(B0 + 6144, 4, T)
        convT = scratch(B0 + 7168, 12, T)
        sigT = scratch(B0 + 10240, 16, T)
        bias1 = scratch(B0 + 14336, HEADS, T)
        mixT = scratch(B0 + 3072, 8, T)
        cin = scratch(B0, 4, T + 2)
        mT = scratch(B0 + 5120, KT, T)
        wgr = scratch(B0, KT, 36)
        silu_h = scratch(B0 + 512, FT, T)
        hidT = scratch(B0 + 2048, FT, T)
        def part(name, at, *shape):
            return nc.alloc_sbuf_tensor_at(name, [P, *shape], F32R, offset=at)

        def scratch_part(name, at, *shape):
            return part(name, arena_at + 4 * (SCR + at), *shape)

        M0 = B0 + 512
        picked = scratch(M0, TT, EXPERTS)
        place = scratch(M0 + 64, TT, EXPERTS + 2)
        row_w = scratch(M0 + 136, 1)
        xn_lo = scratch_part("xn_lo", 0, TT, D)
        xn_hi = scratch_part("xn_hi", M0 + 256, TT, D)
        pick = scratch_part("pick", M0 + 2304, 2, TT, P)
        pickT = scratch_part("pickT", M0 + 2816, TT, P)
        gathT_hi = scratch_part("gathT_hi", M0 + 3072, KT, P)
        gathT_lo = scratch_part("gathT_lo", M0 + 4096, KT, P)
        silu_r = scratch(M0 + 5120, FF)
        hid_r = scratch(M0 + 5632, FF)
        hid_rT_hi = scratch_part("hid_rT_hi", M0 + 6144, FT, P)
        hid_rT_lo = scratch_part("hid_rT_lo", M0 + 6656, FT, P)
        out_hi = scratch_part("out_hi", M0 + 7168, D)
        out_lo = scratch_part("out_lo", M0 + 8192, D)
        PORTIONS, HI_BUFS = 6, 3
        w_hi = scratch_part("w_hi", M0 + 9216, HI_BUFS, 4, 512)
        slot_lo = [part(f"slot_lo_{r}", arena_at + 4 * SLOT * r, SLOT) for r in range(RING)]
        nT_hi = scratch_part("nT_hi", 0, KT, T)
        nT_lo = part("nT_lo", nT_at, KT, T)
        w_in_hi = scratch_part("w_in_hi", B0 + 3072, 2, KT, T)
        w_in2_hi = [scratch_part("w_in2_hi_0", B0 + 7680, KT, T), scratch_part("w_in2_hi_1", B0 + 14336, KT, T)]
        log_tmp = scratch(2048, 2, T)
        gain_row = scratch(M0 + 9216, D)

        def portion_of(ring, j, g):
            v = ring[(MOE_AT + 3 * j + g // 2) % RING]
            if g < 4:
                return v[:, 2048 * (g % 2):2048 * (g % 2) + 2048].rearrange("p (k n) -> p k n", n=512)
            return v[:, :].rearrange("p (k n) -> p k n", n=D)[:, :, 512 * (g % 2):512 * (g % 2) + 512]

        p_tok = scratch(B0, TT, 256)
        pT = scratch(B0 + 512, 2, T)
        gate_t = scratch(B0 + 1024, TT, D)
        gqkT = scratch(B0, 4, T)
        gv = scratch(B0 + 1024, TT, 512)
        gr = scratch(B0 + 2048, TT, 512)
        loga = scratch(B0 + 3072, 2, T)
        bcum = scratch(B0 + 3584, 2, T)
        nqT = scratch(B0 + 4096, 4, T)
        kvT = scratch(B0 + 5120, 4, T)
        v_sw = scratch(B0 + 6144, 2, TT, P)
        dupT = scratch(B0 + 6656, 4, T)
        catT = scratch(B0 + 7680, KT, T)
        q_dec = scratch(B0 + 9728, 2, T)
        gla_a = scratch(B0 + 10240, GLA_HEADS, 2, T)
        diag = scratch(B0 + 12288, NSUB, SUB, SUB)
        k_dec = scratch(0, 2, 2, T)
        o_gla = scratch(1024, TT, 512)
        cmp_w1 = scratch(B0 + 10240, 2, SUB, P)
        cmp_in = scratch(B0 + 14336, 2, SUB, 2, N_CMP)
        bias_sw = scratch(B0 + 10240, HEADS, T)
        bias_c = scratch(B0 + 12288, HEADS, T)
        dist_oh = scratch(B0 + 9728, T)
        dist_row = scratch(B0 + 10240, TAB)
        mem_tok = scratch(B0, TT, D)
        xkT = scratch(B0 + 2048, KT, T)
        xv = scratch(B0 + 4096, TT, D)
        xqT = scratch(B0 + 6144, KT, T)
        xoT = scratch(B0 + 8192, KT, T)
        TABLE = NKEYS * T
        gtab = piece(0, NKEYS, T)
        PR = 4
        down = [piece(TABLE + D * r, D) for r in range(PR)]
        DT = TABLE + PR * D
        downT_hi = part("downT_hi", arena_at + 4 * DT, 2, KT, P)
        downT_lo = part("downT_lo", arena_at + 4 * (DT + 2048), 2, KT, P)
        x_hi = part("x_hi", arena_at + 4 * (DT + 4096), KT, T)
        x_lo = nT_lo
        idxT = piece(DT + 6144, 3, T)
        hot = piece(TABLE, 2, 2, 2, P)
        gates = piece(TABLE + 1024, 4, 4 * P)
        e_hi = part("e_hi", arena_at + 4 * (TABLE + 1024), 2, T)
        e_lo = part("e_lo", arena_at + 4 * (TABLE + 1536), 2, T)
        u_hi = part("u_hi", arena_at + 4 * (TABLE + 2048), 2, D)
        u_lo = part("u_lo", arena_at + 4 * (TABLE + 4096), 2, D)
        up = [piece(TABLE + 6144 + D * r, D) for r in range(PR)]
        Q0 = SCR + B0
        pqT = piece(Q0, PH, T)
        sk_rows = piece(Q0 + 2048, 16, DH)
        skT = piece(Q0 + 3072, PH, P)
        TOP = TABLE // 2
        sc = piece(TOP, 16, NKEYS)
        tv = piece(TOP + 2048, TT, 16, TOPK)
        tif = piece(TOP + 2560, TT, 16, TOPK)
        ti = piece(TOP + 3072, TT, 16, TOPK).bitcast(U32)
        cand = piece(TOP + 3584, TT, PH, TOPK, TOPK)
        ci = piece(TOP + 7680, TT, PH, TOPK).bitcast(U32)
        cab = piece(TOP + 7936, 2, TT, PH * TOPK).bitcast(U32)
        cabf = piece(TOP + 8448, 2, TT, PH * TOPK)
        eq = piece(TOP + 8960, 2, 2, TOPK, TOPK)
        fin3 = small[:, 0:768].rearrange("p (c t a) -> p c t a", c=3, t=TT)
        cv = small[:, 768:1024].rearrange("p (t a k) -> p t a k", t=TT, a=PH)
        psum16 = small[:, 1024:1056].rearrange("p (c a) -> p c a", c=2)
        gfin = scratch(B0, D)
        iota16 = iota[:, 0:TOPK]

        first, later = weight_slots(w)
        NF = len(first)
        MOE_AT, LATE_AT = NF, NF + 3 * EXPERTS
        landed = [S(f"slot_landed_{r}") for r in range(RING)]
        split_slots = [n for n, pieces in enumerate(first) if len(pieces) > 1]

        def slot_ready(eng, n, i=0):
            extra = sum(1 for m in split_slots if m % RING == n % RING and m <= n)
            eng.wait_ge(landed[n % RING], i * 16 + 16 * (n // RING + 1 + extra))

        def slot_view(n, kt, width):
            return slot[n % RING][:, 0:kt * width].rearrange("p (k n) -> p k n", n=width)

        def col(name, k):
            c = COL[name] + k
            return vecs[:, c:c + 1]

        phases = {}

        def phase_end(eng, key):
            phases[key] = phases.get(key, 0) + 1
            eng.drain().then_inc(S("phase"), 1)
            eng.wait_ge(S("phase"), 3 * phases[key])

        def units_block1():
            for qt in range(TT):
                for head in range(HEADS):
                    r, nb = DH * (head % 2), qt + 1
                    q0 = P * qt
                    yield dict(
                        q=[qT[r:r + DH, head // 2, q0:q0 + P]], k=[kT[r:r + DH, head // 2, 0:P * nb]], n=P * nb,
                        bias=[bias1[:, head, q0 - P * b:q0 - P * b + P] for b in range(nb)],
                        v=[[z_tok[:, 2, b, DH * head:DH * head + DH] for b in range(nb)]],
                        gate=None, base=r, start=True, last=True,
                        dest=mixT[:, head // 2, q0:q0 + P] if head % 2 else None)

        def units_nsa():
            for qt in range(TT):
                q0 = P * qt
                for head in range(HEADS):
                    r, g, nb = DH * (head % 2), head // 4, qt + 1
                    q = [nqT[r:r + DH, head // 2, q0:q0 + P]]
                    yield dict(
                        q=q, k=[k_cmpT[r:r + DH, N_CMP * g:N_CMP * g + N_CMP]], n=N_CMP,
                        bias=[bias_c[0:N_CMP, head, q0:q0 + P]], v=[[v_cmp[:, g, :]]],
                        gate=nsa_gate[:, qt, 3 * head:3 * head + 1], base=r, start=True, last=False, dest=None)
                    for b3 in range(2):
                        yield dict(
                            q=q, k=[dupT[r:r + DH, 2 * b3 + g, 0:P * nb]], n=P * nb,
                            bias=[bias_sw[:, head, q0 - P * b:q0 - P * b + P] for b in range(nb)],
                            v=[[v_sw[:, b3, b, DH * g:DH * g + DH] for b in range(nb)]],
                            gate=nsa_gate[:, qt, 3 * head + 1 + b3:3 * head + 2 + b3], base=r,
                            start=False, last=b3 == 1,
                            dest=catT[:, 4 + head // 2, q0:q0 + P] if head % 2 and b3 == 1 else None)

        def units_cross():
            for qt in range(TT):
                q0 = P * qt
                for head in range(XHEADS):
                    yield dict(
                        q=[xqT[:, 2 * head + c, q0:q0 + P] for c in range(2)],
                        k=[xkT[:, 2 * head + c, :] for c in range(2)], n=T, bias=[],
                        v=[[xv[:, b, 256 * head + P * c:256 * head + P * c + P] for b in range(2)] for c in range(2)],
                        gate=None, base=0, start=True, last=True, dest=xoT[:, 2 * head:2 * head + 2, q0:q0 + P])

        n1, n2 = len(list(units_block1())), len(list(units_nsa()))
        ATT1, NSA, CROSS = (0, 0), (n1, HEADS), (n1 + n2, 2 * HEADS)

        def score_bank(u):
            return bank[(0, 1, 6, 7)[u % DEPTH]]

        def probs(u):
            return att_p[:, u % DEPTH, :] if u % DEPTH < 2 else nT[:, u % DEPTH, :]

        def attention_pe(pe, at, units):
            units = list(units)
            u0, g0 = at
            group = 0

            def scores(u):
                a = units[u]
                if u >= DEPTH:
                    pe.wait_ge(S("att_exp"), u0 + u - DEPTH + 1)
                s = score_bank(u)[:, 0:a["n"]]
                last = len(a["bias"]) == 0
                for c, (q, k) in enumerate(zip(a["q"], a["k"])):
                    mm = nc.tensor.matmul(s, lhsT=q, rhs=k, start=c == 0, stop=last and c == len(a["q"]) - 1)
                for b, bias in enumerate(a["bias"]):
                    n = min(P, a["n"])
                    mm = nc.tensor.matmul(score_bank(u)[:, P * b:P * b + n], lhsT=bias, rhs=mirror[0:n, P - n:P],
                                          start=False, stop=b == len(a["bias"]) - 1)
                mm.then_inc(S("att_scores"), 1)

            def turn(u):
                a = units[u]
                pe.wait_ge(S("att_probs"), u0 + u + 1)
                if u >= 2:
                    pe.wait_ge(S("att_turned"), u0 + u - 1)
                nb = (a["n"] + P - 1) // P
                n = min(P, a["n"])
                for b in range(nb):
                    mm = nc.tensor.transpose(bank[2 + u % 2][0:n, P * b:P * b + P],
                                             probs(u)[:, P * b:P * b + n], ident[:, :])
                mm.then_inc(S("att_turns"), 1)

            def values(u):
                nonlocal group
                a = units[u]
                pe.wait_ge(S("att_turned"), u0 + u + 1)
                if group >= 2 and a["start"]:
                    pe.wait_ge(S("att_out"), g0 + group - 1)
                n = min(P, a["n"])
                for c, blocks in enumerate(a["v"]):
                    for b, v in enumerate(blocks):
                        o = bank[4 + group % 2][a["base"]:a["base"] + v.shape[1], P * c:P * c + P]
                        mm = nc.tensor.matmul(o, lhsT=v, rhs=att_pt[0:n, u % 2, b, :],
                                              start=a["start"] and b == 0, stop=a["last"] and b == len(blocks) - 1)
                mm.then_inc(S("att_values"), 1)
                if a["dest"] is not None:
                    group += 1

            for u in range(len(units) + DEPTH):
                if u < len(units):
                    scores(u)
                if 0 <= u - (DEPTH - 1) < len(units):
                    turn(u - (DEPTH - 1))
                if u >= DEPTH:
                    values(u - DEPTH)

        def attention_dve(dve, at, units):
            units = list(units)
            u0, g0 = at

            def peak(u):
                dve.wait_ge(S("att_scores"), u0 + u + 1)
                if u >= DEPTH:
                    dve.wait_ge(S("att_exp"), u0 + u - DEPTH + 1)
                nc.vector.tensor_reduce(unit[:, 0, u % DEPTH:u % DEPTH + 1], score_bank(u)[:, 0:units[u]["n"]], X, ALU.max,
                                        negate=True).then_inc(S("att_max"), 1)

            def norm(u):
                a = units[u]
                n = a["n"]
                dve.wait_ge(S("att_exp"), u0 + u + 1)
                nc.vector.reciprocal(unit[:, 2, u % DEPTH:u % DEPTH + 1], unit[:, 1, u % DEPTH:u % DEPTH + 1]).then_inc(
                    S("att_inv"), 1)
                dve.wait_ge(S("att_inv"), u0 + u + 1)
                if a["gate"] is None:
                    ins = nc.vector.tensor_scalar(probs(u)[:, 0:n], probs(u)[:, 0:n],
                                                  unit[:, 2, u % DEPTH:u % DEPTH + 1], None, ALU.mult)
                else:
                    ins = nc.vector.tensor_scalar(probs(u)[:, 0:n], probs(u)[:, 0:n],
                                                  unit[:, 2, u % DEPTH:u % DEPTH + 1], a["gate"], ALU.mult, ALU.mult)
                ins.then_inc(S("att_probs"), 1)

            for u in range(len(units) + 1):
                if u < len(units):
                    peak(u)
                if u >= 1:
                    norm(u - 1)

        def attention_act(act, at, units):
            units = list(units)
            u0, g0 = at
            group = 0

            def exps(u):
                n = units[u]["n"]
                act.wait_ge(S("att_max"), u0 + u + 1)
                if u >= DEPTH:
                    act.wait_ge(S("att_turns"), u0 + u - DEPTH + 1)
                nc.scalar.activation(probs(u)[:, 0:n], score_bank(u)[:, 0:n], ACT.Exp,
                                     bias=unit[:, 0, u % DEPTH:u % DEPTH + 1],
                                     accum_out=unit[:, 1, u % DEPTH:u % DEPTH + 1]).then_inc(S("att_exp"), 1)

            def copy(u):
                nb, n = (units[u]["n"] + P - 1) // P, min(P, units[u]["n"])
                act.wait_ge(S("att_turns"), u0 + u + 1)
                if u >= 2:
                    act.wait_ge(S("att_values"), u0 + u - 1)
                nc.scalar.copy(att_pt[0:n, u % 2, 0:nb, :].rearrange("p b q -> p (b q)"),
                               bank[2 + u % 2][0:n, 0:P * nb]).then_inc(S("att_turned"), 1)

            def outs(u):
                nonlocal group
                dest = units[u]["dest"]
                if dest is None:
                    return
                act.wait_ge(S("att_values"), u0 + u + 1)
                src = bank[4 + group % 2]
                if len(units[u]["v"]) == 2:
                    src = src[:, 0:2 * P].rearrange("p (c q) -> p c q", c=2)
                else:
                    src = src[:, 0:P]
                nc.scalar.copy(dest, src).then_inc(S("att_out"), 1)
                group += 1

            for u in range(len(units) + DEPTH):
                if u < len(units):
                    exps(u)
                if 0 <= u - (DEPTH - 1) < len(units):
                    copy(u - (DEPTH - 1))
                if u >= DEPTH:
                    outs(u - DEPTH)

        NORMS = ["mix", "ffn", "ple", "mix2", "mem", "xa", "peer", "fin"]

        def wait_nT(eng, tag, k):
            eng.wait_ge(S("norm_nT"), KT * NORMS.index(tag) + k)

        def norm_act(act, chain, tag, src):
            for t in range(TT):
                chain(nc.scalar.activation(xn[:, t, :], src[:, t, :], ACT.Square, accum_out=stat[:, 0, t:t + 1]))
            nc.scalar.activation(stat[:, 1, :], stat[:, 0, :], ACT.Sqrt, bias=eps[:, 0:1],
                                 scale=1.0 / D).then_inc(S("norm_rms"), 1)

        def norm_dve(dve, chain, tag, src, gain):
            dve.wait_ge(S("norm_rms"), NORMS.index(tag) + 1)
            chain(nc.vector.reciprocal(stat[:, 2, :], stat[:, 1, :]))
            for t in range(TT):
                nc.vector.tensor_scalar(xn[:, t, :], src[:, t, :], stat[:, 2, t:t + 1], None,
                                        ALU.mult).then_inc(S("norm_xn"), 1)
            for k in range(KT):
                if k % 2 == 0:
                    dve.wait_ge(S("norm_turned"), 4 * NORMS.index(tag) + k // 2 + 1)
                nc.vector.tensor_scalar(nT[:, k, :], bank[k // 2][:, T * (k % 2):T * (k % 2) + T], col(gain, k),
                                        None, ALU.mult).then_inc(S("norm_nT"), 1)

        def norm_pe(pe, tag):
            pe.wait_ge(S("norm_xn"), TT * (NORMS.index(tag) + 1))
            for k in range(KT):
                for t in range(TT):
                    at = T * (k % 2) + P * t
                    mm = nc.tensor.transpose(bank[k // 2][:, at:at + P], xn[:, t, P * k:P * k + P], ident[:, :])
                if k % 2:
                    mm.then_inc(S("norm_turned"), 1)

        tile_no = {}
        spent_at = {}

        def tile_bank(pe, tag):
            n = tile_no[tag] = len(tile_no)
            if n >= 4:
                pe.wait_ge(S("tile_read"), n - 3)
            return bank[4 + n % 4]

        def project_T(pe, tag, wv, kt, c0, cols, src):
            b = tile_bank(pe, tag)
            for k in range(kt):
                mm = nc.tensor.matmul(b[0:cols, 0:T], lhsT=wv[:, k, c0:c0 + cols], rhs=src[:, k, :],
                                      start=k == 0, stop=k == kt - 1)
            mm.then_inc(S("tile_done"), 1)

        def project_tok(pe, tag, wv, kt, c0, cols, t, src, bias=None):
            b = tile_bank(pe, tag)
            if bias is not None:
                nc.tensor.matmul(b[:, 0:cols], lhsT=ones[0:1, :], rhs=bias, start=True, stop=False)
            for k in range(kt):
                mm = nc.tensor.matmul(b[:, 0:cols], lhsT=src[:, k, P * t:P * t + P], rhs=wv[:, k, c0:c0 + cols],
                                      start=k == 0 and bias is None, stop=k == kt - 1)
            mm.then_inc(S("tile_done"), 1)

        def spent(n):
            spent_at[n] = len(tile_no)

        def tile_in(eng, tag):
            n = tile_no[tag]
            eng.wait_ge(S("tile_done"), n + 1)
            return bank[4 + n % 4]

        SPLIT = {"mix": range(0, 10), "mix2": range(LATE_AT + 5, LATE_AT + 9),
                 "mem": range(LATE_AT + 11, LATE_AT + 15),
                 "xa": range(LATE_AT + 15, LATE_AT + 17), "peer": range(LATE_AT + 19, LATE_AT + 21)}
        LAYERS = list(SPLIT)
        portion_done = {}

        def portions(tag):
            base = sum(2 * len(SPLIT[x]) for x in LAYERS[:LAYERS.index(tag)])
            return [(base + q, SPLIT[tag][q // 2], q % 2) for q in range(2 * len(SPLIT[tag]))]

        def layer_part(p, n, half, which):
            if which == "hi":
                if n < MOE_AT:
                    return w_in_hi[:, p % 2, :, :]
                if n < LATE_AT + 9:
                    return w_in2_hi[p % 2][:, :, :]
                return w_hi[:, 1 + p % 2, :, :].rearrange("p a b -> p (a b)").rearrange("p (k n) -> p k n", n=T)
            ring = (slot if which == "whole" else slot_lo)[n % RING]
            return ring[:, :].rearrange("p (k n) -> p k n", n=512)[:, :, T * half:T * half + T]

        def layer_hi(act, p, n, half):
            if p - 2 in portion_done:
                act.wait_ge(*portion_done[p - 2])
            slot_ready(act, n)
            nc.scalar.copy(layer_part(p, n, half, "hi"), layer_part(p, n, half, "whole")).then_inc(S("layer_hi"), 1)

        def layer_act(act, tag, read, before=None):
            ports = portions(tag)
            for port in ports[:2]:
                layer_hi(act, *port)
            for b in range(2):
                wait_nT(act, tag, 4 * b + 4)
                if b == 0:
                    act.wait_ge(S("norm_turned"), 4 * NORMS.index(tag) + 4)
                nc.scalar.copy(nT_hi[:, 4 * b:4 * b + 4, :], nT[:, 4 * b:4 * b + 4, :]).then_inc(S("nT_hi"), 1)
            if before is not None:
                before()
            for q in range(len(ports)):
                if q + 2 < len(ports):
                    layer_hi(act, *ports[q + 2])
                read(q)

        def layer_dve(dve, tag, last_whole=None):
            def layer_lo(p, n, half):
                dve.wait_ge(S("layer_hi"), p + 1)
                nc.vector.tensor_tensor(layer_part(p, n, half, "lo"), layer_part(p, n, half, "whole"),
                                        layer_part(p, n, half, "hi").bitcast(F32), ALU.subtract).then_inc(
                                            S("layer_lo"), 1)

            ports = portions(tag)
            if last_whole is not None:
                for port in ports[:2]:
                    layer_lo(*port)
                ports = ports[2:]
                tile_in(dve, last_whole)
            for b in range(2):
                dve.wait_ge(S("nT_hi"), 2 * LAYERS.index(tag) + b + 1)
                nc.vector.tensor_tensor(nT_lo[:, 4 * b:4 * b + 4, :], nT[:, 4 * b:4 * b + 4, :],
                                        nT_hi[:, 4 * b:4 * b + 4, :].bitcast(F32), ALU.subtract).then_inc(S("nT_lo"), 1)
            for port in ports:
                layer_lo(*port)

        def layer_products(pe, tag, port, out, operands, biased=False):
            p, n, half = port
            hi, lo = layer_part(p, n, half, "hi"), layer_part(p, n, half, "lo")
            for x, wp in ((nT_hi, hi), (nT_lo, hi), (nT_hi, lo)):
                if wp is lo:
                    pe.wait_ge(S("layer_lo"), p + 1)
                elif x is nT_lo:
                    pe.wait_ge(S("nT_lo"), 2 * LAYERS.index(tag) + 2)
                else:
                    pe.wait_ge(S("layer_hi"), p + 1)
                    pe.wait_ge(S("nT_hi"), 2 * LAYERS.index(tag) + 2)
                for k in range(KT):
                    lhsT, rhs = operands(k, x, wp)
                    mm = nc.tensor.matmul(out, lhsT=lhsT, rhs=rhs, start=x is nT_hi and wp is hi and k == 0 and not biased,
                                          stop=wp is lo and k == KT - 1)
            return mm

        def layer_T(pe, tag, name, ports, m0):
            for port in ports:
                for x in range(2):
                    b = tile_bank(pe, (name, m0 + 2 * port[2] + x))
                    layer_products(pe, tag, port, b[:, 0:T],
                                   lambda k, src, wp: (wp[:, k, P * x:P * x + P], src[:, k, :])).then_inc(
                                       S("tile_done"), 1)
                portion_done[port[0]] = (S("tile_done"), len(tile_no))
            spent(port[1])

        def layer_tok(pe, tag, name, ports, s, bias=None):
            banks = [tile_bank(pe, (name, s, t)) for t in range(TT)]
            for port in ports:
                half = port[2]
                for t in range(TT):
                    out = banks[t][:, T * half:T * half + T]
                    if bias is not None:
                        nc.tensor.matmul(out, lhsT=ones[0:1, :], rhs=bias[0:1, T * half:T * half + T], start=True,
                                         stop=False)
                    mm = layer_products(pe, tag, port, out, lambda k, src, wp: (src[:, k, P * t:P * t + P], wp[:, k, :]),
                                        bias is not None)
                    if half:
                        mm.then_inc(S("tile_done"), 1)
                if not half:
                    mm.then_inc(S("first_half_used"), 1)
                    halves_used.append(port[0])
                    portion_done[port[0]] = (S("first_half_used"), len(halves_used))
            portion_done[port[0]] = (S("tile_done"), len(tile_no))
            spent(port[1])

        halves_used = []

        def residual_pe(pe, tag, at, src):
            for j in range(2):
                slot_ready(pe, at + j)
                for t in range(TT):
                    project_tok(pe, (tag, j, t), slot_view(at + j, KT, 512), KT, 0, 512, t, src)
                spent(at + j)

        def residual_dve(dve, tag):
            for j in range(2):
                for t in range(TT):
                    b = tile_in(dve, (tag, j, t))
                    hs = h[:, t, 512 * j:512 * j + 512]
                    nc.vector.tensor_tensor(hs, hs, b[:, :], ALU.add).then_inc(S("tile_read"), 1)

        def spread(ap, n):
            return ap.unsqueeze(len(ap.shape)).to_broadcast(list(ap.shape) + [n])

        def toeplitz(tensor, offset, step, rows, heads, pitch, width):
            return bass.AP(tensor=tensor, offset=offset, ap=[[step, rows], [pitch, heads], [1, width]])

        block = ctx.enter_context(nc.Block())

        @block.tensor
        def _(pe):
            pe.wait_ge(S("consts"), 1)
            pe.wait_ge(S("vrows_landed"), 16 * NVROWS)
            nc.tensor.transpose(bank[0][:, 0:NVEC], vrows[0:NVEC, :], ident[0:NVEC, 0:NVEC]).then_inc(S("vecs_turned"), 1)
            pe.wait_ge(S("table_in"), 32)
            nc.tensor.matmul(bank[1][0:HEADS, 0:T], lhsT=rel2[:, :], rhs=dist_oh[0:BUCKETS, :], start=True,
                             stop=True).then_inc(S("table_done"), 1)
            phase_end(pe, "pe")

            norm_pe(pe, "mix")
            pe.wait_ge(S("brow_in"), 16)
            ports = portions("mix")
            for s in range(3):
                layer_tok(pe, "mix", "qkv", ports[2 * s:2 * s + 2], s, brow[0:1, 512 * s:512 * s + 512])
            for s in range(3, 10):
                layer_T(pe, "mix", "in1", ports[2 * s:2 * s + 2], 4 * (s - 3))
            phase_end(pe, "pe")

            for s in range(2):
                pe.wait_ge(S("qk_normed"), s + 1)
                for m in range(4):
                    for t in range(TT):
                        at = T * (m % 2) + P * t
                        mm = nc.tensor.transpose(bank[2 * s + m // 2][:, at:at + P],
                                                 z_tok[:, s, t, P * m:P * m + P], ident[:, :])
                mm.then_inc(S("qk_turned"), 1)
            phase_end(pe, "pe")
            attention_pe(pe, ATT1, units_block1())
            phase_end(pe, "pe")
            pe.wait_ge(S("conv_done"), 4)
            for s in range(10, 12):
                slot_ready(pe, s)
                wv = slot_view(s, KT, 512)
                for m in range(4):
                    b = tile_bank(pe, ("mix", 4 * (s - 10) + m))
                    for part in range(2):
                        for k in range(4):
                            mm = nc.tensor.matmul(b[:, T * part:T * part + T],
                                                  lhsT=wv[:, 4 * part + k, P * m:P * m + P],
                                                  rhs=mixT[:, 4 * part + k, :], start=k == 0, stop=k == 3)
                    mm.then_inc(S("tile_done"), 1)
                spent(s)
            pe.wait_ge(S("mT_ready"), KT)
            residual_pe(pe, "wo", 12, mT)
            phase_end(pe, "pe")

            norm_pe(pe, "ffn")
            wait_nT(pe, "ffn", KT)
            pe.wait_ge(S("router_in"), 16 * 4)
            for t in range(TT):
                project_tok(pe, ("router", t), wgr, KT, 0, 36, t, nT, br36[0:1, :])
            pe.wait_ge(S("picked_ready"), 1)
            b = bank[0]
            nc.tensor.matmul(b[:, 0:EXPERTS], lhsT=earlier[:, :], rhs=picked[:, 0, :], start=True, stop=True)
            nc.tensor.matmul(b[:, 64:64 + EXPERTS], lhsT=earlier[:, :], rhs=picked[:, 1, :], start=True, stop=False)
            nc.tensor.matmul(b[:, 64:64 + EXPERTS], lhsT=ones[:, :], rhs=picked[:, 0, :], start=False, stop=True)
            nc.tensor.matmul(b[:, 128:128 + EXPERTS], lhsT=ones[:, :], rhs=picked[:, 0, :], start=True, stop=False)
            nc.tensor.matmul(b[:, 128:128 + EXPERTS], lhsT=ones[:, :], rhs=picked[:, 1, :], start=False,
                             stop=True).then_inc(S("rows_counted"), 1)
            phase_end(pe, "pe")
            phases["routed"] = phases["pe"]
            def gather(buf, ks):
                for k in ks:
                    for t in range(TT):
                        for xp in (xn_hi, xn_lo):
                            mm = nc.tensor.matmul(bank[k // 4][:, P * (k % 4):P * (k % 4) + P],
                                                  lhsT=xp[:, t, P * k:P * k + P], rhs=pick[:, buf, t, :],
                                                  start=t == 0 and xp is xn_hi, stop=t == TT - 1 and xp is xn_lo)
                if k == KT - 1:
                    mm.then_inc(S("gathered"), 1)

            def scatter(i, j, t):
                if t == 0:
                    pe.wait_ge(S("out_lo"), i * 4 + (2 * j + 2))
                    pe.wait_ge(S("turned_pick"), i * 2 + (j + 1))
                for c in (2 * t, 2 * t + 1):
                    if c >= 2:
                        pe.wait_ge(S("row_added"), i * 8 + (4 * j + c - 1))
                    for op in (out_hi, out_lo):
                        mm = nc.tensor.matmul(bank[6 + c % 2][:, :], lhsT=pickT[:, t, :],
                                              rhs=op[:, 512 * (c % 2):512 * (c % 2) + 512], start=op is out_hi,
                                              stop=op is out_lo)
                    mm.then_inc(S("scattered"), 1)

            def portion(i, j, g, dst, lhs_hi, lhs_lo, wait_lhs_lo, first, last):
                at = (PORTIONS * j + g) % HI_BUFS
                lo = portion_of(slot_lo, j, g)
                pe.wait_ge(S("w_hi"), i * (2 * PORTIONS) + (PORTIONS * j + g + 1))
                for k in range(4):
                    nc.tensor.matmul(dst, lhsT=lhs_hi(k), rhs=w_hi[:, at, k, :], start=first and k == 0, stop=False)
                wait_lhs_lo()
                for k in range(4):
                    nc.tensor.matmul(dst, lhsT=lhs_lo(k), rhs=w_hi[:, at, k, :], start=False, stop=False)
                if g < 4:
                    pe.wait_ge(S("w13_lo"), i * 8 + (4 * j + g + 1))
                else:
                    pe.wait_ge(S("w2_lo"), i * 4 + (2 * j + g - 3))
                for k in range(4):
                    mm = nc.tensor.matmul(dst, lhsT=lhs_hi(k), rhs=lo[:, k, :], start=False, stop=last and k == 3)
                mm.then_inc(S("portion_used"), 1)

            def expert(i, j):
                def hidden(g):
                    k0 = 4 * (g % 2)
                    portion(i, j, g, bank[2 + g // 2][:, :], lambda k: gathT_hi[:, k0 + k, :],
                            lambda k: gathT_lo[:, k0 + k, :],
                            lambda: pe.wait_ge(S("gathT_lo"), i * 4 + (2 * j + 2)), g % 2 == 0, g % 2 == 1)

                pe.wait_ge(S("gathT_hi"), i * 4 + (2 * j + 2))
                pe.wait_ge(S("hid_ready"), i * 2 + (j + 1))
                hidden(0)
                hidden(1)
                scatter(i, j, 0)
                hidden(2)
                scatter(i, j, 1)
                hidden(3)
                for t in range(TT):
                    nc.tensor.transpose(bank[5][:, P * (t + 1):P * (t + 2)], pick[:, j, t, :].bitcast(F32), ident[:, :])
                for t in range(TT):
                    mm = nc.tensor.matmul(bank[5][:, 0:1], lhsT=pick[:, j, t, :].bitcast(F32),
                                          rhs=gatew[:, t, bass.ds(i * 2 + j, 1)], start=t == 0, stop=t == TT - 1)
                mm.then_inc(S("pick_turned"), 1)
                pe.wait_ge(S("pick_ready"), i * 2 + (j + 2))
                gather((j + 1) % 2, range(4))
                pe.wait_ge(S("hid_ready"), i * 2 + (j + 2))
                pe.wait_ge(S("hid_rT_lo"), i * 2 + (j + 1))
                for f in range(FT):
                    mm = nc.tensor.transpose(bank[4][:, P * f:P * f + P], hid_r[:, P * f:P * f + P], ident[:, :])
                mm.then_inc(S("hid_turned"), 1)
                gather((j + 1) % 2, range(4, KT))
                pe.wait_ge(S("hid_rT_hi"), i * 2 + (j + 1))
                for half in range(2):
                    pe.wait_ge(S("row_added"), i * 8 + (4 * j + 3 + half))
                    portion(i, j, 4 + half, bank[6 + half][:, :], lambda f: hid_rT_hi[:, f, :],
                            lambda f: hid_rT_lo[:, f, :],
                            lambda: pe.wait_ge(S("hid_rT_lo"), i * 2 + (j + 2)), True, True)

            over = pe.value_load(overfull[0:1, 0:1], min_val=0, max_val=1)
            with pe.If(over < 1):
                gather(0, range(KT))
                with pe.Fori(0, EXPERTS // 2) as i:
                    for j in range(2):
                        expert(i, j)
                for t in range(TT):
                    scatter(EXPERTS // 2, 0, t)
            with pe.Else():
                with pe.Fori(0, EXPERTS // 2) as i:
                    for j in range(2):
                        n = MOE_AT + 3 * j
                        slot_ready(pe, n, i)
                        slot_ready(pe, n + 1, i)
                        w1v, w3v = slot_view(n, KT, FF), slot_view(n + 1, KT, FF)
                        for f in range(FT):
                            pe.wait_ge(S("moe_hidden"), i * (2 * FT) + (FT * j + f + 1))
                            for part, wv in enumerate((w1v, w3v)):
                                for k in range(KT):
                                    mm = nc.tensor.matmul(bank[f][:, T * part:T * part + T],
                                                          lhsT=wv[:, k, P * f:P * f + P], rhs=nT[:, k, :],
                                                          start=k == 0, stop=k == KT - 1)
                            mm.then_inc(S("moe_products"), 1)
                        pe.drain().then_inc(S("portion_used"), 4)
                        slot_ready(pe, n + 2, i)
                        w2v = slot_view(n + 2, FT, D)
                        pe.wait_ge(S("moe_hidden"), i * (2 * FT) + FT * (j + 2))
                        for c in range(4):
                            t, half = c // 2, c % 2
                            pe.wait_ge(S("moe_added"), i * 8 + (4 * j + c + 1))
                            for f in range(FT):
                                mm = nc.tensor.matmul(bank[4 + c][:, :], lhsT=hidT[:, f, P * t:P * t + P],
                                                      rhs=w2v[:, f, 512 * half:512 * half + 512],
                                                      start=f == 0, stop=f == FT - 1)
                            mm.then_inc(S("moe_out"), 1)
                        pe.drain().then_inc(S("portion_used"), 2)
            phase_end(pe, "pe")

            norm_pe(pe, "ple")
            pe.wait_ge(S("ple_in"), 32)
            for k in range(2):
                for t in range(TT):
                    wait_nT(pe, "ple", 2)
                    mm = nc.tensor.transpose(bank[0][:, T * k + P * t:T * k + P * t + P],
                                             p_tok[:, t, P * k:P * k + P], ident[:, :])
            mm.then_inc(S("p_turned"), 1)
            wait_nT(pe, "ple", KT)
            for j in range(2):
                n = LATE_AT + j
                slot_ready(pe, n)
                for t in range(TT):
                    project_tok(pe, ("gate", j, t), slot_view(n, KT, 512), KT, 0, 512, t, nT,
                                brow[0:1, 512 * j:512 * j + 512])
                spent(n)
            pe.wait_ge(S("pT_ready"), 1)
            n = LATE_AT + 2
            slot_ready(pe, n)
            for j in range(2):
                for t in range(TT):
                    project_tok(pe, ("ple", j, t), slot_view(n, 2, D), 2, 512 * j, 512, t, pT)
            spent(n)
            phase_end(pe, "pe")

            norm_pe(pe, "mix2")
            wait_nT(pe, "mix2", KT)
            n = LATE_AT + 3
            slot_ready(pe, n)
            for m in range(3):
                project_T(pe, ("kv", m), slot_view(n, KT, 384), KT, P * m, P, nT)
            spent(n)
            slot_ready(pe, n + 1)
            wv = slot_view(n + 1, KT, 408)
            project_T(pe, ("kv", 3), wv, KT, P, P, nT)
            for s in range(2):
                for t in range(TT):
                    project_tok(pe, ("vsw", s, t), wv, KT, 256 * s, P, t, nT)
            for t in range(TT):
                project_tok(pe, ("ng", t), wv, KT, 384, 24, t, nT)
            spent(n + 1)
            pe.wait_ge(S("late_in"), 16 * NLATE)
            project_T(pe, ("glr", 0), w_glr, KT, 0, 16, nT)
            ports = portions("mix2")
            layer_T(pe, "mix2", "gqk", ports[0:2], 0)
            pe.wait_ge(S("glr_ready"), 1)
            for c in range(2):
                b = tile_bank(pe, ("loga", c))
                nc.tensor.matmul(b[:, 0:T], lhsT=gate_w2[:, P * c:P * c + P], rhs=glrT[:, :], start=True,
                                 stop=True).then_inc(S("tile_done"), 1)
            for s in range(2):
                layer_tok(pe, "mix2", "gvr", ports[2 + 2 * s:4 + 2 * s], s)
            layer_T(pe, "mix2", "nq", ports[6:8], 0)
            phase_end(pe, "pe")

            for b, m in ((0, 0), (1, 1), (4, 2), (5, 3)):
                for g in range(2):
                    mm = nc.tensor.matmul(bank[b][:, T * g:T * g + T], lhsT=sel_dup[:, g, :], rhs=kvT[:, m, :],
                                          start=True, stop=True)
                mm.then_inc(S("dup_done"), 1)
            for s in range(2):
                mm = nc.tensor.transpose(bank[6][:, SUB * s:SUB * s + SUB], pos_rows[:, s, :], ident[0:SUB, 0:SUB])
            mm.then_inc(S("pos_turned"), 1)
            pe.wait_ge(S("cmp_in_ready"), 2)
            for s in range(2):
                for i in range(SUB):
                    mm = nc.tensor.matmul(bank[2][:, 32 * s:32 * s + 2 * N_CMP], lhsT=cmp_w1[:, s, i, :],
                                          rhs=cmp_in[:, s, i, :, :].rearrange("p g n -> p (g n)"),
                                          start=i == 0, stop=i == SUB - 1)
            mm.then_inc(S("cmp_hidden"), 1)
            pe.wait_ge(S("cmp_gelu"), 1)
            for half in range(2):
                nc.tensor.matmul(bank[3][DH * half:DH * half + DH, 0:2 * N_CMP], lhsT=cmp_w2[:, 0, :],
                                 rhs=cmp_h[:, 0, :], start=True, stop=True)
            for g in range(2):
                mm = nc.tensor.matmul(bank[7][0:N_CMP, DH * g:DH * g + DH],
                                      lhsT=cmp_h[:, 1, N_CMP * g:N_CMP * g + N_CMP], rhs=cmp_w2[:, 1, :],
                                      start=True, stop=True)
            mm.then_inc(S("cmp_out"), 1)
            phase_end(pe, "pe")

            pe.wait_ge(S("q_dec_ready"), 2)
            for u in range(NSUB):
                for c in range(2):
                    pe.wait_ge(S("k_dec_ready"), 2 * u + c + 1)
                    for r in range(2):
                        rows = slice(DH * r, DH * r + DH)
                        for st in range(1 if u < NSUB // 2 else 2):
                            mm = nc.tensor.matmul(bank[2 * c + r][:, T * st + SUB * u:T * st + SUB * u + SUB],
                                                  lhsT=k_dec[rows, u % 2, c, P * st:P * st + P],
                                                  rhs=q_dec[rows, c, SUB * u:SUB * u + SUB], start=True, stop=True)
                    mm.then_inc(S("k_dec_used"), 1)
            for n in range(4):
                c, part = n // 2, n % 2
                pe.wait_ge(S("diag_ready"), n + 1)
                for r in range(2):
                    rows = slice(DH * r, DH * r + DH)
                    dv = diag[rows, 8 * part:8 * part + 8, :, :].rearrange("p u t j -> p (u t) j")
                    for j in range(SUB):
                        mm = nc.tensor.matmul(bank[4 + 2 * c + r][:, P * part:P * part + P], lhsT=modmask[rows, SUB - 1 - j:SUB - 1 - j + P],
                                              rhs=dv[:, :, j], start=j == 0, stop=j == SUB - 1)
                mm.then_inc(S("diag_used"), 1)
            pe.wait_ge(S("gla_a_ready"), 1)
            for t in range(TT):
                for hh in range(GLA_HEADS):
                    for st in range(t + 1):
                        mm = nc.tensor.matmul(bank[t][:, P * hh:P * hh + P], lhsT=gla_a[:, hh, st, P * t:P * t + P],
                                              rhs=gv[:, st, P * hh:P * hh + P], start=st == 0, stop=st == t)
            mm.then_inc(S("gla_out"), 1)
            pe.wait_ge(S("gla_normed"), 1)
            for hh in range(GLA_HEADS):
                for t in range(TT):
                    at = T * (hh % 2) + P * t
                    mm = nc.tensor.transpose(bank[2 + hh // 2][:, at:at + P], o_gla[:, t, P * hh:P * hh + P],
                                             ident[:, :])
            mm.then_inc(S("gla_turned"), 1)
            phase_end(pe, "pe")
            pe.wait_ge(S("bias2_in"), 32)
            attention_pe(pe, NSA, units_nsa())
            phase_end(pe, "pe")
            residual_pe(pe, "wout", LATE_AT + 9, catT)
            phase_end(pe, "pe")

            norm_pe(pe, "mem")
            ports = portions("mem")
            for s in range(2):
                layer_T(pe, "mem", "xk", ports[2 * s:2 * s + 2], 4 * s)
            for s in range(2):
                layer_tok(pe, "mem", "xv", ports[4 + 2 * s:6 + 2 * s], s)
            phase_end(pe, "pe")
            norm_pe(pe, "xa")
            ports = portions("xa")
            for s in range(2):
                layer_T(pe, "xa", "xq", ports[2 * s:2 * s + 2], 4 * s)
            phase_end(pe, "pe")
            attention_pe(pe, CROSS, units_cross())
            phase_end(pe, "pe")
            residual_pe(pe, "xo", LATE_AT + 17, xoT)
            phase_end(pe, "pe")
            phases["rings free"] = phases["pe"]

            norm_pe(pe, "peer")
            pe.wait_ge(S("sk_in"), 16)
            for hh in range(PH):
                wait_nT(pe, "peer", 4)
                mm = nc.tensor.transpose(bank[hh // 4][:, P * (hh % 4):P * (hh % 4) + P],
                                         sk_rows[:, 2 * hh:2 * hh + 2, :].rearrange("p a d -> p (a d)"), ident[:, :])
            mm.then_inc(S("sk_turned"), 1)
            ports = portions("peer")
            for s in range(2):
                layer_T(pe, "peer", "pq", ports[2 * s:2 * s + 2], 4 * s)
            phase_end(pe, "pe")
            for t in range(TT):
                for q in range(4):
                    for x in range(4):
                        hp = 2 * (4 * (q % 2) + x) + q // 2
                        rows = slice(DH * (hp % 2), DH * (hp % 2) + DH)
                        mm = nc.tensor.matmul(bank[4 * t + q][:, P * x:P * x + P],
                                              lhsT=pqT[rows, hp // 2, P * t:P * t + P], rhs=skT[rows, hp // 2, :],
                                              start=True, stop=True)
                    mm.then_inc(S("peer_scores"), 1)
            phase_end(pe, "pe")
            def turn(t, r, i, first=False):
                pe.wait_ge(S(f"down_landed_{r}"), i * 16 + 16)
                for b in range(2):
                    if not first:
                        pe.wait_ge(S(f"down_lo_{b}"), t)
                    for k in range(4 * b, 4 * b + 4):
                        mm = nc.tensor.transpose(bank[4 + b][:, P * (k % 4):P * (k % 4) + P],
                                                 down[r][:, P * k:P * k + P], ident[:, :])
                    mm.then_inc(S(f"down_turned_{b}"), 1)

            def expert_scores(t, r, early):
                if not early:
                    pe.wait_ge(S("expert_gelu"), t - 1)
                out_bank = bank[6 + r % 2][:, 0:T]
                terms = [(downT_hi, x_hi, "down_hi"), (downT_hi, x_lo, None), (downT_lo, x_hi, "down_lo")]
                for a, b, sem in terms:
                    for k in range(KT):
                        if sem and k % 4 == 0:
                            pe.wait_ge(S(f"{sem}_{k // 4}"), t + 1)
                        mm = nc.tensor.matmul(out_bank, lhsT=a[:, r % 2, k, :], rhs=b[:, k, :],
                                              start=a is downT_hi and b is x_hi and k == 0,
                                              stop=a is downT_lo and k == KT - 1)
                mm.then_inc(S("expert_scored"), 1)

            steps = NKEYS // PR
            turn(0, 0, 0, first=True)
            for t in range(PR):
                turn(t + 1, (t + 1) % PR, (t + 1) // PR)
                expert_scores(t, t, t < 2)
            with pe.Fori(1, steps - 1) as i:
                for r in range(PR):
                    turn(i * PR + (r + 1), (r + 1) % PR, i if r + 1 < PR else i + 1)
                    expert_scores(i * PR + r, r, False)
            for t in range(NKEYS - PR, NKEYS):
                if t + 1 < NKEYS:
                    turn(t + 1, (t + 1) % PR, (t + 1) // PR)
                expert_scores(t, t % PR, False)
            phase_end(pe, "pe")
            phases["scores done"] = phases["pe"]

            pe.wait_ge(S("peer_top"), 1)
            for a in range(3):
                for t in range(TT):
                    mm = nc.tensor.transpose(bank[a][:, P * t:P * t + P], fin3[:, a, t, :], ident[:, :])
                mm.then_inc(S("top_turned"), 1)
            phase_end(pe, "pe")
            phases["indices turned"] = phases["pe"]

            def gate_group(i, q):
                for pair in range(2):
                    pe.wait_ge(S("hot_ready"), i * (2 * GROUPS) + (2 * q + pair + 1))
                    if pair == 0:
                        pe.wait_ge(S("gate_read"), i * GROUPS + (q + 1))
                    for x in range(2):
                        tok = 2 * pair + x
                        mm = nc.tensor.matmul(bank[4 + q % 4][:, P * tok:P * tok + P], lhsT=hot[:, pair, x, 1, :],
                                              rhs=hot[:, pair, x, 0, :], start=True, stop=True)
                    if pair == 0:
                        mm.then_inc(S("hot_used0"), 1)
                mm.then_inc(S("hot_used1"), 1)

            with pe.Fori(0, T // (4 * GROUPS)) as i:
                for q in range(GROUPS):
                    gate_group(i, q)
            phase_end(pe, "pe")

            def expert_out(t, r, first_tile, last_tile):
                terms = [(e_hi, u_hi, ("expert_hi", "up_hi")), (e_lo, u_hi, ("expert_lo",)), (e_hi, u_lo, ("up_lo",))]
                for n, (a, b, needed) in enumerate(terms):
                    for sem in needed:
                        pe.wait_ge(S(sem), t + 1)
                    for c in range(4):
                        mm = nc.tensor.matmul(bank[c][:, :], lhsT=a[:, r % 2, P * (c // 2):P * (c // 2) + P],
                                              rhs=b[:, r % 2, 512 * (c % 2):512 * (c % 2) + 512],
                                              start=first_tile and n == 0, stop=last_tile and n == 2,
                                              skip_group_check=True)
                mm.then_inc(S("up_used"), 1)

            for t in range(PR):
                expert_out(t, t, t == 0, False)
            with pe.Fori(1, steps - 1) as i:
                for r in range(PR):
                    expert_out(i * PR + r, r, False, False)
            for t in range(NKEYS - PR, NKEYS):
                expert_out(t, t % PR, False, t == NKEYS - 1)
            phase_end(pe, "pe")

        @block.scalar
        def _(act):
            chain = Chain(act, S("act_chain"))
            for name, rows in ROWS:
                src = w[name][0]
                src = src.rearrange("j (k p) -> (j k) p", p=P) if name == "conv_w" else \
                    src.rearrange("(k p) -> k p", p=P)
                act.dma_start(vrows[COL[name]:COL[name] + rows, :], src).then_inc(S("vrows_landed"), 16)
            for name in ("g_q", "g_k"):
                for half in range(2):
                    act.dma_start(vrows[COL[name]:COL[name] + 1, DH * half:DH * half + DH],
                                  w[name][0:1, :]).then_inc(S("vrows_landed"), 16)
            act.dma_start(dist_oh[0:BUCKETS, :], buckets).then_inc(S("table_in"), 16)
            act.dma_start(rel2[:, :], w["rel_bias_2"]).then_inc(S("table_in"), 16)
            act.dma_start(h[:, :, :], w["x"][0].rearrange("(t p) d -> p t d", p=P)).then_inc(S("x_in"), 16)
            act.dma_start(brow[0:1, :], w["b_in"][0:1, 0:1536]).then_inc(S("brow_in"), 16)
            act.wait_ge(S("table_done"), 1)
            nc.scalar.copy(dist_row[0:HEADS, T:TAB], bank[1][0:HEADS, 0:T]).then_inc(S("table_row"), 1)
            act.wait_ge(S("table_row"), 2)
            act.dma_start(table_dram[:, :], dist_row[0:HEADS, :]).then_inc(S("table_out"), 16)
            act.wait_ge(S("table_out"), 16)
            phase_end(act, "act")

            rel1 = w["rel_bias"]
            act.dma_start(bias1[64:P, :, :], toeplitz(rel1.tensor, 0, 1, 64, HEADS, REL, T)).then_inc(S("bias1_in"), 16)
            act.dma_start(bias1[0:64, :, 64:T],
                          toeplitz(rel1.tensor, 0, 1, 64, HEADS, REL, T - 64)).then_inc(S("bias1_in"), 16)
            act.wait_ge(S("x_in"), 16)
            norm_act(act, chain, "mix", h)

            def read_in1(q):
                if q < 6:
                    for t in range(TT if q % 2 else 0):
                        b = tile_in(act, ("qkv", q // 2, t))
                        nc.scalar.copy(z_tok[:, q // 2, t, :], b[:, :]).then_inc(S("tile_read"), 1)
                    return
                for m in (2 * q - 12, 2 * q - 11):
                    b = tile_in(act, ("in1", m))
                    dst = convT[:, m, :] if m < 12 else sigT[:, m - 12, :]
                    nc.scalar.activation(dst, b[:, 0:T], ACT.Identity if m < 12 else ACT.Sigmoid,
                                         bias=col("b_in", 12 + m)).then_inc(S("tile_read"), 1)

            layer_act(act, "mix", read_in1)
            phase_end(act, "act")
            act.wait_ge(S("qk_squares"), 2)
            nc.scalar.activation(qk_stat[:, 1, :], qk_stat[:, 0, :], ACT.Sqrt, bias=eps[:, 0:1],
                                 scale=1.0 / DH).then_inc(S("qk_rms"), 1)
            act.wait_ge(S("bias1_in"), 32)
            phase_end(act, "act")
            attention_act(act, ATT1, units_block1())
            phase_end(act, "act")
            act.dma_start(brow[0:1, 0:D], w["b_ple_gate"]).then_inc(S("ple_in"), 16)
            phase_end(act, "act")

            act.dma_start(wgr[:, :, 0:4], w["w_group"][0].rearrange("(k p) n -> p k n", p=P)).then_inc(S("router_in"), 16)
            act.dma_start(wgr[:, :, 4:36], w["w_router"][0].rearrange("(k p) n -> p k n", p=P)).then_inc(S("router_in"), 16)
            act.dma_start(br36[0:1, 0:4], w["b_group"]).then_inc(S("router_in"), 16)
            act.dma_start(br36[0:1, 4:36], w["b_router"]).then_inc(S("router_in"), 16)
            act.dma_start(gain_row[:, :], w["g_ffn"][0].partition_broadcast(P)).then_inc(S("gain_in"), 16)
            norm_act(act, chain, "ffn", h)
            for t in range(TT):
                b = tile_in(act, ("router", t))
                nc.scalar.copy(logit[:, t, 0:36], b[:, 0:36]).then_inc(S("tile_read"), 1)
            act.wait_ge(S("tile_read"), tile_no[("router", 1)] + 1)
            act.sem_inc(S("logits"), 1)
            act.wait_ge(S("group_shifted"), 1)
            for t in range(TT):
                nc.scalar.activation(route[:, t, 12:16], route[:, t, 12:16], ACT.Exp,
                                     accum_out=route[:, t, 16:17]).then_inc(S("group_exp"), 1)
            act.wait_ge(S("second_gap"), 1)
            nc.scalar.activation(route[:, :, 18:19], route[:, :, 18:19], ACT.Exp).then_inc(S("second_exp"), 1)
            act.wait_ge(S("xn_gained"), TT)
            nc.scalar.copy(xn_hi[:, :, :], xn[:, :, :]).then_inc(S("xn_hi"), 1)
            phase_end(act, "act")
            over = act.value_load(overfull[0:1, 0:1], min_val=0, max_val=1)

            def weight_hi(i, j, g):
                slot_ready(act, MOE_AT + 3 * j + g // 2, i)
                if not (isinstance(i, int) and PORTIONS * (2 * i + j) + g < HI_BUFS):
                    act.wait_ge(S("portion_used"), i * (2 * PORTIONS) + (PORTIONS * j + g - HI_BUFS + 1))
                nc.scalar.copy(w_hi[:, (PORTIONS * j + g) % HI_BUFS, :, :],
                               portion_of(slot, j, g)).then_inc(S("w_hi"), 1)

            def gathered_hi(i, j):
                act.wait_ge(S("gathered"), i * 2 + (j + 1))
                for b in range(2):
                    nc.scalar.copy(gathT_hi[:, 4 * b:4 * b + 4, :].rearrange("p k s -> p (k s)"),
                                   bank[b][:, :]).then_inc(S("gathT_hi"), 1)

            def expert_act(i, j, last):
                nxt = (i + 1, 0) if j else (i, 1)
                weight_hi(i, j, 3)
                act.wait_ge(S("portion_used"), i * (2 * PORTIONS) + (PORTIONS * j + 2))
                act.wait_ge(S("hid_ready"), i * 2 + (j + 1))
                nc.scalar.activation(silu_r[:, :], bank[2][:, :], ACT.Silu).then_inc(S("silu_ready"), 1)
                weight_hi(i, j, 4)
                weight_hi(i, j, 5)
                if not last:
                    weight_hi(*nxt, 0)
                act.wait_ge(S("hid_turned"), i * 2 + (j + 2))
                nc.scalar.copy(hid_rT_hi[:, :, :].rearrange("p f s -> p (f s)"), bank[4][:, :]).then_inc(
                    S("hid_rT_hi"), 1)
                act.wait_ge(S("pick_turned"), i * 2 + (j + 1))
                act.wait_ge(S("scattered"), i * 8 + (4 * j + 4))
                act.wait_ge(S("out_lo"), i * 4 + (2 * j + 2))
                nc.scalar.copy(row_w[:, :], bank[5][:, 0:1])
                nc.scalar.copy(pickT[:, :, :].rearrange("p t s -> p (t s)"), bank[5][:, P:3 * P]).then_inc(
                    S("turned_pick"), 1)
                gathered_hi(i, j + 1)
                if not last:
                    weight_hi(*nxt, 1)
                act.wait_ge(S("turned_pick"), i * 2 + (j + 2))
                for half in range(2):
                    act.wait_ge(S("portion_used"), i * (2 * PORTIONS) + (PORTIONS * j + 5 + half))
                    nc.scalar.activation(out_hi[:, 512 * half:512 * half + 512], bank[6 + half][:, :], ACT.Copy,
                                         scale=row_w[:, 0:1]).then_inc(S("out_hi"), 1)
                if not last:
                    weight_hi(*nxt, 2)

            with act.If(over < 1):
                for g in range(HI_BUFS):
                    weight_hi(0, 0, g)
                gathered_hi(0, 0)
                with act.Fori(0, EXPERTS // 2 - 1) as i:
                    for j in range(2):
                        expert_act(i, j, False)
                for j in range(2):
                    expert_act(EXPERTS // 2 - 1, j, j == 1)
            with act.Else():
                with act.Fori(0, EXPERTS // 2) as i:
                    for j in range(2):
                        for f in range(FT):
                            act.wait_ge(S("moe_products"), i * (2 * FT) + (FT * j + f + 1))
                            act.wait_ge(S("moe_hidden"), i * (2 * FT) + (FT * j + f + 1))
                            nc.scalar.activation(silu_h[:, f, :], bank[f][:, 0:T], ACT.Silu).then_inc(S("moe_silu"), 1)
            phase_end(act, "act")

            act.dma_start(p_tok[:, :, :], w["p"][0, 0].rearrange("(t p) d -> p t d", p=P)).then_inc(S("ple_in"), 16)
            norm_act(act, chain, "ple", h)
            act.wait_ge(S("p_turned"), 1)
            nc.scalar.copy(pT[:, :, :].rearrange("p k t -> p (k t)"), bank[0][:, :]).then_inc(S("pT_ready"), 1)
            for j in range(2):
                for t in range(TT):
                    b = tile_in(act, ("gate", j, t))
                    nc.scalar.activation(gate_t[:, t, 512 * j:512 * j + 512], b[:, :], ACT.Sigmoid).then_inc(
                        S("tile_read"), 1)
            act.wait_ge(S("tile_read"), tile_no[("gate", 1, 1)] + 1)
            act.sem_inc(S("gate_ready"), 1)
            act.dma_start(w_glr[:, :, :], w["w_in_2"][0].rearrange("(k p) n -> p k n", p=P)[:, :, 1536:1552]).then_inc(
                S("late_in"), 16)
            act.dma_start(gate_w2[:, :], w["gla_gate_w2_2"][0]).then_inc(S("late_in"), 16)
            for s, name in enumerate(("k", "v")):
                act.dma_start(cmp_w2[:, s, :], w[f"cmp_{name}_w2_2"][0]).then_inc(S("late_in"), 16)
                act.dma_start(pos_rows[:, s, :], w[f"cmp_pos_{name}_2"][0].rearrange("(i a) d -> i (a d)", a=2)).then_inc(
                    S("late_in"), 16)
            phase_end(act, "act")

            for s, name in enumerate(("k", "v")):
                act.dma_start(cmp_w1[:, s, :, :], w[f"cmp_{name}_w1_2"][0].rearrange("(i p) n -> p i n", p=P)).then_inc(
                    S("cmp_w1_in"), 16)
            norm_act(act, chain, "mix2", h)

            def read_front():
                for m in range(4):
                    b = tile_in(act, ("kv", m))
                    nc.scalar.copy(kvT[:, m, :], b[:, 0:T]).then_inc(S("tile_read"), 1)
                for s in range(2):
                    for t in range(TT):
                        b = tile_in(act, ("vsw", s, t))
                        nc.scalar.copy(v_sw[:, s, t, :], b[:, 0:P]).then_inc(S("tile_read"), 1)
                for t in range(TT):
                    b = tile_in(act, ("ng", t))
                    nc.scalar.activation(nsa_gate[:, t, :], b[:, 0:24], ACT.Sigmoid).then_inc(S("tile_read"), 1)
                b = tile_in(act, ("glr", 0))
                nc.scalar.copy(glrT[:, :], b[0:16, 0:T]).then_inc(S("tile_read"), 1)
                act.wait_ge(S("tile_read"), tile_no[("glr", 0)] + 1)
                act.sem_inc(S("glr_ready"), 1)

            def read_in2(q):
                if q < 2:
                    for m in (2 * q, 2 * q + 1):
                        b = tile_in(act, ("gqk", m))
                        nc.scalar.activation(gqkT[:, m, :], b[:, 0:T], ACT.Copy, scale=0.125 if m < 2 else 1.0).then_inc(
                            S("tile_read"), 1)
                if q == 1:
                    for c in range(2):
                        b = tile_in(act, ("loga", c))
                        nc.scalar.activation(loga[:, c, :], b[:, 0:T], ACT.Identity,
                                             bias=col("gla_gate_b_2", c)).then_inc(S("tile_read"), 1)
                if q in (3, 5):
                    s = q // 2 - 1
                    for t in range(TT):
                        b = tile_in(act, ("gvr", s, t))
                        nc.scalar.activation((gv, gr)[s][:, t, :], b[:, :], (ACT.Copy, ACT.Silu)[s]).then_inc(
                            S("tile_read"), 1)
                if q >= 6:
                    for m in (2 * q - 12, 2 * q - 11):
                        b = tile_in(act, ("nq", m))
                        nc.scalar.activation(nqT[:, m, :], b[:, 0:T], ACT.Copy, scale=0.125).then_inc(S("tile_read"), 1)

            layer_act(act, "mix2", read_in2, read_front)
            act.wait_ge(S("tile_read"), tile_no[("loga", 1)] + 1)
            tmp = log_tmp
            chain(nc.scalar.activation(tmp, loga[:, :, :], ACT.Abs))
            chain(nc.scalar.activation(tmp, tmp, ACT.Exp, scale=-1.0))
            nc.scalar.activation(tmp, tmp, ACT.Ln, bias=1.0).then_inc(S("log_part"), 1)
            act.wait_ge(S("cmp_w1_in"), 32)
            phase_end(act, "act")

            act.wait_ge(S("pos_turned"), 1)
            nc.scalar.copy(posT[:, :, :].rearrange("p s i -> p (s i)"), bank[6][:, 0:2 * SUB]).then_inc(S("pos_ready"), 1)
            act.wait_ge(S("dup_done"), 4)
            for s in range(2):
                nc.scalar.copy(dupT[:, 2 * s:2 * s + 2, :].rearrange("p g t -> p (g t)"), bank[4 + s][:, :])
            act.wait_ge(S("cmp_hidden"), 1)
            nc.scalar.activation(cmp_h[:, :, :], bank[2][:, 0:64].rearrange("p (s n) -> p s n", s=2)[:, :, 0:2 * N_CMP],
                                 ACT.Gelu_apprx_tanh).then_inc(S("cmp_gelu"), 1)
            act.wait_ge(S("cmp_out"), 1)
            nc.scalar.copy(k_cmpT[:, :], bank[3][:, 0:2 * N_CMP])
            nc.scalar.copy(v_cmp[:, :, :].rearrange("n g d -> n (g d)"), bank[7][0:N_CMP, 0:P])
            phase_end(act, "act")

            for c in range(2):
                act.wait_ge(S("q_diff"), c + 1)
                nc.scalar.activation(q_dec[:, c, :], q_dec[:, c, :], ACT.Exp).then_inc(S("q_exp"), 1)
            for u in range(NSUB):
                for c in range(2):
                    act.wait_ge(S("k_diff"), 2 * u + c + 1)
                    nc.scalar.activation(k_dec[:, u % 2, c, :], k_dec[:, u % 2, c, :], ACT.Exp, scale=-1.0).then_inc(
                        S("k_exp"), 1)
            for n in range(4):
                act.wait_ge(S("diag_diff"), n + 1)
                d = diag[:, 8 * (n % 2):8 * (n % 2) + 8, :, :]
                nc.scalar.activation(d, d, ACT.Exp).then_inc(S("diag_exp"), 1)
            act.wait_ge(S("gla_out"), 1)
            for t in range(TT):
                nc.scalar.copy(o_gla[:, t, :], bank[t][:, :]).then_inc(S("o_gla_ready"), 1)
            act.wait_ge(S("gla_squares"), 1)
            nc.scalar.activation(gla_stat[:, 1, :], gla_stat[:, 0, :], ACT.Sqrt, bias=eps[:, 0:1],
                                 scale=1.0 / P).then_inc(S("gla_rms"), 1)
            phase_end(act, "act")
            act.dma_start(bias_sw[:, :, :], toeplitz(table_dram, T - P + 1, 1, P, HEADS, TAB, T)).then_inc(S("bias2_in"), 16)
            act.dma_start(bias_c[0:N_CMP, :, :], toeplitz(
                table_dram, T - (CMP_BLOCK - 1) - CMP_STRIDE * (N_CMP - 1), CMP_STRIDE, N_CMP, HEADS, TAB, T)).then_inc(S("bias2_in"), 16)
            attention_act(act, NSA, units_nsa())
            phase_end(act, "act")
            act.dma_start(mem_tok[:, :, :], w["mem_2"][0].rearrange("(t p) d -> p t d", p=P)).then_inc(S("mem_in"), 16)
            phase_end(act, "act")

            act.wait_ge(S("mem_in"), 16)
            norm_act(act, chain, "mem", mem_tok)

            def read_mem(q):
                if q < 4:
                    for m in (2 * q, 2 * q + 1):
                        b = tile_in(act, ("xk", m))
                        nc.scalar.copy(xkT[:, m, :], b[:, 0:T]).then_inc(S("tile_read"), 1)
                    return
                j = (q - 4) // 2
                for t in range(TT if q % 2 else 0):
                    b = tile_in(act, ("xv", j, t))
                    nc.scalar.copy(xv[:, t, 512 * j:512 * j + 512], b[:, :]).then_inc(S("tile_read"), 1)

            layer_act(act, "mem", read_mem)
            phase_end(act, "act")
            norm_act(act, chain, "xa", h)

            def read_xq(q):
                for m in (2 * q, 2 * q + 1):
                    b = tile_in(act, ("xq", m))
                    nc.scalar.activation(xqT[:, m, :], b[:, 0:T], ACT.Copy, scale=1.0 / 16).then_inc(S("tile_read"), 1)

            layer_act(act, "xa", read_xq)
            phase_end(act, "act")
            attention_act(act, CROSS, units_cross())
            phase_end(act, "act")
            act.dma_start(sk_rows[:, :, :], w["peer_subkeys_2"][0].rearrange("h a k d -> k (h a) d")).then_inc(
                S("sk_in"), 16)
            phase_end(act, "act")

            norm_act(act, chain, "peer", h)
            act.wait_ge(S("sk_turned"), 1)
            for b in range(2):
                nc.scalar.copy(skT[:, 4 * b:4 * b + 4, :].rearrange("p a k -> p (a k)"), bank[b][:, :])

            def read_pq(q):
                for m in (2 * q, 2 * q + 1):
                    b = tile_in(act, ("pq", m))
                    nc.scalar.copy(pqT[:, m, :], b[:, 0:T]).then_inc(S("tile_read"), 1)

            layer_act(act, "peer", read_pq)
            phase_end(act, "act")
            nc.scalar.copy(x_hi[:, :, :], nT_hi[:, :, :].bitcast(F32))
            for q in range(4):
                act.wait_ge(S("peer_scores"), q + 5)
                nc.scalar.copy(sc[:, 8 * (q % 2) + q // 2:8 * (q % 2) + 8:2, :],
                               bank[4 + q][:, :].rearrange("p (a k) -> p a k", k=NKEYS))
            phase_end(act, "act")

            def down_hi(t, r, early):
                for b in range(2):
                    act.wait_ge(S(f"down_turned_{b}"), t + 1)
                    if not early:
                        act.wait_ge(S("expert_scored"), t - 1)
                    nc.scalar.copy(downT_hi[:, r % 2, 4 * b:4 * b + 4, :].rearrange("p k e -> p (k e)"),
                                   bank[4 + b][:, :]).then_inc(S(f"down_hi_{b}"), 1)

            def gelu(t, r, column):
                act.wait_ge(S("expert_scored"), t + 1)
                nc.scalar.activation(column, bank[6 + r % 2][:, 0:T],
                                     ACT.Gelu_apprx_tanh).then_inc(S("expert_gelu"), 1)

            down_hi(0, 0, True)
            for t in range(PR):
                down_hi(t + 1, t + 1, t + 1 < 2)
                gelu(t, t, gtab[:, t, :])
            with act.Fori(1, NKEYS // PR - 1) as i:
                for r in range(PR):
                    down_hi(i * PR + (r + 1), r + 1, False)
                    gelu(i * PR + r, r, gtab[:, bass.ds(i * PR + r, 1), :].rearrange("p a t -> p (a t)"))
            for t in range(NKEYS - PR, NKEYS):
                if t + 1 < NKEYS:
                    down_hi(t + 1, t + 1, False)
                gelu(t, t, gtab[:, t, :])
            phase_end(act, "act")

            act.wait_ge(S("gate_shifted"), 1)
            nc.scalar.activation(cv[:, :, :, :], cv[:, :, :, :], ACT.Exp).then_inc(S("gate_exp"), 1)
            for a in range(3):
                act.wait_ge(S("top_turned"), a + 1)
                nc.scalar.copy(idxT[:, a, :], bank[a][:, 0:T])
            phase_end(act, "act")
            with act.Fori(0, T // (4 * GROUPS)) as i:
                for q in range(GROUPS):
                    act.wait_ge(S("hot_used1"), i * GROUPS + (q + 2))
                    act.wait_ge(S("gate_scores"), i * GROUPS + (q + 1))
                    nc.scalar.copy(gates[:, q % 4, :], bank[4 + q % 4][:, :]).then_inc(S("gate_read"), 1)
            act.wait_ge(S("gate_scores"), T // 4 + 4)
            phase_end(act, "act")

            def up_parts(t, r, i, column, early):
                if not early:
                    act.wait_ge(S("up_used"), t - 1)
                nc.scalar.copy(e_hi[:, r % 2, :], column).then_inc(S("expert_hi"), 1)
                act.wait_ge(S(f"up_landed_{r}"), i * 16 + 16)
                nc.scalar.copy(u_hi[:, r % 2, :], up[r]).then_inc(S("up_hi"), 1)

            for t in range(PR):
                up_parts(t, t, 0, gtab[:, t, :], t < 2)
            with act.Fori(1, NKEYS // PR) as i:
                for r in range(PR):
                    up_parts(i * PR + r, r, i, gtab[:, bass.ds(i * PR + r, 1), :].rearrange("p a t -> p (a t)"), False)
            phase_end(act, "act")
            act.dma_start(gfin[:, :], w["norm_final_2"].partition_broadcast(P)).then_inc(S("gfin_in"), 16)
            act.wait_ge(S("h_final"), 4)
            norm_act(act, chain, "fin", h)
            for t in range(TT):
                act.wait_ge(S("fin_out"), t + 1)
                act.dma_start(out[0].rearrange("(t p) d -> p t d", p=P)[:, t, :], h[:, t, :]).then_inc(S("stored"), 16)
            act.wait_ge(S("stored"), 16 * TT)

        @block.vector
        def _(dve):
            chain = Chain(dve, S("dve_chain"))
            dve.wait_ge(S("vecs_turned"), 1)
            nc.vector.tensor_copy(vecs[:, 0:NVEC], bank[0][:, 0:NVEC])
            nc.vector.memset(dist_row[0:HEADS, 0:T], NEG).then_inc(S("table_row"), 1)
            phase_end(dve, "dve")
            dve.wait_ge(S("x_in"), 16)
            norm_dve(dve, chain, "mix", h, "g_mix")
            layer_dve(dve, "mix")
            phase_end(dve, "dve")

            for s in range(2):
                chain(nc.vector.tensor_tensor(sq_tok[:, s, :, :], z_tok[:, s, :, :], z_tok[:, s, :, :], ALU.mult))
                nc.vector.tensor_reduce(qk_stat[:, 0, 16 * s:16 * s + 16],
                                        sq_tok[:, s, :, :].rearrange("p t (a d) -> p (t a) d", d=DH), X,
                                        ALU.add).then_inc(S("qk_squares"), 1)
            dve.wait_ge(S("qk_rms"), 1)
            chain(nc.vector.reciprocal(qk_stat[:, 2, :], qk_stat[:, 1, :]))
            for s in range(2):
                zv = z_tok[:, s, :, :].rearrange("p t (a d) -> p (t a) d", d=DH)
                nc.vector.tensor_tensor(zv, zv, spread(qk_stat[:, 2, 16 * s:16 * s + 16], DH),
                                        ALU.mult).then_inc(S("qk_normed"), 1)
            for s in range(2):
                dve.wait_ge(S("qk_turned"), s + 1)
                for m in range(4):
                    src = bank[2 * s + m // 2][:, T * (m % 2):T * (m % 2) + T]
                    nc.vector.tensor_scalar((qT, kT)[s][:, m, :], src, col(("g_q", "g_k")[s], 0),
                                            (0.125, 1.0)[s], ALU.mult, ALU.mult)
            phase_end(dve, "dve")
            attention_dve(dve, ATT1, units_block1())
            phase_end(dve, "dve")
            chain(nc.vector.memset(cin[:, :, 0:2], 0.0))
            chain(nc.vector.tensor_tensor(cin[:, :, 2:T + 2], convT[:, 8:12, :], convT[:, 0:4, :], ALU.mult))
            for m in range(4):
                y = mixT[:, 4 + m, :]
                chain(nc.vector.tensor_scalar(y, cin[:, m, 0:T], col("conv_w", m), col("conv_b", m), ALU.mult, ALU.add))
                for j in (1, 2):
                    chain(nc.vector.scalar_tensor_tensor(out=y, in0=cin[:, m, j:j + T], scalar=col("conv_w", 4 * j + m),
                                                         in1=y, op0=ALU.mult, op1=ALU.add))
                nc.vector.tensor_tensor(y, y, convT[:, 4 + m, :], ALU.mult).then_inc(S("conv_done"), 1)
            for m in range(KT):
                b = tile_in(dve, ("mix", m))
                chain(nc.vector.tensor_tensor(mT[:, m, :], sigT[:, m, :], b[:, 0:T], ALU.mult))
                chain(nc.vector.tensor_tensor(sigT[:, 8 + m, :], sigT[:, 8 + m, :], b[:, T:2 * T], ALU.mult))
                nc.vector.tensor_tensor(mT[:, m, :], mT[:, m, :], sigT[:, 8 + m, :], ALU.add).then_inc(S("mT_ready"), 1)
                dve.wait_ge(S("mT_ready"), m + 1)
                dve.sem_inc(S("tile_read"), 1)
            residual_dve(dve, "wo")
            phase_end(dve, "dve")

            norm_dve(dve, chain, "ffn", h, "g_ffn")
            dve.wait_ge(S("logits"), 1)
            chain(nc.vector.memset(route[:, :, 4:8], NEG))
            chain(nc.vector.tensor_copy(route[:, :, 0:4], logit[:, :, 0:4]))
            for t in range(TT):
                chain(nc.vector.max(top8[:, t, 0:8], route[:, t, 0:8]))
                chain(nc.vector.max_index(idx8[:, t, 0:8], top8[:, t, 0:8], route[:, t, 0:8]))
            chain(nc.vector.tensor_copy(idx8f[:, :, 0:8], idx8[:, :, 0:8]))
            for t in range(TT):
                r = route[:, t, :]
                chain(nc.vector.tensor_scalar(r[:, 12:16], r[:, 0:4], top8[:, t, 0:1], None, ALU.subtract))
                chain(nc.vector.tensor_scalar(r[:, 8:12], iota[:, 0:4], idx8f[:, t, 0:1], None, ALU.is_equal))
                chain(nc.vector.tensor_scalar(r[:, 20:24], r[:, 8:12], -1.0, -NEG, ALU.add, ALU.mult))
                chain(nc.vector.tensor_tensor(r[:, 24:56].rearrange("p (g e) -> p g e", g=GROUPS),
                                              logit[:, t, 4:36].rearrange("p (g e) -> p g e", g=GROUPS),
                                              spread(r[:, 20:24], PER_GROUP), ALU.add))
                chain(nc.vector.max(top8[:, t, 8:16], r[:, 24:56]))
                chain(nc.vector.max_index(idx8[:, t, 8:16], top8[:, t, 8:16], r[:, 24:56]))
                chain(nc.vector.tensor_tensor(r[:, 18:19], top8[:, t, 9:10], top8[:, t, 8:9], ALU.subtract))
            chain(nc.vector.tensor_copy(idx8f[:, :, 8:16], idx8[:, :, 8:16]))
            dve.sem_inc(S("group_shifted"), 1)
            dve.sem_inc(S("second_gap"), 1)
            dve.wait_ge(S("group_exp"), TT)
            dve.wait_ge(S("second_exp"), 1)
            for t in range(TT):
                r = route[:, t, :]
                chain(nc.vector.reciprocal(r[:, 17:18], r[:, 16:17]))
                chain(nc.vector.tensor_scalar(r[:, 19:20], r[:, 18:19], 1.0, None, ALU.add))
                chain(nc.vector.reciprocal(r[:, 19:20], r[:, 19:20]))
                chain(nc.vector.tensor_tensor(r[:, 56:57], r[:, 19:20], r[:, 17:18], ALU.mult))
                chain(nc.vector.tensor_tensor(r[:, 57:58], r[:, 56:57], r[:, 18:19], ALU.mult))
                chain(nc.vector.tensor_scalar(gatew[:, t, :], iota[:, 0:EXPERTS], idx8f[:, t, 8:9], r[:, 56:57],
                                              ALU.is_equal, ALU.mult))
                chain(nc.vector.tensor_scalar(r[:, 24:56], iota[:, 0:EXPERTS], idx8f[:, t, 9:10], r[:, 57:58],
                                              ALU.is_equal, ALU.mult))
                chain(nc.vector.tensor_tensor(gatew[:, t, :], gatew[:, t, :], r[:, 24:56], ALU.add))
                chain(nc.vector.tensor_scalar(picked[:, t, :], iota[:, 0:EXPERTS], idx8f[:, t, 8:9], None, ALU.is_equal))
                chain(nc.vector.scalar_tensor_tensor(out=picked[:, t, :], in0=iota[:, 0:EXPERTS],
                                                     scalar=idx8f[:, t, 9:10], in1=picked[:, t, :],
                                                     op0=ALU.is_equal, op1=ALU.add))
            dve.sem_inc(S("picked_ready"), 1)
            dve.wait_ge(S("gain_in"), 16)
            for t in range(TT):
                nc.vector.tensor_tensor(xn[:, t, :], xn[:, t, :], gain_row[:, :], ALU.mult).then_inc(S("xn_gained"), 1)
            chain(nc.vector.memset(silu_r[:, :], 0.0))
            for zeros in (out_hi[:, 0:512], out_hi[:, 512:D], out_lo[:, 0:512], out_lo[:, 512:D],
                          pickT[:, :, :].rearrange("p t s -> p (t s)")):
                nc.vector.tensor_copy(zeros, silu_r[:, 0:zeros.shape[1]])
            nc.vector.memset(place[:, :, EXPERTS:EXPERTS + 2], -1.0)
            dve.wait_ge(S("rows_counted"), 1)
            for t in range(TT):
                pl = place[:, t, 0:EXPERTS]
                chain(nc.vector.scalar_tensor_tensor(out=pl, in0=bank[0][:, 64 * t:64 * t + EXPERTS], scalar=1.0,
                                                     in1=picked[:, t, :], op0=ALU.add, op1=ALU.mult))
                chain(nc.vector.tensor_scalar(pl, pl, -1.0, None, ALU.add))
            chain(nc.vector.tensor_reduce(fullest[:, :], bank[0][:, 128:128 + EXPERTS], X, ALU.max))
            chain(nc.vector.tensor_scalar(overfull[:, :], fullest[:, :], float(P), None, ALU.is_gt))

            def one_hot(buf, column):
                for t in range(TT):
                    ins = nc.vector.tensor_scalar(pick[:, buf, t, :], iota[:, :], place[:, t, column], None,
                                                  ALU.is_equal)
                ins.then_inc(S("pick_ready"), 1)

            for name in ("hid_ready", "hid_rT_lo", "hid_turned", "turned_pick"):
                dve.sem_inc(S(name), 1)
            dve.sem_inc(S("out_lo"), 2)
            one_hot(0, slice(0, 1))
            one_hot(1, slice(1, 2))
            dve.wait_ge(S("xn_hi"), 1)
            nc.vector.tensor_tensor(xn_lo[:, :, :], xn[:, :, :], xn_hi[:, :, :].bitcast(F32), ALU.subtract)
            dve.sem_inc(S("moe_hidden"), FT)
            dve.sem_inc(S("moe_added"), 4)
            phase_end(dve, "dve")
            over = dve.value_load(overfull[0:1, 0:1], min_val=0, max_val=1)

            def add_rows(i, j):
                for c in range(4):
                    dve.wait_ge(S("scattered"), i * 8 + (4 * j + c + 1))
                    hs = h[:, c // 2, 512 * (c % 2):512 * (c % 2) + 512]
                    nc.vector.tensor_tensor(hs, hs, bank[6 + c % 2][:, :], ALU.add).then_inc(S("row_added"), 1)

            def weight_lo(i, j, g):
                dve.wait_ge(S("w_hi"), i * (2 * PORTIONS) + (PORTIONS * j + g + 1))
                nc.vector.tensor_tensor(portion_of(slot_lo, j, g), portion_of(slot, j, g),
                                        w_hi[:, (PORTIONS * j + g) % HI_BUFS, :, :].bitcast(F32),
                                        ALU.subtract).then_inc(S("w13_lo"), 1)

            def gathered_lo(i, j):
                for b in range(2):
                    dve.wait_ge(S("gathT_hi"), i * 4 + (2 * j + b + 1))
                    v = [x[:, 4 * b:4 * b + 4, :].rearrange("p k s -> p (k s)") for x in (gathT_lo, gathT_hi)]
                    nc.vector.tensor_tensor(v[0], bank[b][:, :], v[1].bitcast(F32), ALU.subtract).then_inc(
                        S("gathT_lo"), 1)

            def output_lo(i, j, half):
                dve.wait_ge(S("out_hi"), i * 4 + (2 * j + half + 1))
                cols = slice(512 * half, 512 * half + 512)
                nc.vector.scalar_tensor_tensor(out=out_lo[:, cols], in0=bank[6 + half][:, :], scalar=row_w[:, 0:1],
                                               in1=out_hi[:, cols].bitcast(F32), op0=ALU.mult,
                                               op1=ALU.subtract).then_inc(S("out_lo"), 1)

            def expert_dve(i, j, last):
                nxt = (i + 1, 0) if j else (i, 1)
                weight_lo(i, j, 3)
                add_rows(i, j)
                dve.wait_ge(S("silu_ready"), i * 2 + (j + 1))
                dve.wait_ge(S("hid_turned"), i * 2 + (j + 1))
                dve.wait_ge(S("portion_used"), i * (2 * PORTIONS) + (PORTIONS * j + 4))
                nc.vector.tensor_tensor(hid_r[:, :], silu_r[:, :], bank[3][:, :], ALU.mult).then_inc(S("hid_ready"), 1)
                dve.wait_ge(S("hid_rT_hi"), i * 2 + (j + 1))
                v = [x[:, :, :].rearrange("p f s -> p (f s)") for x in (hid_rT_lo, hid_rT_hi)]
                nc.vector.tensor_tensor(v[0], bank[4][:, :], v[1].bitcast(F32), ALU.subtract).then_inc(
                    S("hid_rT_lo"), 1)
                if not last:
                    weight_lo(*nxt, 0)
                gathered_lo(i, j + 1)
                dve.wait_ge(S("pick_turned"), i * 2 + (j + 1))
                one_hot(j, bass.ds(i * 2 + (j + 2), 1))
                output_lo(i, j, 0)
                if not last:
                    weight_lo(*nxt, 1)
                output_lo(i, j, 1)
                if not last:
                    weight_lo(*nxt, 2)

            with dve.If(over < 1):
                for g in range(HI_BUFS):
                    weight_lo(0, 0, g)
                gathered_lo(0, 0)
                with dve.Fori(0, EXPERTS // 2 - 1) as i:
                    for j in range(2):
                        expert_dve(i, j, False)
                for j in range(2):
                    expert_dve(EXPERTS // 2 - 1, j, j == 1)
                add_rows(EXPERTS // 2, 0)
            with dve.Else():
                with dve.Fori(0, EXPERTS // 2) as i:
                    for j in range(2):
                        for f in range(FT):
                            dve.wait_ge(S("moe_silu"), i * (2 * FT) + (FT * j + f + 1))
                            dve.wait_ge(S("moe_added"), i * 8 + (4 * j + 4))
                            nc.vector.tensor_tensor(hidT[:, f, :], silu_h[:, f, :], bank[f][:, T:2 * T],
                                                    ALU.mult).then_inc(S("moe_hidden"), 1)
                        for c in range(4):
                            t, half = c // 2, c % 2
                            dve.wait_ge(S("moe_out"), i * 8 + (4 * j + c + 1))
                            hs = h[:, t, 512 * half:512 * half + 512]
                            nc.vector.scalar_tensor_tensor(out=hs, in0=bank[4 + c][:, :],
                                                           scalar=gatew[:, t, bass.ds(i * 2 + j, 1)], in1=hs,
                                                           op0=ALU.mult, op1=ALU.add).then_inc(S("moe_added"), 1)
            phase_end(dve, "dve")

            norm_dve(dve, chain, "ple", h, "g_ple")
            dve.wait_ge(S("gate_ready"), 1)
            for j in range(2):
                for t in range(TT):
                    b = tile_in(dve, ("ple", j, t))
                    g = gate_t[:, t, 512 * j:512 * j + 512]
                    hs = h[:, t, 512 * j:512 * j + 512]
                    nc.vector.tensor_tensor(g, g, b[:, :], ALU.mult).then_inc(S("tile_read"), 1)
                    dve.wait_ge(S("tile_read"), tile_no[("ple", j, t)] + 1)
                    nc.vector.tensor_tensor(hs, hs, g, ALU.add)
            phase_end(dve, "dve")

            norm_dve(dve, chain, "mix2", h, "norm_mix_2")
            layer_dve(dve, "mix2", ("glr", 0))
            dve.wait_ge(S("log_part"), 1)
            chain(nc.vector.tensor_scalar(loga[:, :, :], loga[:, :, :], 0.0, None, ALU.min))
            chain(nc.vector.tensor_tensor(loga[:, :, :], loga[:, :, :], log_tmp, ALU.subtract))
            chain(nc.vector.tensor_scalar(loga[:, :, :], loga[:, :, :], 0.5 / 16.0, None, ALU.mult))
            for c in range(2):
                nc.vector.tensor_tensor_scan(bcum[:, c, :], loga[:, c, :], loga[:, c, :], 0.0, ALU.add, ALU.add)
            cg = nsa_gate[:, 0, :].rearrange("p (a b) -> p a b", b=3)[:, :, 0]
            nc.vector.tensor_scalar(cg, cg, late_row[:, 0:1], None, ALU.mult)
            phase_end(dve, "dve")

            dve.wait_ge(S("dup_done"), 2)
            dve.wait_ge(S("pos_ready"), 1)
            for s in range(2):
                for g in range(2):
                    for half in range(2):
                        rows = slice(DH * half, DH * half + DH)
                        kv = bank[s][rows, T * g:T * g + T].rearrange("p (n a) -> p a n", a=CMP_STRIDE)
                        for far in range(2):
                            ins = nc.vector.tensor_tensor(
                                cmp_in[rows, s, 8 * far:8 * far + 8, g, :], kv[:, half::2, far:far + N_CMP],
                                spread(posT[rows, s, 8 * far:8 * far + 8], N_CMP), ALU.add)
                ins.then_inc(S("cmp_in_ready"), 1)
            phase_end(dve, "dve")

            for c in range(2):
                chain(nc.vector.tensor_copy(q_dec[:, c, 0:SUB], bcum[:, c, 0:SUB]))
                nc.vector.tensor_tensor(q_dec[:, c, SUB:T].rearrange("p (u t) -> p u t", t=SUB),
                                        bcum[:, c, SUB:T].rearrange("p (u t) -> p u t", t=SUB),
                                        spread(bcum[:, c, SUB - 1:T - SUB:SUB], SUB), ALU.subtract).then_inc(
                    S("q_diff"), 1)
            for c in range(2):
                dve.wait_ge(S("q_exp"), c + 1)
                nc.vector.tensor_tensor(q_dec[:, c, :], q_dec[:, c, :], gqkT[:, c, :], ALU.mult).then_inc(
                    S("q_dec_ready"), 1)

            def k_diff(u):
                for c in range(2):
                    if u >= 2:
                        dve.wait_ge(S("k_dec_used"), 2 * (u - 2) + c + 1)
                    before = bcum[:, c, SUB * u - 1:SUB * u] if u else 0.0
                    nc.vector.tensor_scalar(k_dec[:, u % 2, c, :], bcum[:, c, :], before, 0.0, ALU.subtract,
                                            ALU.max).then_inc(S("k_diff"), 1)

            k_diff(0)
            for u in range(NSUB):
                if u + 1 < NSUB:
                    k_diff(u + 1)
                for c in range(2):
                    dve.wait_ge(S("k_exp"), 2 * u + c + 1)
                    nc.vector.tensor_tensor(k_dec[:, u % 2, c, :], k_dec[:, u % 2, c, :], gqkT[:, 2 + c, :],
                                            ALU.mult).then_inc(S("k_dec_ready"), 1)
            def diag_views(n):
                c, part = n // 2, n % 2
                d = diag[:, 8 * part:8 * part + 8, :, :]

                def by_key(v):
                    return v[:, P * part:P * part + P].rearrange("p (u t) -> p u t", t=SUB).unsqueeze(2).to_broadcast(
                        [P, NSUB // 2, SUB, SUB])

                def by_query(v):
                    return spread(v[:, P * part:P * part + P], SUB)

                return c, d, d.rearrange("p u t j -> p (u t) j"), by_key, by_query

            def diag_diff(n):
                c, d, flat, by_key, by_query = diag_views(n)
                if n >= 2:
                    dve.wait_ge(S("diag_used"), n - 1)
                chain(nc.vector.tensor_copy(d, by_key(bcum[:, c, :])))
                chain(nc.vector.tensor_tensor(flat, by_query(bcum[:, c, :]), flat, ALU.subtract))
                nc.vector.tensor_scalar(flat, flat, 0.0, None, ALU.min).then_inc(S("diag_diff"), 1)

            def diag_products(n):
                c, d, flat, by_key, by_query = diag_views(n)
                dve.wait_ge(S("diag_exp"), n + 1)
                chain(nc.vector.tensor_tensor(flat, flat, by_query(gqkT[:, c, :]), ALU.mult))
                nc.vector.tensor_tensor(d, d, by_key(gqkT[:, 2 + c, :]), ALU.mult).then_inc(S("diag_ready"), 1)

            diag_diff(0)
            diag_diff(1)
            diag_products(0)
            diag_products(1)
            for n in (2, 3):
                diag_diff(n)
                diag_products(n)
            dve.wait_ge(S("diag_used"), 4)
            dve.wait_ge(S("k_dec_used"), 2 * NSUB)
            for hh in range(GLA_HEADS):
                far, near = bank[hh], bank[4 + hh]
                tmp = k_dec[:, 0, 0, 0:P]
                nc.vector.tensor_copy(gla_a[:, hh, 0, P:T], far[:, P:T])
                for t in range(TT):
                    a = gla_a[:, hh, t, P * t:P * t + P]
                    chain(nc.vector.tensor_tensor(a, far[:, T * t + P * t:T * t + P * t + P], mask_prev[:, :], ALU.mult))
                    chain(nc.vector.tensor_tensor(tmp, near[:, P * t:P * t + P], mask_same[:, :], ALU.mult))
                    chain(nc.vector.tensor_tensor(a, a, tmp, ALU.add))
            dve.sem_inc(S("gla_a_ready"), 1)
            dve.wait_ge(S("o_gla_ready"), TT)
            og = o_gla[:, :, :].rearrange("p t (a d) -> p (t a) d", d=P)
            sq = scratch(0, TT * GLA_HEADS, P)
            chain(nc.vector.tensor_tensor(sq, og, og, ALU.mult))
            nc.vector.tensor_reduce(gla_stat[:, 0, :], sq, X, ALU.add).then_inc(S("gla_squares"), 1)
            dve.wait_ge(S("gla_rms"), 1)
            chain(nc.vector.reciprocal(gla_stat[:, 2, :], gla_stat[:, 1, :]))
            chain(nc.vector.tensor_tensor(og, og, spread(gla_stat[:, 2, :], P), ALU.mult))
            nc.vector.tensor_tensor(o_gla[:, :, :], o_gla[:, :, :], gr[:, :, :], ALU.mult).then_inc(S("gla_normed"), 1)
            dve.wait_ge(S("gla_turned"), 1)
            for hh in range(GLA_HEADS):
                nc.vector.tensor_scalar(catT[:, hh, :], bank[2 + hh // 2][:, T * (hh % 2):T * (hh % 2) + T],
                                        col("gla_out_norm_2", 0), None, ALU.mult)
            phase_end(dve, "dve")
            attention_dve(dve, NSA, units_nsa())
            phase_end(dve, "dve")
            residual_dve(dve, "wout")
            phase_end(dve, "dve")
            dve.wait_ge(S("mem_in"), 16)
            norm_dve(dve, chain, "mem", mem_tok, "norm_mem_2")
            layer_dve(dve, "mem")
            phase_end(dve, "dve")
            norm_dve(dve, chain, "xa", h, "norm_xattn_2")
            layer_dve(dve, "xa")
            phase_end(dve, "dve")
            attention_dve(dve, CROSS, units_cross())
            phase_end(dve, "dve")
            residual_dve(dve, "xo")
            phase_end(dve, "dve")
            norm_dve(dve, chain, "peer", h, "norm_ffn_2")
            layer_dve(dve, "peer")
            phase_end(dve, "dve")
            phase_end(dve, "dve")

            def best16(scores, values, places):
                chain(nc.vector.max(values[:, 0:8], scores))
                chain(nc.vector.max_index(places[:, 0:8], values[:, 0:8], scores))
                chain(nc.vector.match_replace(scores, values[:, 0:8], scores, -3.0e38))
                chain(nc.vector.max(values[:, 8:16], scores))
                chain(nc.vector.max_index(places[:, 8:16], values[:, 8:16], scores))

            def best_keys(n):
                t, hp = n // 16, n % 16
                q, x = 2 * (hp % 2) + hp // 8, hp // 2 % 4
                scores = sc[:, hp, :] if t else bank[q][:, NKEYS * x:NKEYS * x + NKEYS]
                best16(scores, tv[:, t, hp, :], ti[:, t, hp, :])

            def best_sums(n):
                t, hh = n // PH, n % PH
                if n == 0:
                    chain(nc.vector.tensor_copy(tif[:, :, :, :], ti))
                chain(nc.vector.tensor_tensor(
                    cand[:, t, hh, :, :], spread(tv[:, t, 2 * hh, :], TOPK),
                    tv[:, t, 2 * hh + 1, :].unsqueeze(1).to_broadcast([P, TOPK, TOPK]), ALU.add))
                best16(cand[:, t, hh, :, :].rearrange("p a b -> p (a b)"), cv[:, t, hh, :], ci[:, t, hh, :])

            def key_indices(n):
                t, a, g = n // 8, n // 4 % 2, n % 4
                if n == 0:
                    cif = ci.rearrange("p t a k -> p t (a k)")
                    nc.vector.tensor_scalar(cab[:, 0, :, :], cif, 4, None, ALU.logical_shift_right)
                    chain(nc.vector.tensor_scalar(cab[:, 1, :, :], cif, TOPK - 1, None, ALU.bitwise_and))
                    chain(nc.vector.tensor_copy(cabf[:, :, :, :], cab))
                part_of = slice(2 * TOPK * g, 2 * TOPK * g + 2 * TOPK)
                e = eq[:, n % 2, :, :, :].rearrange("p h k j -> p (h k) j")
                chain(nc.vector.tensor_tensor(e, spread(cabf[:, a, t, part_of], TOPK),
                                              iota16.unsqueeze(1).to_broadcast([P, 2 * TOPK, TOPK]), ALU.is_equal))
                for x in range(2):
                    hh = 2 * g + x
                    ex = e[:, TOPK * x:TOPK * x + TOPK, :]
                    chain(nc.vector.tensor_tensor(
                        ex, ex, tif[:, t, 2 * hh + a, :].unsqueeze(1).to_broadcast([P, TOPK, TOPK]), ALU.mult))
                chain(nc.vector.tensor_reduce(fin3[:, a, t, part_of], e, X, ALU.add))

            pieces = [(best_keys, n) for n in range(TT * 16)] + [(best_sums, n) for n in range(TT * PH)] + \
                [(key_indices, n) for n in range(16)]
            assert len(pieces) == NKEYS // 2

            def down_lo(t, r, early):
                for b in range(2):
                    dve.wait_ge(S(f"down_hi_{b}"), t + 1)
                    if not early:
                        dve.wait_ge(S("expert_scored"), t - 1)
                    part = slice(4 * b, 4 * b + 4)
                    nc.vector.tensor_tensor(downT_lo[:, r % 2, part, :].rearrange("p k e -> p (k e)"), bank[4 + b][:, :],
                                            downT_hi[:, r % 2, part, :].bitcast(F32).rearrange("p k e -> p (k e)"),
                                            ALU.subtract).then_inc(S(f"down_lo_{b}"), 1)

            for t, (work, n) in enumerate(pieces):
                down_lo(t, t % PR, t < 2)
                work(n)
            with dve.Fori(NKEYS // 2 // PR, NKEYS // PR) as i:
                for r in range(PR):
                    down_lo(i * PR + r, r, False)
            chain(nc.vector.tensor_copy(psum16[:, 1, :], cv[:, :, :, 0].rearrange("p t a -> p (t a)")))
            cvf = cv[:, :, :, :].rearrange("p t a k -> p (t a) k")
            nc.vector.tensor_tensor(cvf, cvf, spread(psum16[:, 1, :], TOPK), ALU.subtract).then_inc(S("gate_shifted"), 1)
            phase_end(dve, "dve")
            dve.wait_ge(S("gate_exp"), 1)
            chain(nc.vector.tensor_reduce(psum16[:, 0, :], cvf, X, ALU.add))
            chain(nc.vector.reciprocal(psum16[:, 1, :], psum16[:, 0, :]))
            nc.vector.tensor_tensor(fin3[:, 2, :, :].rearrange("p t (a k) -> p (t a) k", k=TOPK), cvf,
                                    spread(psum16[:, 1, :], TOPK), ALU.mult).then_inc(S("peer_top"), 1)
            dve.sem_inc(S("gate_read"), 4)
            dve.sem_inc(S("gate_scores"), 4)
            dve.sem_inc(S("hot_used0"), 1)
            dve.sem_inc(S("hot_used1"), 1)
            phase_end(dve, "dve")

            with dve.Fori(0, T // (4 * GROUPS)) as i:
                for q in range(GROUPS):
                    for pair in range(2):
                        dve.wait_ge(S(f"hot_used{pair}"), i * GROUPS + (q + 1))
                        toks = bass.ds(i * (4 * GROUPS) + (4 * q + 2 * pair), 2)
                        nc.vector.tensor_tensor(hot[:, pair, :, 0, :], iota[:, :].unsqueeze(1).to_broadcast([P, 2, P]),
                                                spread(idxT[:, 0, toks], P), ALU.is_equal)
                        for x in range(2):
                            tok = bass.ds(i * (4 * GROUPS) + (4 * q + 2 * pair + x), 1)
                            ins = nc.vector.tensor_scalar(hot[:, pair, x, 1, :], iota[:, :], idxT[:, 1, tok],
                                                          idxT[:, 2, tok], ALU.is_equal, ALU.mult)
                        ins.then_inc(S("hot_ready"), 1)
            phase_end(dve, "dve")

            def lower_parts(t, r, column):
                dve.wait_ge(S("expert_hi"), t + 1)
                nc.vector.tensor_tensor(e_lo[:, r % 2, :], column, e_hi[:, r % 2, :].bitcast(F32),
                                        ALU.subtract).then_inc(S("expert_lo"), 1)
                dve.wait_ge(S("up_hi"), t + 1)
                nc.vector.tensor_tensor(u_lo[:, r % 2, :], up[r], u_hi[:, r % 2, :].bitcast(F32),
                                        ALU.subtract).then_inc(S("up_lo"), 1)

            with dve.Fori(0, NKEYS // PR) as i:
                for r in range(PR):
                    lower_parts(i * PR + r, r, gtab[:, bass.ds(i * PR + r, 1), :].rearrange("p a t -> p (a t)"))
            phase_end(dve, "dve")
            for c in range(4):
                hs = h[:, c // 2, 512 * (c % 2):512 * (c % 2) + 512]
                nc.vector.tensor_tensor(hs, hs, bank[c][:, :], ALU.add).then_inc(S("h_final"), 1)
            dve.wait_ge(S("norm_rms"), len(NORMS))
            dve.wait_ge(S("h_final"), 4)
            dve.wait_ge(S("gfin_in"), 16)
            chain(nc.vector.reciprocal(stat[:, 2, :], stat[:, 1, :]))
            for t in range(TT):
                nc.vector.scalar_tensor_tensor(out=h[:, t, :], in0=h[:, t, :], scalar=stat[:, 2, t:t + 1],
                                               in1=gfin, op0=ALU.mult, op1=ALU.mult).then_inc(S("fin_out"), 1)

        @block.gpsimd
        def _(pool):
            chain = Chain(pool, S("pool_chain"))
            nc.gpsimd.memset(eps[:, :], EPS)
            nc.gpsimd.memset(sel_dup[:, :, :], 0.0)
            nc.gpsimd.memset(modmask[:, :], 0.0)
            nc.gpsimd.memset(ident[:, :], 0.0)
            nc.gpsimd.memset(mirror[:, :], 0.0)
            chain(nc.gpsimd.memset(ones[:, :], 1.0))
            nc.gpsimd.iota(iota[:, :], pattern=[[1, P]], base=0, channel_multiplier=0,
                           allow_small_or_imprecise_dtypes=True)
            nc.gpsimd.affine_select(out=ident[:, :], in_=ident[:, :], compare_op=ALU.not_equal, fill=1.0, base=0,
                                    pattern=[[-1, P]], channel_multiplier=1)
            nc.gpsimd.affine_select(out=mirror[:, :], in_=mirror[:, :], compare_op=ALU.not_equal, fill=1.0, base=1 - P,
                                    pattern=[[1, P]], channel_multiplier=1)
            nc.gpsimd.memset(modmask[:, SUB - 1::SUB], 1.0)
            for g in range(2):
                d = sel_dup[:, g, :].rearrange("p (a b) -> p a b", a=2)
                nc.gpsimd.affine_select(out=d, in_=d, compare_op=ALU.not_equal, fill=1.0, base=-DH * g,
                                        pattern=[[0, 2], [-1, DH]], channel_multiplier=1)
            nc.gpsimd.affine_select(out=mask_prev[:, :].rearrange("p (u t) -> p u t", t=SUB),
                                    in_=ones[:, :].rearrange("p (u t) -> p u t", t=SUB), compare_op=ALU.is_gt, fill=0.0,
                                    base=0, pattern=[[SUB, P // SUB], [0, SUB]], channel_multiplier=-1)
            nc.gpsimd.affine_select(out=earlier[:, :], in_=ones[:, :], compare_op=ALU.is_gt, fill=0.0, base=0,
                                    pattern=[[1, P]], channel_multiplier=-1)
            chain(nc.gpsimd.affine_select(out=mask_same[:, :], in_=ones[:, :], compare_op=ALU.is_ge, fill=0.0, base=0,
                                          pattern=[[1, P]], channel_multiplier=-1))
            nc.gpsimd.tensor_tensor(mask_same[:, :], mask_same[:, :], mask_prev[:, :], ALU.subtract)
            chain(nc.gpsimd.affine_select(out=late_row[:, :], in_=ones[:, 0:1], compare_op=ALU.is_ge, fill=0.0,
                                          base=-(CMP_BLOCK - 1), pattern=[[0, 1]], channel_multiplier=1))
            nc.gpsimd.memset(bias1[0:64, :, 0:64], NEG)
            pool.drain().then_inc(S("consts"), 1)
            pool.wait_ge(S("phase"), 3 * phases["routed"])
            over = pool.value_load(overfull[0:1, 0:1], min_val=0, max_val=1)
            with pool.If(over < 1):
                with pool.Fori(0, EXPERTS // 2) as i:
                    for j in range(2):
                        for g in (4, 5):
                            pool.wait_ge(S("w_hi"), i * (2 * PORTIONS) + (PORTIONS * j + g + 1))
                            nc.gpsimd.tensor_tensor(portion_of(slot_lo, j, g), portion_of(slot, j, g),
                                                    w_hi[:, (PORTIONS * j + g) % HI_BUFS, :, :].bitcast(F32),
                                                    ALU.subtract).then_inc(S("w2_lo"), 1)
            pool.wait_ge(S("phase"), 3 * phases["indices turned"])
            with pool.Fori(0, T // (4 * GROUPS)) as i:
                for q in range(GROUPS):
                    pool.wait_ge(S("gate_read"), i * GROUPS + (q + 5))
                    view = gtab[:, :, bass.ds(i * (4 * GROUPS) + 4 * q, 4)].rearrange("p i t -> p t i")
                    nc.gpsimd.tensor_tensor(view, view, gates[:, q % 4, :].rearrange("p (t i) -> p t i", t=4),
                                            ALU.mult).then_inc(S("gate_scores"), 1)

        @block.sync
        def _(sp):
            def load(n, pieces):
                if n >= RING:
                    m = n - RING
                    if m in spent_at:
                        sp.wait_ge(S("tile_done"), spent_at[m])
                    else:
                        e, kind = (m - MOE_AT) // 3, (m - MOE_AT) % 3
                        sp.wait_ge(S("portion_used"), PORTIONS * e + 2 * kind + 2)
                for at, src in pieces:
                    kt, width = src.shape[1], src.shape[2]
                    dst = slot[n % RING][:, at:at + kt * width].rearrange("p (k n) -> p k n", n=width)
                    sp.dma_start(dst, src).then_inc(landed[n % RING], 16)

            sp.wait_ge(S("vrows_landed"), 16 * NVROWS)
            sp.wait_ge(S("table_in"), 32)
            sp.wait_ge(S("x_in"), 16)
            for n, pieces in enumerate(first):
                load(n, pieces)
            tabs = [w["w1"][0].rearrange("e (k p) n -> e p k n", p=P), w["w3"][0].rearrange("e (k p) n -> e p k n", p=P),
                    w["w2"][0].rearrange("e (k p) n -> e p k n", p=P)]
            for j in range(6):
                load(MOE_AT + j, [(0, tabs[j % 3][j // 3])])
            with sp.Fori(1, EXPERTS // 2) as i:
                for j in range(6):
                    sp.wait_ge(S("portion_used"),
                               i * (2 * PORTIONS) + (PORTIONS * (j // 3 - 2) + 2 * (j % 3) + 2))
                    src = tabs[j % 3][bass.ds(i * 2 + j // 3, 1)].rearrange("e p k n -> p (e k) n")
                    dst = slot[(MOE_AT + j) % RING].rearrange("p (k n) -> p k n", n=src.shape[2])
                    sp.dma_start(dst, src).then_inc(landed[(MOE_AT + j) % RING], 16)
            for m, pieces in enumerate(later):
                load(LATE_AT + m, pieces)
            dn = w["peer_down_2"][0].rearrange("(i p) d -> i p d", p=P)
            upt = w["peer_up_2"][0].rearrange("(i p) d -> i p d", p=P)
            sp.wait_ge(S("phase"), 3 * phases["rings free"])
            for r in range(PR):
                sp.dma_start(down[r], dn[r]).then_inc(S(f"down_landed_{r}"), 16)
            with sp.Fori(1, NKEYS // PR) as i:
                for r in range(PR):
                    e = bass.ds(i * PR + r, 1)
                    sp.wait_ge(S("down_turned_1"), i * PR + (r - PR + 1))
                    sp.dma_start(down[r], dn[e].rearrange("a p d -> p (a d)")).then_inc(S(f"down_landed_{r}"), 16)
            sp.wait_ge(S("phase"), 3 * phases["scores done"])
            for r in range(PR):
                sp.dma_start(up[r], upt[r]).then_inc(S(f"up_landed_{r}"), 16)
            with sp.Fori(1, NKEYS // PR) as i:
                for r in range(PR):
                    e = bass.ds(i * PR + r, 1)
                    sp.wait_ge(S("up_lo"), i * PR + (r - PR + 1))
                    sp.dma_start(up[r], upt[e].rearrange("a p d -> p (a d)")).then_inc(S(f"up_landed_{r}"), 16)

        assert phases["pe"] == phases["act"] == phases["dve"], phases


_INS = ['x', 'p', 'g_mix', 'w_in', 'b_in', 'g_q', 'g_k', 'rel_bias', 'conv_w', 'conv_b', 'w_pa', 'w_pc', 'w_o',
        'g_ffn', 'w_group', 'b_group', 'w_router', 'b_router', 'w1', 'w3', 'w2', 'g_ple', 'w_ple_gate',
        'b_ple_gate', 'w_ple_proj', 'mem_2', 'rel_bias_2', 'norm_mix_2', 'w_in_2', 'gla_gate_w2_2',
        'gla_gate_b_2', 'gla_out_norm_2', 'cmp_pos_k_2', 'cmp_pos_v_2', 'cmp_k_w1_2', 'cmp_k_w2_2',
        'cmp_v_w1_2', 'cmp_v_w2_2', 'w_out_2', 'norm_xattn_2', 'norm_mem_2', 'xa_wq_2', 'xa_wk_2',
        'xa_wv_2', 'xa_wo_2', 'norm_ffn_2', 'peer_wq_2', 'peer_subkeys_2', 'peer_down_2', 'peer_up_2',
        'norm_final_2']


def kernel(**inputs):
    import concourse.bacc as _bacc
    from concourse.bass_utils import run_bass_kernel_spmd as _run

    nc = _bacc.Bacc("TRN2", target_bir_lowering=False, num_devices=1)
    arrays, args = {}, {}
    for name in _INS:
        a = np.ascontiguousarray(inputs[name])
        arrays[f"in_{name}_dram"] = a
        args[name] = nc.dram_tensor(f"in_{name}_dram", a.shape, mybir.dt.from_np(a.dtype), kind="ExternalInput").ap()
    buckets = nc.inline_tensor(distance_buckets(), "distance_buckets").ap()
    out = nc.dram_tensor("out_0_dram", (1, T, D), F32, kind="ExternalOutput").ap()
    build(nc, args, buckets, out)
    r = _run(nc, [arrays], core_ids=[0])
    return r.results[0]["out_0_dram"]
```
